# Optimizing a Trainium2 kernel written in Bass

```python
import jax, jax.numpy as jnp
from jax import lax
import numpy as np

D_MODEL = 1024
BATCH = 1
SEQ = 256
DEPTH = 2

N_MIXERS = 2
D_FF = 2816
EPS = 1e-6

SSD_EXPAND = 2
SSD_D_INNER = SSD_EXPAND * D_MODEL
SSD_HEAD_DIM = 64
SSD_HEADS = SSD_D_INNER // SSD_HEAD_DIM
SSD_GROUPS = 8
SSD_STATE = 128
SSD_CONV = 5
SSD_CHUNK = 128
SSD_CONV_CH = SSD_D_INNER + 2 * SSD_GROUPS * SSD_STATE
SSD_IN = SSD_D_INNER + SSD_CONV_CH + 2 * SSD_HEADS

ATTN_HEADS = 16
ATTN_KV_HEADS = 4
ATTN_HEAD_DIM = 64
ATTN_QKV = (ATTN_HEADS + 2 * ATTN_KV_HEADS) * ATTN_HEAD_DIM
WINDOW = 128
ATTN_BLOCK = 128
ROPE_THETA = 10000.0

N_SSD_LAYERS = (DEPTH + 1) // 2
N_ATTN_LAYERS = DEPTH // 2

kernel_name = "hybrid_ssd_swa_macaron_encoder"

def rms_norm(x, w):
    xf = x.astype(jnp.float32)
    y = xf * lax.rsqrt(jnp.mean(xf * xf, axis=-1, keepdims=True) + EPS)
    return (y * w.astype(jnp.float32)).astype(x.dtype)

def swiglu(h, w_gate, w_up, w_down):
    return (jax.nn.silu(h @ w_gate) * (h @ w_up)) @ w_down

def rotary(x, pos):
    half = x.shape[-1] // 2
    inv_freq = ROPE_THETA ** (-jnp.arange(half, dtype=jnp.float32) / half)
    ang = pos.astype(jnp.float32)[:, None] * inv_freq[None, :]
    cos = jnp.cos(ang)[None, :, None, :]
    sin = jnp.sin(ang)[None, :, None, :]
    xf = x.astype(jnp.float32)
    x1, x2 = xf[..., :half], xf[..., half:]
    return jnp.concatenate([x1 * cos - x2 * sin, x2 * cos + x1 * sin], axis=-1).astype(x.dtype)

def dwconv_centred(u, w, b):
    k = w.shape[0]
    out = lax.conv_general_dilated(
        u, w[:, None, :].astype(u.dtype), window_strides=(1,),
        padding=[((k - 1) // 2, k // 2)],
        dimension_numbers=('NWC', 'WIO', 'NWC'),
        feature_group_count=u.shape[-1])
    return out + b.astype(u.dtype)

def ssd_scan(x, dt, a, b_mat, c_mat):
    f32 = jnp.float32
    bsz, L, H, P = x.shape
    G, N = b_mat.shape[-2:]
    E = H // G
    T = SSD_CHUNK
    nc = L // T
    xdt = (x.astype(f32) * dt[..., None]).reshape(bsz, nc, T, G, E, P)
    bc = b_mat.astype(f32).reshape(bsz, nc, T, G, N)
    cc = c_mat.astype(f32).reshape(bsz, nc, T, G, N)
    da = (dt * a).reshape(bsz, nc, T, G, E)
    cum = jnp.cumsum(da, axis=2).transpose(0, 1, 3, 4, 2)
    lower = jnp.tril(jnp.ones((T, T), dtype=bool))
    seg = cum[..., :, None] - cum[..., None, :]
    decay = jnp.exp(jnp.where(lower, seg, -jnp.inf))
    cb = jnp.einsum('bctgn,bcsgn->bcgts', cc, bc)
    y_diag = jnp.einsum('bcgts,bcgets,bcsgep->bctgep', cb, decay, xdt)
    decay_to_end = jnp.exp(cum[..., -1:] - cum)
    states = jnp.einsum('bctgn,bcget,bctgep->bcgepn', bc, decay_to_end, xdt)
    chunk_decay = jnp.exp(cum[..., -1])

    def step(h, inp):
        s_k, d_k = inp
        return h * d_k[..., None, None] + s_k, h

    h0 = jnp.zeros((bsz, G, E, P, N), f32)
    _, h_in = lax.scan(step, h0, (jnp.moveaxis(states, 1, 0), jnp.moveaxis(chunk_decay, 1, 0)))
    h_in = jnp.moveaxis(h_in, 0, 1)
    y_off = jnp.einsum('bctgn,bcgepn,bcget->bctgep', cc, h_in, jnp.exp(cum))
    return (y_diag + y_off).reshape(bsz, L, H, P)

def ssd_mixer(h, w_in, conv_w, conv_b, dt_bias, a_log, d_skip, norm_w, w_out):
    f32 = jnp.float32
    bsz, L, _ = h.shape
    proj = h @ w_in
    z, xbc, dt_raw = jnp.split(proj, [SSD_D_INNER, SSD_D_INNER + SSD_CONV_CH], axis=-1)
    xbc = jax.nn.silu(dwconv_centred(xbc, conv_w, conv_b))
    xs, b_mat, c_mat = jnp.split(xbc, [SSD_D_INNER, SSD_D_INNER + SSD_GROUPS * SSD_STATE], axis=-1)
    xs = xs.reshape(bsz, L, SSD_HEADS, SSD_HEAD_DIM)
    b_mat = b_mat.reshape(bsz, L, SSD_GROUPS, SSD_STATE)
    c_mat = c_mat.reshape(bsz, L, SSD_GROUPS, SSD_STATE)
    dt = jax.nn.softplus(dt_raw.astype(f32).reshape(bsz, L, 2, SSD_HEADS) + dt_bias.astype(f32))
    a = -jnp.exp(a_log.astype(f32))
    y_fwd = ssd_scan(xs, dt[:, :, 0], a[0], b_mat, c_mat)
    flip = lambda t: jnp.flip(t, axis=1)
    y_bwd = flip(ssd_scan(flip(xs), flip(dt[:, :, 1]), a[1], flip(b_mat), flip(c_mat)))
    y = y_fwd + y_bwd + xs.astype(f32) * d_skip.astype(f32)[:, None]
    y = y.reshape(bsz, L, SSD_D_INNER) * jax.nn.silu(z.astype(f32))
    y = rms_norm(y, norm_w).astype(h.dtype)
    return y @ w_out

def window_attention(h, w_qkv, q_norm_w, k_norm_w, sink, w_out, pos):
    f32 = jnp.float32
    bsz, L, _ = h.shape
    hq, hk, dh, blk = ATTN_HEADS, ATTN_KV_HEADS, ATTN_HEAD_DIM, ATTN_BLOCK
    grp = hq // hk
    nb = L // blk
    q, k, v = jnp.split(h @ w_qkv, [hq * dh, (hq + hk) * dh], axis=-1)
    q = rotary(rms_norm(q.reshape(bsz, L, hq, dh), q_norm_w), pos)
    k = rotary(rms_norm(k.reshape(bsz, L, hk, dh), k_norm_w), pos)
    v = v.reshape(bsz, L, hk, dh)
    q = q.reshape(bsz, nb, blk, hk, grp, dh)

    def band(t):
        tp = jnp.pad(t, ((0, 0), (blk, blk), (0, 0), (0, 0))).reshape(bsz, nb + 2, blk, hk, dh)
        return jnp.concatenate([tp[:, :-2], tp[:, 1:-1], tp[:, 2:]], axis=2)

    kb, vb = band(k), band(v)
    scores = jnp.einsum('bnqkgd,bnskd->bnkgqs', q, kb).astype(f32) * (dh ** -0.5)
    qpos = jnp.arange(nb)[:, None] * blk + jnp.arange(blk)[None, :]
    kpos = jnp.arange(nb)[:, None] * blk - blk + jnp.arange(3 * blk)[None, :]
    rel = kpos[:, None, :] - qpos[:, :, None]
    valid = (jnp.abs(rel) <= WINDOW) & (kpos[:, None, :] >= 0) & (kpos[:, None, :] < L)
    scores = jnp.where(valid[None, :, None, None], scores, -jnp.inf)
    sink_col = jnp.broadcast_to(sink.astype(f32).reshape(hk, grp)[None, None, :, :, None, None],
                                scores.shape[:-1] + (1,))
    probs = jax.nn.softmax(jnp.concatenate([scores, sink_col], axis=-1), axis=-1)[..., :-1]
    out = jnp.einsum('bnkgqs,bnskd->bnqkgd', probs.astype(v.dtype), vb).reshape(bsz, L, hq * dh)
    return out @ w_out

def setup_inputs(seed: int = 0) -> dict:
    key = jax.random.key(seed)
    ks = jax.random.split(key, 24)
    f32 = jnp.float32
    nrm = lambda k, shape, fan_in: jax.random.normal(k, shape, f32) * (fan_in ** -0.5)
    x = jax.random.normal(ks[0], (BATCH, SEQ, D_MODEL), f32)
    norm_w = 1.0 + 0.02 * jax.random.normal(ks[1], (DEPTH, 3, D_MODEL), f32)
    ffn_w_gate = nrm(ks[2], (DEPTH, 2, D_MODEL, D_FF), D_MODEL)
    ffn_w_up = nrm(ks[3], (DEPTH, 2, D_MODEL, D_FF), D_MODEL)
    ffn_w_down = nrm(ks[4], (DEPTH, 2, D_FF, D_MODEL), D_FF)
    ns = N_SSD_LAYERS
    ssd_w_in = nrm(ks[5], (ns, D_MODEL, SSD_IN), D_MODEL)
    ssd_conv_w = nrm(ks[6], (ns, SSD_CONV, SSD_CONV_CH), SSD_CONV)
    ssd_conv_b = 0.02 * jax.random.normal(ks[7], (ns, SSD_CONV_CH), f32)
    dt0 = jnp.exp(jax.random.uniform(ks[8], (ns, 2, SSD_HEADS), f32, np.log(1e-3), np.log(1e-1)))
    ssd_dt_bias = dt0 + jnp.log(-jnp.expm1(-dt0))
    ssd_a_log = jnp.log(jax.random.uniform(ks[9], (ns, 2, SSD_HEADS), f32, 1.0, 16.0))
    ssd_d = 1.0 + 0.1 * jax.random.normal(ks[10], (ns, SSD_HEADS), f32)
    ssd_norm_w = 1.0 + 0.02 * jax.random.normal(ks[11], (ns, SSD_D_INNER), f32)
    ssd_w_out = nrm(ks[12], (ns, SSD_D_INNER, D_MODEL), SSD_D_INNER)
    na = N_ATTN_LAYERS
    attn_w_qkv = nrm(ks[13], (na, D_MODEL, ATTN_QKV), D_MODEL)
    attn_q_norm = 1.0 + 0.02 * jax.random.normal(ks[14], (na, ATTN_HEAD_DIM), f32)
    attn_k_norm = 1.0 + 0.02 * jax.random.normal(ks[15], (na, ATTN_HEAD_DIM), f32)
    attn_sink = 0.5 * jax.random.normal(ks[16], (na, ATTN_HEADS), f32)
    attn_w_out = nrm(ks[17], (na, ATTN_HEADS * ATTN_HEAD_DIM, D_MODEL), ATTN_HEADS * ATTN_HEAD_DIM)
    return {"x": x, "norm_w": norm_w, "ffn_w_gate": ffn_w_gate, "ffn_w_up": ffn_w_up,
            "ffn_w_down": ffn_w_down, "ssd_w_in": ssd_w_in, "ssd_conv_w": ssd_conv_w,
            "ssd_conv_b": ssd_conv_b, "ssd_dt_bias": ssd_dt_bias, "ssd_a_log": ssd_a_log,
            "ssd_d": ssd_d, "ssd_norm_w": ssd_norm_w, "ssd_w_out": ssd_w_out,
            "attn_w_qkv": attn_w_qkv, "attn_q_norm": attn_q_norm, "attn_k_norm": attn_k_norm,
            "attn_sink": attn_sink, "attn_w_out": attn_w_out}

def reference(x, norm_w, ffn_w_gate, ffn_w_up, ffn_w_down, ssd_w_in, ssd_conv_w, ssd_conv_b,
              ssd_dt_bias, ssd_a_log, ssd_d, ssd_norm_w, ssd_w_out, attn_w_qkv, attn_q_norm,
              attn_k_norm, attn_sink, attn_w_out):
    pos = jnp.arange(x.shape[1], dtype=jnp.int32)
    for i in range(DEPTH):
        x = x + 0.5 * swiglu(rms_norm(x, norm_w[i, 0]), ffn_w_gate[i, 0], ffn_w_up[i, 0], ffn_w_down[i, 0])
        h = rms_norm(x, norm_w[i, 1])
        j = i // N_MIXERS
        if i % N_MIXERS == 0:
            x = x + ssd_mixer(h, ssd_w_in[j], ssd_conv_w[j], ssd_conv_b[j], ssd_dt_bias[j],
                              ssd_a_log[j], ssd_d[j], ssd_norm_w[j], ssd_w_out[j])
        else:
            x = x + window_attention(h, attn_w_qkv[j], attn_q_norm[j], attn_k_norm[j],
                                     attn_sink[j], attn_w_out[j], pos)
        x = x + 0.5 * swiglu(rms_norm(x, norm_w[i, 2]), ffn_w_gate[i, 1], ffn_w_up[i, 1], ffn_w_down[i, 1])
    return x


_drawn_inputs = setup_inputs


def setup_inputs(seed=0):
    import zlib

    import numpy as np

    out = dict(_drawn_inputs(seed))
    spreads = {}
    factors = {'ssd_norm_w': 3.846, 'attn_q_norm': 8.0, 'attn_k_norm': 8.0, 'attn_sink': 8.0}
    for name, (base, spread) in spreads.items():
        noise = np.random.default_rng([zlib.crc32(name.encode()), seed]).standard_normal(out[name].shape)
        drawn = base * np.exp(spread * noise) if base else spread * noise
        out[name] = __import__('jax').numpy.asarray(drawn.astype(out[name].dtype))
    for name, factor in factors.items():
        out[name] = (out[name] * factor).astype(out[name].dtype)
    return out
```

```python
from contextlib import ExitStack

import numpy as np
import concourse.bass as bass
from concourse import mybir

F32 = mybir.dt.float32
F32R = mybir.dt.float32r
ALU = mybir.AluOpType
ACT = mybir.ActivationFunctionType
AX_X = mybir.AxisListType.X

P = 128
TOK = 256
NT = TOK // P
D = 1024
KD = D // P
EPS = 1e-6

D_FF = 2816
FB = 256
NBLK = D_FF // FB

INNER = 2048
HEADS = 32
HD = 64
GROUPS = 8
STATE = 128
TAPS = 5
GH = HEADS // GROUPS
GC = GH * HD
NQ = 11

AH = 16
KVH = 4
AD = 64
WINDOW = 128
QKV = (AH + 2 * KVH) * AD

SLAB = KD * 512
PIECE = 2048

WORK = 9300

PHASES = ("ffn", "ssd", "ffn", "ffn", "attn", "ffn")
SLABS_OF = {"ffn": NBLK, "ssd": GROUPS, "attn": 5}
PIECES_OF = {"ffn": NBLK, "ssd": 1 + 2 * GROUPS, "attn": 0}
ROWS_OF = {"ffn": NBLK, "ssd": GROUPS, "attn": KVH}


def before(of, p):
    return sum(of[k] for k in PHASES[:p])


def at(c, i, m):
    return c if i is None else i * m + c


def wait(eng, sem, value):
    if isinstance(value, int) and value <= 0:
        return
    eng.wait_ge(sem, value)


class Own:

    def __init__(self, eng, sem):
        self.eng, self.sem, self.n, self.turn = eng, sem, 0, None

    def done(self, ins):
        ins.then_inc(self.sem, 1)
        self.n += 1

    def wait(self):
        self.eng.wait_ge(self.sem, self.n if self.turn is None else self.turn + self.n)

    def enter(self, i, per):
        self.turn, self.start, self.per = i * per, self.n, per

    def leave(self, turns):
        assert self.n - self.start == self.per, (self.n, self.start, self.per)
        self.turn, self.n = None, self.start + turns * self.per


def build_program(nc, a_dram, b_dram, x_dram, norm_dram, convp_dram, ynw_dram, heads_dram,
                  consts_dram, rows_dram, mask_dram, rope_dram, attn_dram, out_dram):
    last = len(PHASES) - 1

    with ExitStack() as ctx:
        def sb(name, shape, dt=F32):
            return ctx.enter_context(nc.sbuf_tensor(name, shape, dt))

        def sem(name):
            return ctx.enter_context(nc.semaphore(name))

        x = sb("x", [P, NT, D])
        xn = sb("xn", [P, NT, D])
        xT_hi = sb("xT_hi", [P, KD, TOK], F32R)
        xT_lo = sb("xT_lo", [P, KD, TOK], F32R)
        norm_w = sb("norm_w", [P, 2, D])
        raw_a = sb("raw_a", [P, 2, 2, PIECE])
        raw_b = sb("raw_b", [P, PIECE])
        a_hi = sb("a_hi", [P, 2, SLAB], F32R)
        a_lo = sb("a_lo", [P, 2, SLAB], F32R)
        b_hi = sb("b_hi", [P, PIECE], F32R)
        b_lo = sb("b_lo", [P, PIECE], F32R)
        hT_hi = sb("hT_hi", [P, 2, TOK], F32R)
        hT_lo = sb("hT_lo", [P, 2, TOK], F32R)
        consts = sb("consts", [P, 5, P])
        small = sb("small", [P, 16])
        work = sb("work", [P, WORK])

        class Carve:
            def __init__(self):
                self.at = 0

            def __call__(self, *shape):
                n = int(np.prod(shape))
                v = work[:, self.at:self.at + n]
                self.at += n
                assert self.at <= WORK, self.at
                if len(shape) == 1:
                    return v
                names = "abcd"[:len(shape)]
                return v.rearrange(f"p ({' '.join(names)}) -> p {' '.join(names)}",
                                   **dict(zip(names, shape)))

        ident = consts[:, 0, :]
        upto, downto, above, below = (consts[:, i, :] for i in range(1, 5))
        mean_sq, rms, minus_half = small[:, 0:2], small[:, 2:4], small[:, 4:5]
        mean_eps = small[:, 5:7]
        y_ss, y_mean, y_rms = small[:, 8:10], small[:, 10:12], small[:, 12:14]

        banks = [ctx.enter_context(nc.psum_tensor(f"bank{i}", [P, 512], F32)) for i in range(8)]
        acc = banks[0:4]

        small_in = sem("small_in")
        x_in = [sem("x_in0"), sem("x_in1")]
        norm_in = [sem("norm_in0"), sem("norm_in1")]
        a_in = [[sem(f"a_in{s}{h}") for h in range(2)] for s in range(2)]
        b_in = sem("b_in")
        a_hi_made = sem("a_hi_made")
        a_lo_made = sem("a_lo_made")
        a_used = sem("a_used")
        b_hi_made = sem("b_hi_made")
        b_lo_made = sem("b_lo_made")
        b_used = sem("b_used")
        squares = sem("squares")
        rms_made = sem("rms_made")
        xn_made = sem("xn_made")
        xT_put = sem("xT_put")
        xT_hi_made = sem("xT_hi_made")
        xT_lo_made = sem("xT_lo_made")
        gu_put = sem("gu_put")
        silu_made = sem("silu_made")
        h_made = sem("h_made")
        hT_put = sem("hT_put")
        hT_hi_made = sem("hT_hi_made")
        hT_lo_made = sem("hT_lo_made")
        acc_put = sem("acc_put")
        x_made = sem("x_made")
        stored = sem("stored")
        dve_own = sem("dve_own")
        pool_own = sem("pool_own")
        dt_put = sem("dt_put")
        absdt_made = sem("absdt_made")
        exp_dt_made = sem("exp_dt_made")
        da_made = sem("da_made")
        cums_put = sem("cums_put")
        rows_made = sem("rows_made")
        rows_out = sem("rows_out")
        rows_in = sem("rows_in")
        z_put = sem("z_put")
        zs_made = sem("zs_made")
        proj_put = sem("proj_put")
        conv_made = sem("conv_made")
        act_made = sem("act_made")
        cb_put = sem("cb_put")
        cb_made = sem("cb_made")
        xtok_put = sem("xtok_put")
        xtok_made = sem("xtok_made")
        scal_made = sem("scal_made")
        args_made = sem("args_made")
        exps_made = sem("exps_made")
        dtcl_made = sem("dtcl_made")
        m_made = sem("m_made")
        dx_made = sem("dx_made")
        y_put = sem("y_put")
        gated = sem("gated")
        y_squares = sem("y_squares")
        y_sum = sem("y_sum")
        y_rms_made = sem("y_rms_made")
        attn_in = sem("attn_in")
        tables_made = sem("tables_made")
        qkv_put = sem("qkv_put")
        qkv_made = sem("qkv_made")
        sq_made = sem("sq_made")
        ss_made = sem("ss_made")
        head_rms_made = sem("head_rms_made")
        swap_made = sem("swap_made")
        rot_made = sem("rot_made")
        k_made = sem("k_made")
        turn_put = sem("turn_put")
        turn_made = sem("turn_made")
        s_put = sem("s_put")
        shift_made = sem("shift_made")
        probs_made = sem("probs_made")
        probsT_put = sem("probsT_put")
        probsT_hi = sem("probsT_hi")
        probsT_lo = sem("probsT_lo")
        o_put = sem("o_put")
        o_made = sem("o_made")

        block = ctx.enter_context(nc.Block())

        def blocks(eng, body, peel, end, own=None, per=0):
            for c in range(peel):
                body(c, None)
            turns = (end - peel) // 2
            assert peel + 2 * turns == end
            with eng.Fori(0, turns) as i:
                if own:
                    own.enter(i, per)
                for u in range(2):
                    body(peel + u, i)
            if own:
                own.leave(turns)

        def load_slab(sp, c, i):
            for h in range(2):
                wait(sp, a_lo_made, at(2 * c - 3 + h, i, 4))
                src = a_dram[2 * c + h] if i is None else \
                    a_dram[bass.ds(i * 4 + (2 * c + h), 1)].rearrange("a p n -> p (a n)")
                sp.dma_start(raw_a[:, c % 2, h, :], src).then_inc(a_in[c % 2][h], 16)

        def load_b(sp, c, i, m):
            wait(sp, b_lo_made, at(c, i, m))
            src = b_dram[c] if i is None else \
                b_dram[bass.ds(i * m + c, 1)].rearrange("a p n -> p (a n)")
            sp.dma_start(raw_b[:, :], src).then_inc(b_in, 16)

        def split_slab_hi(act, c, i, h):
            act.wait_ge(a_in[c % 2][h], at(16 * (c // 2 + 1), i, 16))
            if h == 0:
                wait(act, a_used, at(c - 1, i, 2))
            act.activation(a_hi[:, c % 2, h * PIECE:(h + 1) * PIECE], raw_a[:, c % 2, h, :],
                           ACT.Copy).then_inc(a_hi_made, 1)

        def split_slab_lo(dve, c, i, h):
            dve.wait_ge(a_hi_made, at(2 * c + h + 1, i, 4))
            dve.tensor_tensor(a_lo[:, c % 2, h * PIECE:(h + 1) * PIECE], raw_a[:, c % 2, h, :],
                              a_hi[:, c % 2, h * PIECE:(h + 1) * PIECE].bitcast(F32),
                              ALU.subtract).then_inc(a_lo_made, 1)

        def split_b_hi(act, c, i, m):
            act.wait_ge(b_in, at(16 * (c + 1), i, 16 * m))
            wait(act, b_used, at(c, i, m))
            act.activation(b_hi[:, :], raw_b[:, :], ACT.Copy).then_inc(b_hi_made, 1)

        def split_b_lo(dve, c, i, m):
            dve.wait_ge(b_hi_made, at(c + 1, i, m))
            dve.tensor_tensor(b_lo[:, :], raw_b[:, :], b_hi[:, :].bitcast(F32),
                              ALU.subtract).then_inc(b_lo_made, 1)

        def three_passes(pe, out, still, moving, first, final):
            mms = (pe.matmul(out, lhsT=still[0], rhs=moving[0], start=first, stop=False),
                   pe.matmul(out, lhsT=still[1], rhs=moving[0], start=False, stop=False),
                   pe.matmul(out, lhsT=still[0], rhs=moving[1], start=False, stop=final))
            return mms[0], mms[2]

        def xT(k, t):
            return xT_hi[:, k, t * P:(t + 1) * P], xT_lo[:, k, t * P:(t + 1) * P]

        def slab(c, k, lo=0, n=512):
            s = k * 512 + lo
            return a_hi[:, c % 2, s:s + n], a_lo[:, c % 2, s:s + n]

        def wait_slab(pe, c, i, k):
            if k % 4 == 0:
                pe.wait_ge(a_lo_made, at(2 * c + k // 4 + 1, i, 4))

        def hT(j, t):
            return hT_hi[:, j, t * P:(t + 1) * P], hT_lo[:, j, t * P:(t + 1) * P]

        def project_rows(pe, q, i, m, rows, first, final, turned=hT):
            pe.wait_ge(hT_lo_made, at(q + 1, i, m))
            for t in range(NT):
                for j in range(2):
                    w = turned(j, t)
                    for half in range(2):
                        s = j * D + half * 512
                        a, b = three_passes(pe, acc[2 * t + half][:, :], w, rows(s),
                                            first and j == 0, final and j == 1)
                        if t == j == half == 0:
                            start = a
                if final:
                    b.then_inc(acc_put, 1)
            return start, b

        def b_rows(s):
            return b_hi[:, s:s + 512], b_lo[:, s:s + 512]

        def norm_act(act, p):
            for t in range(NT):
                if p == 0:
                    act.wait_ge(x_in[t], 16)
                else:
                    act.wait_ge(x_made, 2 * (p - 1) + t + 1)
                act.activation(xn[:, t, :], x[:, t, :], ACT.Square,
                               accum_out=mean_sq[:, t:t + 1]).then_inc(squares, 1)
            for t in range(NT):
                act.wait_ge(xT_put, 2 * p + t + 1)
                for i in range(2):
                    ins = act.activation(xT_hi[:, 4 * i:4 * i + 4, t * P:(t + 1) * P],
                                         banks[4 + 2 * t + i][:, :].rearrange("p (k n) -> p k n", k=4),
                                         ACT.Copy)
                ins.then_inc(xT_hi_made, 1)

        def norm_pool(pool, own, p):
            for t in range(NT):
                pool.wait_ge(squares, 2 * p + t + 1)
                own.done(pool.tensor_scalar(mean_eps[:, t:t + 1], mean_sq[:, t:t + 1], 1.0 / D, EPS,
                                            ALU.mult, ALU.add))
                own.wait()
                pool.tensor_tensor(rms[:, t:t + 1], mean_eps[:, t:t + 1], minus_half,
                                   ALU.pow).then_inc(rms_made, 1)

        def norm_dve(dve, p):
            for t in range(NT):
                dve.wait_ge(rms_made, 2 * p + t + 1)
                if t == 0:
                    dve.wait_ge(norm_in[p % 2], 16 * (p // 2 + 1))
                dve.scalar_tensor_tensor(xn[:, t, :], x[:, t, :], rms[:, t:t + 1], norm_w[:, p % 2, :],
                                         ALU.mult, ALU.mult).then_inc(xn_made, 1)
            for t in range(NT):
                dve.wait_ge(xT_hi_made, 2 * p + t + 1)
                n = slice(t * P, (t + 1) * P)
                for i in range(2):
                    ins = dve.tensor_tensor(xT_lo[:, 4 * i:4 * i + 4, n],
                                            banks[4 + 2 * t + i][:, :].rearrange("p (k n) -> p k n", k=4),
                                            xT_hi[:, 4 * i:4 * i + 4, n].bitcast(F32), ALU.subtract)
                ins.then_inc(xT_lo_made, 1)

        def norm_pe(pe, p):
            for t in range(NT):
                pe.wait_ge(xn_made, 2 * p + t + 1)
                for k in range(KD):
                    mm = pe.transpose(banks[4 + 2 * t + k // 4][:, (k % 4) * P:(k % 4 + 1) * P],
                                      xn[:, t, k * P:(k + 1) * P], ident)
                    if t == k == 0 and p > 0 and PIECES_OF[PHASES[p - 1]]:
                        mm.then_inc(b_used, 1)
                    if t == k == 0 and p > 0 and PHASES[p - 1] == "attn":
                        mm.then_inc(a_used, 1)
                mm.then_inc(xT_put, 1)

        def residual_dve(dve, p, scale):
            for t in range(NT):
                dve.wait_ge(acc_put, 2 * p + t + 1)
                for half in range(2):
                    s = slice(half * 512, (half + 1) * 512)
                    ins = dve.scalar_tensor_tensor(x[:, t, s], acc[2 * t + half][:, :], scale(t),
                                                   x[:, t, s], ALU.mult, ALU.add)
                ins.then_inc(x_made, 1)

        def rows_hi(act, q, i, m, bank):
            act.wait_ge(hT_put, at(q + 1, i, m))
            act.activation(hT_hi[:, :, :], bank[:, :].rearrange("p (j n) -> p j n", j=2),
                           ACT.Copy).then_inc(hT_hi_made, 1)

        def rows_lo(dve, q, i, m, bank):
            dve.wait_ge(hT_hi_made, at(q + 1, i, m))
            dve.tensor_tensor(hT_lo[:, :, :], bank[:, :].rearrange("p (j n) -> p j n", j=2),
                              hT_hi[:, :, :].bitcast(F32), ALU.subtract).then_inc(hT_lo_made, 1)

        gate_up, turned = banks[4:6], banks[6]
        carve = Carve()
        silu_g = carve(NT, FB)
        h = carve(NT, FB)

        def bases(p):
            return (before(SLABS_OF, p), before(PIECES_OF, p), before(ROWS_OF, p),
                    NBLK * sum(k == "ffn" for k in PHASES[:p]))

        def ffn_sync(sp, p):
            a0, b0, _, _ = bases(p)

            def body(c, i):
                load_slab(sp, a0 + c + 1, i)
                load_b(sp, b0 + c, i, 2)

            blocks(sp, body, 2, NBLK - 1)
            if p < last:
                load_slab(sp, a0 + NBLK, None)
            load_b(sp, b0 + NBLK - 1, None, 2)

        def ffn_act(act, p):
            a0, b0, q0, f0 = bases(p)

            def block_act(c, i, split_next=True):
                for t in range(NT):
                    if split_next:
                        split_slab_hi(act, a0 + c + 1, i, t)
                    act.wait_ge(gu_put, at(2 * (f0 + c) + t + 1, i, 4))
                    wait(act, h_made, at(2 * (f0 + c) + t - 1, i, 4))
                    act.activation(silu_g[:, t, :], gate_up[t][:, 0:FB], ACT.Silu).then_inc(silu_made, 1)
                rows_hi(act, q0 + c, i, 2, turned)
                split_b_hi(act, b0 + c, i, 2)

            norm_act(act, p)
            blocks(act, block_act, 2, NBLK - 1)
            block_act(NBLK - 1, None, p < last)

        def ffn_dve(dve, own, p):
            a0, b0, q0, f0 = bases(p)

            def block_dve(c, i, split_next=True):
                for t in range(NT):
                    if split_next:
                        split_slab_lo(dve, a0 + c + 1, i, t)
                    dve.wait_ge(silu_made, at(2 * (f0 + c) + t + 1, i, 4))
                    wait(dve, hT_put, at(q0 + c, i, 2))
                    dve.tensor_tensor(h[:, t, :], gate_up[t][:, FB:2 * FB], silu_g[:, t, :],
                                      ALU.mult).then_inc(h_made, 1)
                rows_lo(dve, q0 + c, i, 2, turned)
                split_b_lo(dve, b0 + c, i, 2)

            norm_dve(dve, p)
            blocks(dve, block_dve, 2, NBLK - 1)
            block_dve(NBLK - 1, None, p < last)
            residual_dve(dve, p, lambda t: 0.5)

        def ffn_pe(pe, p):
            a0, b0, q0, f0 = bases(p)

            def gate_and_up(c, i):
                for t in range(NT):
                    if c == 0:
                        pe.wait_ge(xT_lo_made, 2 * p + t + 1)
                    for k in range(KD):
                        if t == 0:
                            wait_slab(pe, a0 + c, i, k)
                        _, mm = three_passes(pe, gate_up[t][:, :], xT(k, t), slab(a0 + c, k),
                                             k == 0, k == KD - 1)
                    mm.then_inc(gu_put, 1)

            def down(c, i, final=False):
                pe.wait_ge(b_lo_made, at(b0 + c + 1, i, 2))
                return project_rows(pe, q0 + c, i, 2, b_rows, c == 0, final)

            def turn(c, i):
                pe.wait_ge(h_made, at(2 * (f0 + c) + 2, i, 4))
                for t in range(NT):
                    for j in range(2):
                        mm = pe.transpose(turned[:, j * TOK + t * P:j * TOK + (t + 1) * P],
                                          h[:, t, j * P:(j + 1) * P], ident)
                        if c == t == j == 0:
                            mm.then_inc(a_used, 1)
                mm.then_inc(hT_put, 1)

            def block_pe(c, i):
                gate_and_up(c, i)
                if c > 0:
                    start, end = down(c - 1, i)
                    start.then_inc(a_used, 1)
                    end.then_inc(b_used, 1)
                turn(c, i)

            norm_pe(pe, p)
            blocks(pe, block_pe, 3, NBLK)
            down(NBLK - 1, None, final=True)

        proj_bc, proj_x, z_bank, y_bank = banks[4:8]
        carve = Carve()
        chan = carve(4, TOK)
        zs = carve(2, NT * GC)
        x_tok = carve(NT * GC)
        cb_off = carve(2, P)
        cb_upto = carve(2, P)
        cb_downto = carve(2, P)
        decay = carve(GH, 4, P)
        dtcl = carve(GH, 2, P)
        y = carve(NT * GC)
        dx = carve(NT * GC)
        junk = carve(NT, GC)
        table = carve(GROUPS, NQ, GH)
        scal = carve(NQ, GH)
        convp = carve(GROUPS, 4, TAPS + 1)
        ynw = carve(GROUPS, 2)
        heads_in = carve(5, 32)
        ysq = carve(NT, GROUPS)
        dtv = decay.rearrange("p a b c -> p (a b c)")
        rows = xn[:, :, :].rearrange("p t d -> p (t d)").rearrange("p (h d n) -> p h d n", h=GH, d=2)
        rows_flat = xn[:, :, :].rearrange("p t d -> p (t d)")
        v_dt, max_dt, e_dt, s_dt, s2_dt, poly_dt, dt, da = (dtv[:, n * P:(n + 1) * P] for n in range(8))
        dt_bias, a_log, d_skip = (heads_in[:, 0:2, :].rearrange("p a h -> p (a h)"),
                                  heads_in[:, 2:4, :].rearrange("p a h -> p (a h)"), heads_in[:, 4, :])
        exp_a = dtv[:, 8 * P:8 * P + 2 * HEADS]
        rows_sb = dtcl.rearrange("p a b c -> p (a b c)")[0:HEADS, 0:2 * TOK]
        dt_bank, cum_bank, row_bank = acc[0], acc[1], acc[2]
        NF, SD, REM, DTF, DTB, DSKIP = 0, 2, 4, 6, 8, 10

        def z_piece(c):
            return 1 + c if c < 2 else 2 * c - 1

        def ssd_sync(sp, p):
            a0, b0, _, _ = bases(p)

            def body(c, i):
                load_slab(sp, a0 + c + 1, i)
                if c >= 2:
                    load_b(sp, b0 + 2 * c, i, 4)
                load_b(sp, b0 + z_piece(c + 1), i, 4)

            load_b(sp, b0, None, 4)
            load_b(sp, b0 + 1, None, 4)
            blocks(sp, body, 2, GROUPS)
            load_b(sp, b0 + 2 * GROUPS, None, 4)

        def ssd_pool(pool, own, p):
            def scaled(c, i):
                pool.wait_ge(scal_made, at(c, i, 2))
                for j in range(GH):
                    pool.tensor_tensor(dtcl[:, j, :, :], cb_downto,
                                       scal[:, DTB:DTB + 2, j:j + 1].broadcast_to([P, 2, P]),
                                       ALU.mult).then_inc(dtcl_made, 1)
                pool.wait_ge(xtok_made, at(c, i, 2))
                for t in range(NT):
                    s = slice(t * GC, (t + 1) * GC)
                    ins = pool.tensor_tensor(dx[:, s].rearrange("p (h n) -> p h n", h=GH),
                                             x_tok[:, s].rearrange("p (h n) -> p h n", h=GH),
                                             scal[:, DSKIP, :].unsqueeze(2).broadcast_to([P, GH, HD]),
                                             ALU.mult)
                ins.then_inc(dx_made, 1)

            def body(c, i):
                if c >= 1:
                    scaled(c, i)
                    pool.wait_ge(exps_made, at(GH * c, i, 2 * GH))
                pool.wait_ge(rows_out, 16)
                src = rows_dram[c * GH:(c + 1) * GH, :] if i is None else \
                    rows_dram[bass.ds(i * (2 * GH) + c * GH, GH), :]
                pool.dma_start(rows_flat, src.rearrange("h n -> (h n)").unsqueeze(0)
                               .broadcast_to([P, GH * 2 * TOK])).then_inc(rows_in, 16)

            pool.wait_ge(rows_made, 1)
            pool.wait_ge(xT_put, 2 * p + 2)
            pool.dma_start(rows_dram[:, :], rows_sb).then_inc(rows_out, 16)
            pool.wait_ge(rows_out, 16)
            blocks(pool, body, 2, GROUPS)
            scaled(GROUPS, None)
            pool.wait_ge(y_sum, 1)
            own.done(pool.tensor_scalar(y_mean, y_ss, 1.0 / INNER, EPS, ALU.mult, ALU.add))
            own.wait()
            for t in range(NT):
                ins = pool.tensor_tensor(y_rms[:, t:t + 1], y_mean[:, t:t + 1], minus_half, ALU.pow)
            ins.then_inc(y_rms_made, 1)

        def ssd_act(act, p):
            a0, b0, q0, _ = bases(p)

            def y_square(c, i):
                act.wait_ge(gated, at(c + 1, i, 2))
                wait(act, y_squares, at(c, i, 2))
                for t in range(NT):
                    n = ysq[:, t, c:c + 1] if i is None else ysq[:, t, bass.ds(i * 2 + c, 1)]
                    ins = act.activation(junk[:, t, :], y[:, t * GC:(t + 1) * GC], ACT.Square, accum_out=n)
                ins.then_inc(y_squares, 1)

            def y_rows_hi(c, i):
                act.wait_ge(hT_put, at(q0 + c + 1, i, 2))
                for j in range(2):
                    w = ynw[:, c, j:j + 1] if i is None else \
                        ynw[:, bass.ds(i * 2 + c, 1), j:j + 1].rearrange("p a b -> p (a b)")
                    ins = act.activation(hT_hi[:, j, :], y_bank[:, j * TOK:(j + 1) * TOK], ACT.Copy,
                                         scale=w)
                ins.then_inc(hT_hi_made, 1)

            def exps(c, i):
                for j in range(GH):
                    act.wait_ge(args_made, at(GH * c + j + 1, i, 2 * GH))
                    for n in range(2):
                        act.activation(decay[:, j, n, :], decay[:, j, n, :], ACT.Exp,
                                       bias=scal[:, NF + n, j:j + 1])
                    act.activation(decay[:, j, 2, :], rows[:, j, 0, P:2 * P], ACT.Exp,
                                   bias=scal[:, REM, j:j + 1])
                    act.activation(decay[:, j, 3, :], rows[:, j, 1, 0:P], ACT.Exp,
                                   bias=scal[:, REM + 1, j:j + 1]).then_inc(exps_made, 1)

            def body(c, i):
                if c >= 2:
                    y_square(c - 2, i)
                for t in range(2):
                    split_slab_hi(act, a0 + c + 1, i, t)
                act.wait_ge(z_put, at(c + 1, i, 2))
                wait(act, gated, at(c - 1, i, 2))
                act.activation(zs[:, c % 2, :], z_bank[:, :], ACT.Silu).then_inc(zs_made, 1)
                if c >= 2:
                    split_b_hi(act, b0 + 2 * c, i, 4)
                    y_rows_hi(c - 2, i)
                if c >= 1:
                    exps(c - 1, i)
                act.wait_ge(conv_made, at(4 * c + 2, i, 8))
                act.activation(chan[:, 0:2, :], chan[:, 0:2, :], ACT.Silu).then_inc(act_made, 1)
                split_b_hi(act, b0 + z_piece(c + 1), i, 4)
                act.wait_ge(conv_made, at(4 * c + 4, i, 8))
                act.activation(chan[:, 2:4, :], chan[:, 2:4, :], ACT.Silu).then_inc(act_made, 1)
                act.wait_ge(xtok_put, at(c + 1, i, 2))
                wait(act, dx_made, at(c, i, 2))
                act.activation(x_tok, proj_x[:, :], ACT.Copy).then_inc(xtok_made, 1)

            norm_act(act, p)
            split_b_hi(act, b0, None, 4)
            act.wait_ge(absdt_made, 1)
            act.activation(exp_a, a_log, ACT.Exp)
            act.activation(e_dt, v_dt, ACT.Exp, scale=-1.0).then_inc(exp_dt_made, 1)
            split_b_hi(act, b0 + 1, None, 4)
            act.wait_ge(cums_put, 1)
            act.activation(rows_sb, row_bank[0:HEADS, :], ACT.Copy).then_inc(rows_made, 1)
            blocks(act, body, 2, GROUPS)
            y_square(GROUPS - 2, None)
            y_rows_hi(GROUPS - 2, None)
            exps(GROUPS - 1, None)
            split_b_hi(act, b0 + 2 * GROUPS, None, 4)
            y_square(GROUPS - 1, None)
            y_rows_hi(GROUPS - 1, None)

        def ssd_dve(dve, own, p):
            a0, b0, q0, _ = bases(p)

            def discretise():
                dve.wait_ge(dt_put, 1)
                dve.wait_ge(small_in, SMALL_IN)
                for t in range(NT):
                    s = slice(t * 2 * HEADS, (t + 1) * 2 * HEADS)
                    own.done(dve.tensor_tensor(v_dt[:, s], dt_bank[:, s], dt_bias, ALU.add))
                own.wait()
                own.done(dve.tensor_scalar(max_dt, v_dt, 0.0, None, ALU.max))
                own.wait()
                dve.scalar_tensor_tensor(v_dt, v_dt, -1.0, v_dt, ALU.mult, ALU.max).then_inc(absdt_made, 1)
                dve.wait_ge(exp_dt_made, 1)
                own.done(dve.tensor_scalar(s2_dt, e_dt, 2.0, None, ALU.add))
                own.wait()
                own.done(dve.reciprocal(poly_dt, s2_dt))
                own.wait()
                own.done(dve.tensor_tensor(s_dt, e_dt, poly_dt, ALU.mult))
                own.wait()
                own.done(dve.tensor_tensor(s2_dt, s_dt, s_dt, ALU.mult))
                own.wait()
                own.done(dve.tensor_scalar(poly_dt, s2_dt, 1.0 / 15, None, ALU.mult))
                for n in range(6, 0, -1):
                    own.wait()
                    own.done(dve.scalar_tensor_tensor(poly_dt, poly_dt, 1.0 / (2 * n + 1), s2_dt,
                                                      ALU.add, ALU.mult))
                own.wait()
                own.done(dve.scalar_tensor_tensor(poly_dt, poly_dt, 1.0, s_dt, ALU.add, ALU.mult))
                own.wait()
                own.done(dve.scalar_tensor_tensor(dt, poly_dt, 2.0, max_dt, ALU.mult, ALU.add))
                own.wait()
                for t in range(NT):
                    s = slice(t * 2 * HEADS, (t + 1) * 2 * HEADS)
                    ins = dve.scalar_tensor_tensor(da[:, s], dt[:, s], -1.0, exp_a, ALU.mult, ALU.mult)
                ins.then_inc(da_made, 1)

            def fill_table():
                def col(n):
                    return table[:, :, n, :]

                def heads(v):
                    return v.rearrange("p (g h) -> p g h", g=GROUPS)

                def cum(n):
                    return heads(cum_bank[:, n * HEADS:(n + 1) * HEADS])

                for n in range(2):
                    for d in range(2):
                        s = (2 * n + d) * HEADS
                        own.done(dve.tensor_copy(col(DTF + 2 * d + n), heads(dt[:, s:s + HEADS])))
                own.done(dve.tensor_copy(col(DSKIP), heads(d_skip)))
                dve.wait_ge(cums_put, 1)
                for n in range(2):
                    own.done(dve.tensor_scalar(col(NF + n), cum(n), -1.0, None, ALU.mult))
                    own.done(dve.tensor_copy(col(REM + n), cum(4 + n)))
                own.wait()
                for n in range(2):
                    own.done(dve.scalar_tensor_tensor(col(SD + n), col(NF + n), -1.0, cum(2 + n),
                                                      ALU.mult, ALU.subtract))
                own.wait()

            def decay_args(c, i):
                src = table[:, c, :, :] if i is None else \
                    table[:, bass.ds(i * 2 + c, 1), :, :].rearrange("p a q h -> p (a q) h")
                dve.tensor_copy(scal, src).then_inc(scal_made, 1)
                dve.wait_ge(scal_made, at(c + 1, i, 2))
                dve.wait_ge(rows_in, at(16 * (c + 1), i, 32))
                wait(dve, y_put, at(c, i, 2))
                for j in range(GH):
                    for n in range(2):
                        s = slice(n * P, (n + 1) * P)
                        ins = dve.scalar_tensor_tensor(decay[:, j, n, :], rows[:, j, 1, s],
                                                       scal[:, SD + n, j:j + 1], rows[:, j, 0, s],
                                                       ALU.add, ALU.min)
                    ins.then_inc(args_made, 1)

            def head_weights(c, i):
                for j in range(GH):
                    dve.wait_ge(exps_made, at(GH * c + j + 1, i, 2 * GH))
                    dve.wait_ge(dtcl_made, at(GH * c + j + 1, i, 2 * GH))
                    for n in range(2):
                        own.done(dve.scalar_tensor_tensor(dtcl[:, j, n, :], cb_upto[:, n, :],
                                                          scal[:, DTF + n, j:j + 1], dtcl[:, j, n, :],
                                                          ALU.mult, ALU.add))
                    for n in range(2):
                        dve.scalar_tensor_tensor(decay[:, j, 2 + n, :], decay[:, j, 2 + n, :],
                                                 scal[:, (DTF, DTB + 1)[n], j:j + 1], cb_off[:, n, :],
                                                 ALU.mult, ALU.mult)
                    own.wait()
                    dve.tensor_tensor(decay[:, j, 0:2, :], decay[:, j, 0:2, :], dtcl[:, j, :, :],
                                      ALU.mult).then_inc(m_made, 1)

            def convolve(c, i, o):
                bank = (proj_bc, proj_bc, proj_x, proj_x)[o]
                u = bank[:, (o % 2) * TOK:(o % 2 + 1) * TOK]
                out = chan[:, o, :]

                def tap(n):
                    return convp[:, c, o, n:n + 1] if i is None else \
                        convp[:, bass.ds(i * 2 + c, 1), o, n:n + 1].rearrange("p a b -> p (a b)")

                dve.wait_ge(proj_put, at(4 * c + 2 * (o // 2) + 2, i, 8))
                mid = TAPS // 2
                own.done(dve.tensor_scalar(out, u, tap(mid), tap(TAPS), ALU.mult, ALU.add))
                for n in [n for n in range(TAPS) if n != mid]:
                    off = n - mid
                    to = slice(max(0, -off), TOK - max(0, off))
                    frm = slice(max(0, off), TOK - max(0, -off))
                    own.wait()
                    ins = dve.scalar_tensor_tensor(out[:, to], u[:, frm], tap(n), out[:, to],
                                                   ALU.mult, ALU.add)
                    if n < TAPS - 1:
                        own.done(ins)
                ins.then_inc(conv_made, 1)

            def gate(c, i, parity):
                dve.wait_ge(y_put, at(c + 1, i, 2))
                dve.wait_ge(dx_made, at(c + 1, i, 2))
                wait(dve, y_squares, at(c, i, 2))
                wait(dve, hT_put, at(q_base[0] + c, i, 2))
                own.done(dve.tensor_tensor(y, y_bank[:, :], dx, ALU.add))
                own.wait()
                dve.tensor_tensor(y, y, zs[:, parity, :], ALU.mult).then_inc(gated, 1)

            def masked(c, i):
                dve.wait_ge(cb_put, at(c + 1, i, 2))
                for n in range(2):
                    d = proj_bc[:, n * 3 * P:(n * 3 + 1) * P]
                    dve.tensor_tensor(cb_upto[:, n, :], d, upto, ALU.mult)
                    dve.tensor_tensor(cb_downto[:, n, :], d, downto, ALU.mult)
                dve.tensor_copy(cb_off, proj_bc[:, P:3 * P].rearrange("p (a b) -> p a b", a=2)
                                ).then_inc(cb_made, 1)

            def y_rows_lo(c, i):
                dve.wait_ge(hT_hi_made, at(q0 + c + 1, i, 2))
                for j in range(2):
                    w = ynw[:, c, j:j + 1] if i is None else \
                        ynw[:, bass.ds(i * 2 + c, 1), j:j + 1].rearrange("p a b -> p (a b)")
                    ins = dve.scalar_tensor_tensor(hT_lo[:, j, :], y_bank[:, j * TOK:(j + 1) * TOK], w,
                                                   hT_hi[:, j, :].bitcast(F32), ALU.mult, ALU.subtract)
                ins.then_inc(hT_lo_made, 1)

            def body(c, i):
                if c >= 1:
                    decay_args(c - 1, i)
                for t in range(2):
                    split_slab_lo(dve, a0 + c + 1, i, t)
                if c >= 2:
                    split_b_lo(dve, b0 + 2 * c, i, 4)
                    y_rows_lo(c - 2, i)
                wait(dve, cb_put, at(c, i, 2))
                wait(dve, xtok_put, at(c, i, 2))
                convolve(c, i, 0)
                convolve(c, i, 1)
                if c >= 1:
                    head_weights(c - 1, i)
                split_b_lo(dve, b0 + z_piece(c + 1), i, 4)
                convolve(c, i, 2)
                convolve(c, i, 3)
                if c >= 1:
                    gate(c - 1, i, (c - 1) % 2)
                masked(c, i)

            q_base = [q0]
            norm_dve(dve, p)
            split_b_lo(dve, b0, None, 4)
            discretise()
            split_b_lo(dve, b0 + 1, None, 4)
            fill_table()
            blocks(dve, body, 2, GROUPS, own, 2 * (4 * 4 + 2 * GH + 1))
            decay_args(GROUPS - 1, None)
            y_rows_lo(GROUPS - 2, None)
            head_weights(GROUPS - 1, None)
            gate(GROUPS - 1, None, (GROUPS - 1) % 2)
            split_b_lo(dve, b0 + 2 * GROUPS, None, 4)
            y_rows_lo(GROUPS - 1, None)
            dve.wait_ge(y_squares, GROUPS)
            dve.tensor_reduce(y_ss, ysq, AX_X, ALU.add).then_inc(y_sum, 1)
            dve.wait_ge(y_rms_made, 1)
            residual_dve(dve, p, lambda t: y_rms[:, t:t + 1])

        def ssd_pe(pe, p):
            a0, b0, q0, _ = bases(p)

            def z_proj(c, i):
                pe.wait_ge(b_lo_made, at(b0 + z_piece(c) + 1, i, 4))
                wait(pe, zs_made, at(c, i, 2))
                for t in range(NT):
                    for k in range(KD):
                        s = slice(k * GC, (k + 1) * GC)
                        _, mm = three_passes(pe, z_bank[:, t * GC:(t + 1) * GC], xT(k, t),
                                             (b_hi[:, s], b_lo[:, s]), k == 0, k == KD - 1)
                mm.then_inc(z_put, 1)

            def chan_proj(c, i, o):
                bank = (proj_bc, proj_bc, proj_x, proj_x)[o]
                s = ((o + 2) % 4) * P
                for k in range(KD):
                    if o == 0:
                        wait_slab(pe, a0 + c, i, k)
                    first, mm = three_passes(pe, bank[:, (o % 2) * TOK:(o % 2 + 1) * TOK],
                                             slab(a0 + c, k, s, P), (xT_hi[:, k, :], xT_lo[:, k, :]),
                                             k == 0, k == KD - 1)
                    if o == k == 0:
                        first.then_inc(b_used, 1)
                mm.then_inc(proj_put, 1)

            def y_turn(c, i):
                pe.wait_ge(gated, at(c + 1, i, 2))
                for t in range(NT):
                    for j in range(2):
                        mm = pe.transpose(y_bank[:, j * TOK + t * P:j * TOK + (t + 1) * P],
                                          y[:, t * GC + j * P:t * GC + (j + 1) * P], ident)
                mm.then_inc(hT_put, 1)

            def out_rows(c, i, piece, m, final=False):
                pe.wait_ge(b_lo_made, at(b0 + piece + 1, i, m))
                _, end = project_rows(pe, q0 + c, i, 2, b_rows, c == 0, final)
                return end

            def y_heads(c, i):
                pe.wait_ge(m_made, at(GH * (c + 1), i, 2 * GH))
                pe.wait_ge(xtok_made, at(c + 1, i, 2))
                wait(pe, hT_lo_made, at(q0 + c - 1 if c else 0, i, 2))
                for t in range(NT):
                    for j in range(GH):
                        out = y_bank[:, t * GC + j * HD:t * GC + (j + 1) * HD]
                        for s in range(NT):
                            tile = {(0, 0): 0, (1, 1): 1, (0, 1): 2, (1, 0): 3}[s, t]
                            mm = pe.matmul(out, lhsT=decay[:, j, tile, :],
                                           rhs=x_tok[:, s * GC + j * HD:s * GC + (j + 1) * HD],
                                           start=s == 0, stop=s == NT - 1)
                mm.then_inc(y_put, 1)

            def c_dot_b(c, i):
                pe.wait_ge(act_made, at(2 * c + 1, i, 4))
                for s in range(NT):
                    mm = pe.matmul(proj_bc[:, s * TOK:(s + 1) * TOK], lhsT=chan[:, 0, s * P:(s + 1) * P],
                                   rhs=chan[:, 1, :], start=True, stop=True)
                    if s == 0:
                        mm.then_inc(a_used, 1)
                mm.then_inc(cb_put, 1)

            def x_turn(c, i):
                pe.wait_ge(act_made, at(2 * c + 2, i, 4))
                for t in range(NT):
                    for j in range(2):
                        mm = pe.transpose(proj_x[:, t * GC + j * P:t * GC + (j + 1) * P],
                                          chan[:, 2 + j, t * P:(t + 1) * P], ident)
                mm.then_inc(xtok_put, 1)

            def body(c, i):
                z_proj(c, i)
                if c >= 2:
                    y_turn(c - 2, i)
                wait(pe, cb_made, at(c, i, 2))
                chan_proj(c, i, 0)
                chan_proj(c, i, 1)
                if c == 0:
                    cumulate()
                if c >= 2:
                    out_rows(c - 2, i, 2 * c, 4).then_inc(b_used, 1)
                wait(pe, xtok_made, at(c, i, 2))
                chan_proj(c, i, 2)
                chan_proj(c, i, 3)
                if c >= 1:
                    y_heads(c - 1, i)
                c_dot_b(c, i)
                x_turn(c, i)

            def dt_proj():
                pe.wait_ge(b_lo_made, b0 + 1)
                for t in range(NT):
                    pe.wait_ge(xT_lo_made, 2 * p + t + 1)
                    for k in range(KD):
                        s = slice(k * 2 * HEADS, (k + 1) * 2 * HEADS)
                        _, mm = three_passes(pe, dt_bank[:, t * 2 * HEADS:(t + 1) * 2 * HEADS], xT(k, t),
                                             (b_hi[:, s], b_lo[:, s]), k == 0, k == KD - 1)
                mm.then_inc(dt_put, 1)

            def cumulate():
                pe.wait_ge(da_made, 1)
                fwd = [da[:, n * 2 * HEADS:n * 2 * HEADS + HEADS] for n in range(2)]
                bwd = [da[:, n * 2 * HEADS + HEADS:(n + 1) * 2 * HEADS] for n in range(2)]
                for n, (tri, v) in enumerate([(upto, fwd[0]), (upto, fwd[1]), (downto, bwd[0]),
                                              (downto, bwd[1]), (below, fwd[0]), (above, bwd[1])]):
                    pe.matmul(cum_bank[:, n * HEADS:(n + 1) * HEADS], lhsT=tri, rhs=v,
                              start=True, stop=True)
                for n, (tri, v) in enumerate([(upto, fwd[0]), (upto, fwd[1]),
                                              (downto, bwd[0]), (downto, bwd[1])]):
                    mm = pe.matmul(row_bank[0:HEADS, n * P:(n + 1) * P], lhsT=v, rhs=tri,
                                   start=True, stop=True)
                mm.then_inc(cums_put, 1)

            norm_pe(pe, p)
            dt_proj()
            pe.transpose(row_bank[:, 0:P], ident, ident).then_inc(b_used, 1)
            blocks(pe, body, 4, GROUPS)
            y_turn(GROUPS - 2, None)
            out_rows(GROUPS - 2, None, 2 * GROUPS - 1, 4).then_inc(b_used, 1)
            y_heads(GROUPS - 1, None)
            y_turn(GROUPS - 1, None)
            out_rows(GROUPS - 1, None, 2 * GROUPS, 4, final=True)

        STEPS = AH // 2
        carve = Carve()
        q_in = carve(2, NT, 512)
        qT = q_in.rearrange("p a b c -> p a (b c)").rearrange("p a (s n) -> p (a s) n", s=4)
        kv = carve(NT, 512)
        k_twice = carve(NT, KVH, 2, AD)
        prT = k_twice.rearrange("p a b c d -> p (a b c d)").rearrange("p (c s n) -> p c s n", c=4, s=2)
        kT = carve(KVH, TOK)
        k_rot = kT.rearrange("p a b -> p (a b)")[:, 0:NT * 256].rearrange("p (t n) -> p t n", t=NT)
        probs = carve(2, 4, TOK)
        scratch = probs.rearrange("p a b c -> p (a b c)")
        squared = scratch[:, 0:NT * 512].rearrange("p (t n) -> p t n", t=NT)
        swapped = scratch[:, NT * 512:2 * NT * 512].rearrange("p (t n) -> p t n", t=NT)
        q_rot = xn[:, :, :].rearrange("p t d -> p (t d)").rearrange("p (a t n) -> p a t n", a=2, t=NT)
        o = xn
        mask = carve(NT, TOK)
        rope = carve(NT, 2, AD)
        norm_rows = carve(4 * AD + AH)
        rope_w = carve(2, NT, 2, AD)
        head_ss = carve(NT, AH + KVH)
        head_mean = carve(NT, AH + KVH)
        head_rms = carve(NT, AH + KVH)
        half_down = carve(NT, AH)
        minus_sink = carve(AH, NT)
        stats = carve(2, 8, 4)
        PARTS = [(AH, KVH, kv, 0), (0, 8, q_in[:, 0, :, :], 1), (8, 8, q_in[:, 1, :, :], 2)]

        def attn_sync(sp, p):
            a0 = bases(p)[0]
            for c in range(1, 5 + (p < last)):
                load_slab(sp, a0 + c, None)

        def heads64(v, n):
            return v.rearrange("p (h d) -> p h d", h=n)

        def attn_load(pool, p):
            pool.wait_ge(xn_made, 2 * (p - 1) + 2)
            pool.dma_start(mask, mask_dram).then_inc(attn_in, 16)
            pool.dma_start(rope, rope_dram).then_inc(attn_in, 16)
            pool.dma_start(norm_rows, attn_dram.unsqueeze(0).broadcast_to([P, 4 * AD + AH])
                           ).then_inc(attn_in, 16)

        def attn_pool(pool, own, p):
            pool.wait_ge(attn_in, 48)
            for n in range(2):
                for r in range(2):
                    w = norm_rows[:, (2 * n + r) * AD:(2 * n + r + 1) * AD]
                    own.done(pool.tensor_tensor(rope_w[:, n, :, r, :], rope[:, :, r, :],
                                                w.unsqueeze(1).broadcast_to([P, NT, AD]), ALU.mult))
            own.done(pool.memset(half_down, -0.5))
            own.done(pool.tensor_scalar(minus_sink,
                                        norm_rows[:, 4 * AD:].unsqueeze(2).broadcast_to([P, AH, NT]),
                                        -1.0, None, ALU.mult))
            own.wait()
            pool.memset(stats[:, 0, 7, 0:1], 0.0).then_inc(tables_made, 1)
            for h0, nh, src, u in PARTS:
                n = 1 if u == 0 else 0
                for t in range(NT):
                    pool.wait_ge(qkv_made, 2 * u + t + 1)
                    wait(pool, rot_made, 2 * (u - 1) + t + 1)
                    v = heads64(src[:, t, 0:nh * AD], nh)
                    to = heads64(swapped[:, t, 0:nh * AD], nh)
                    half = AD // 2
                    sin = rope_w[:, n, t, 1, :].unsqueeze(1).broadcast_to([P, nh, AD])
                    pool.tensor_tensor(to[:, :, 0:half], v[:, :, half:], sin[:, :, 0:half], ALU.mult)
                    pool.tensor_tensor(to[:, :, half:], v[:, :, 0:half], sin[:, :, half:],
                                       ALU.mult).then_inc(swap_made, 1)
                pool.wait_ge(ss_made, 2 * u + 2)
                s = slice(h0, h0 + nh)
                scale = (1.0 / AD, EPS) if u == 0 else (1.0, AD * EPS)
                own.done(pool.tensor_scalar(head_mean[:, :, s], head_ss[:, :, s], *scale,
                                            ALU.mult, ALU.add))
                own.wait()
                pool.tensor_tensor(head_rms[:, :, s], head_mean[:, :, s], half_down[:, :, 0:nh],
                                   ALU.pow).then_inc(head_rms_made, 1)

        def proj_bank(u, t):
            return banks[2 * u + t]

        def turn_bank(u, s):
            return banks[(6, 0, 2)[u] + s]

        def attn_act(act, p):
            a0, _, q0, _ = bases(p)
            norm_act(act, p)
            for c in (1,):
                for t in range(2):
                    split_slab_hi(act, a0 + c, None, t)

            def take_in(u):
                h0, nh, dst, _ = PARTS[u]
                for t in range(NT):
                    act.wait_ge(qkv_put, 2 * u + t + 1)
                    act.activation(dst[:, t, :], proj_bank(u, t)[:, :], ACT.Copy).then_inc(qkv_made, 1)
                    wait(act, ss_made, 2 * (u - 1) + t + 1)
                    act.activation(squared[:, t, 0:nh * AD], proj_bank(u, t)[:, 0:nh * AD],
                                   ACT.Square).then_inc(sq_made, 1)

            def turned_in(u, dst):
                act.wait_ge(turn_put, u + 1)
                for s in range(2):
                    ins = act.activation(dst[:, 2 * s:2 * s + 2, :],
                                         turn_bank(u, s)[:, :].rearrange("p (a n) -> p a n", a=2), ACT.Copy)
                ins.then_inc(turn_made, 1)

            def exps(n):
                act.wait_ge(shift_made, n + 1)
                st = stats[:, n % 2]
                for c in range(4):
                    act.activation(probs[:, n % 2, c, :], probs[:, n % 2, c, :], ACT.Exp,
                                   bias=st[:, NEG, c:c + 1], accum_out=st[:, DEN, c:c + 1])
                act.activation(st[:, SINK, :], st[:, SINK_ARG, :], ACT.Exp).then_inc(probs_made, 1)

            take_in(0)
            for t in range(2):
                split_slab_hi(act, a0 + 2, None, t)
            take_in(1)
            turned_in(0, kT)
            for t in range(2):
                split_slab_hi(act, a0 + 3, None, t)
            take_in(2)
            turned_in(1, qT[:, 0:4, :])
            turned_in(2, qT[:, 4:8, :])
            exps(0)
            for n in range(STEPS):
                if n + 1 < STEPS:
                    exps(n + 1)
                if n == 0:
                    for t in range(2):
                        split_slab_hi(act, a0 + 4, None, t)
                act.wait_ge(probsT_put, n + 1)
                act.activation(prT[:, 0:2, :, :], banks[2][:, :].rearrange("p (c s n) -> p c s n", c=2, s=2),
                               ACT.Copy).then_inc(probsT_hi, 1)
                if n % 2 == 0 and n >= 2:
                    rows_in_hi(act, q0, n // 2 - 1)
            rows_in_hi(act, q0, KVH - 1)
            if p < last:
                for t in range(2):
                    split_slab_hi(act, a0 + 5, None, t)

        def rows_in_hi(act, q0, j):
            act.wait_ge(hT_put, q0 + j + 1)
            act.activation(xT_hi[:, 2 * j:2 * j + 2, :], banks[1][:, :].rearrange("p (a n) -> p a n", a=2),
                           ACT.Copy).then_inc(hT_hi_made, 1)

        MAX, NEG, DEN, SINK_ARG, SINK, SUM, INV = range(7)

        def attn_dve(dve, own, p):
            a0, _, q0, _ = bases(p)

            def take_squares(u):
                h0, nh, _, _ = PARTS[u]
                for t in range(NT):
                    dve.wait_ge(sq_made, 2 * u + t + 1)
                    dve.tensor_reduce(head_ss[:, t, h0:h0 + nh], heads64(squared[:, t, 0:nh * AD], nh),
                                      AX_X, ALU.add).then_inc(ss_made, 1)

            def rotate(u):
                h0, nh, src, _ = PARTS[u]
                n = 1 if u == 0 else 0
                for t in range(NT):
                    to = k_rot[:, t, :] if u == 0 else q_rot[:, u - 1, t, :]
                    dve.wait_ge(qkv_made, 2 * u + t + 1)
                    own.done(dve.tensor_tensor(heads64(to, nh), heads64(src[:, t, 0:nh * AD], nh),
                                               rope_w[:, n, t, 0, :].unsqueeze(1).broadcast_to([P, nh, AD]),
                                               ALU.mult))
                    own.wait()
                    dve.wait_ge(swap_made, 2 * u + t + 1)
                    dve.tensor_tensor(to, to, swapped[:, t, 0:nh * AD], ALU.add).then_inc(rot_made, 1)

            def softmax_args(n):
                st = stats[:, n % 2]
                dve.wait_ge(s_put, n + 1)
                wait(dve, probsT_put, n - 1)
                for c in range(4):
                    e, t = divmod(c, 2)
                    h = 2 * n + e
                    ins = dve.scalar_tensor_tensor(probs[:, n % 2, c, :],
                                                   banks[4 + 2 * (n % 2) + e][:, t * TOK:(t + 1) * TOK],
                                                   head_rms[:, t, h:h + 1], mask[:, t, :],
                                                   ALU.mult, ALU.add)
                own.done(ins)
                own.wait()
                own.done(dve.tensor_reduce(st[:, MAX, :], probs[:, n % 2, :, :], AX_X, ALU.max))
                own.wait()
                sink = minus_sink[:, 2 * n:2 * n + 2, :].rearrange("p a b -> p (a b)")
                own.done(dve.scalar_tensor_tensor(st[:, NEG, :], st[:, MAX, :], -1.0, sink,
                                                  ALU.mult, ALU.min))
                own.wait()
                dve.tensor_tensor(st[:, SINK_ARG, :], st[:, NEG, :], sink, ALU.subtract
                                  ).then_inc(shift_made, 1)

            def rows_in_lo(j):
                dve.wait_ge(hT_hi_made, q0 + j + 1)
                dve.tensor_tensor(xT_lo[:, 2 * j:2 * j + 2, :],
                                  banks[1][:, :].rearrange("p (a n) -> p a n", a=2),
                                  xT_hi[:, 2 * j:2 * j + 2, :].bitcast(F32), ALU.subtract
                                  ).then_inc(hT_lo_made, 1)

            norm_dve(dve, p)
            for t in range(2):
                split_slab_lo(dve, a0 + 1, None, t)
            dve.wait_ge(tables_made, 1)
            take_squares(0)
            rotate(0)
            dve.wait_ge(head_rms_made, 1)
            dve.wait_ge(rot_made, 2)
            for t in range(NT):
                for r in range(2):
                    ins = dve.tensor_tensor(k_twice[:, t, :, r, :], heads64(k_rot[:, t, :], KVH),
                                            head_rms[:, t, AH:].unsqueeze(2).broadcast_to([P, KVH, AD]),
                                            ALU.mult)
            ins.then_inc(k_made, 1)
            for t in range(2):
                split_slab_lo(dve, a0 + 2, None, t)
            take_squares(1)
            rotate(1)
            for t in range(2):
                split_slab_lo(dve, a0 + 3, None, t)
            take_squares(2)
            rotate(2)
            dve.wait_ge(head_rms_made, 3)
            softmax_args(0)
            for n in range(STEPS):
                if n + 1 < STEPS:
                    softmax_args(n + 1)
                if n == 0:
                    for t in range(2):
                        split_slab_lo(dve, a0 + 4, None, t)
                st = stats[:, n % 2]
                dve.wait_ge(probsT_put, n + 1)
                dve.tensor_copy(prT[:, 2:4, :, :], banks[3][:, :].rearrange("p (c s n) -> p c s n", c=2, s=2)
                                ).then_inc(probsT_lo, 1)
                own.done(dve.tensor_tensor(st[:, SUM, :], st[:, DEN, :], st[:, SINK, :], ALU.add))
                own.wait()
                own.done(dve.reciprocal(st[:, INV, :], st[:, SUM, :]))
                own.wait()
                if n % 2 == 0 and n >= 2:
                    rows_in_lo(n // 2 - 1)
                dve.wait_ge(o_put, n + 1)
                dve.tensor_tensor(o[:, :, 2 * n * AD:(2 * n + 2) * AD].rearrange("p t (e d) -> p e t d", e=2),
                                  banks[n % 2][:, 0:4 * AD].rearrange("p (e t d) -> p e t d", e=2, t=2),
                                  st[:, INV, :].rearrange("p (e t) -> p e t", e=2).unsqueeze(3)
                                  .broadcast_to([P, 2, NT, AD]), ALU.mult).then_inc(o_made, 1)
            rows_in_lo(KVH - 1)
            if p < last:
                for t in range(2):
                    split_slab_lo(dve, a0 + 5, None, t)
            residual_dve(dve, p, lambda t: 1.0)

        def attn_pe(pe, p):
            a0, _, q0, _ = bases(p)

            def project(u):
                for t in range(NT):
                    if u == 0:
                        pe.wait_ge(xT_lo_made, 2 * p + t + 1)
                    for k in range(KD):
                        if t == 0:
                            wait_slab(pe, a0 + u, None, k)
                        first, mm = three_passes(pe, proj_bank(u, t)[:, :], xT(k, t), slab(a0 + u, k),
                                                 k == 0, k == KD - 1)
                        if u > 0 and t == k == 0:
                            first.then_inc(a_used, 1)
                    mm.then_inc(qkv_put, 1)

            def turn(u):
                if u == 0:
                    pe.wait_ge(k_made, 1)
                else:
                    pe.wait_ge(rot_made, 2 * u + 2)
                    pe.wait_ge(sq_made, 2 * u)
                for s in range(4):
                    for t in range(NT):
                        src = k_twice[:, t, s, :, :].rearrange("p a b -> p (a b)") if u == 0 else \
                            q_rot[:, u - 1, t, s * P:(s + 1) * P]
                        mm = pe.transpose(turn_bank(u, s // 2)[:, (s % 2) * TOK + t * P:(s % 2) * TOK + (t + 1) * P],
                                          src, ident)
                        if u == 1 and s == t == 0:
                            mm.then_inc(a_used, 1)
                mm.then_inc(turn_put, 1)

            def scores(n):
                if n < 2:
                    pe.wait_ge(turn_made, 3)
                    pe.wait_ge(sq_made, 6)
                else:
                    pe.wait_ge(shift_made, n - 1)
                for e in range(2):
                    for t in range(NT):
                        mm = pe.matmul(banks[4 + 2 * (n % 2) + e][:, t * TOK:(t + 1) * TOK],
                                       lhsT=qT[e * AD:(e + 1) * AD, n, t * P:(t + 1) * P],
                                       rhs=kT[e * AD:(e + 1) * AD, n // 2, :], start=True, stop=True)
                mm.then_inc(s_put, 1)

            def turn_probs(n):
                pe.wait_ge(probs_made, n + 1)
                wait(pe, probsT_hi, n)
                wait(pe, probsT_lo, n)
                for c in range(4):
                    for s in range(NT):
                        mm = pe.transpose(banks[2 + c // 2][:, ((c % 2) * 2 + s) * P:((c % 2) * 2 + s + 1) * P],
                                          probs[:, n % 2, c, s * P:(s + 1) * P], ident)
                mm.then_inc(probsT_put, 1)

            def values(n):
                pe.wait_ge(probsT_hi, n + 1)
                pe.wait_ge(probsT_lo, n + 1)
                wait(pe, o_made, n - 1)
                if n % 2 and n > 2:
                    pe.wait_ge(hT_lo_made, q0 + n // 2)
                for c in range(4):
                    for s in range(NT):
                        mm = pe.matmul(banks[n % 2][:, c * AD:(c + 1) * AD], lhsT=prT[:, c, s, :],
                                       rhs=kv[:, s, 256 + (n // 2) * AD:256 + (n // 2 + 1) * AD],
                                       start=s == 0, stop=s == NT - 1)
                mm.then_inc(o_put, 1)

            def turn_out(j):
                pe.wait_ge(o_made, 2 * j + 2)
                for t in range(NT):
                    for r in range(2):
                        mm = pe.transpose(banks[1][:, r * TOK + t * P:r * TOK + (t + 1) * P],
                                          o[:, t, (2 * j + r) * P:(2 * j + r + 1) * P], ident)
                mm.then_inc(hT_put, 1)

            norm_pe(pe, p)
            project(0)
            project(1)
            turn(0)
            project(2)
            turn(1)
            turn(2)
            scores(0)
            scores(1)
            for n in range(STEPS):
                turn_probs(n)
                if n + 2 < STEPS:
                    scores(n + 2)
                if n % 2 == 0 and n >= 2:
                    turn_out(n // 2 - 1)
                values(n)
            turn_out(KVH - 1)
            pe.wait_ge(hT_lo_made, q0 + KVH)
            for j in range(KVH):
                c, half = a0 + 3 + j // 2, j % 2
                if half == 0:
                    wait_slab(pe, c, None, 0)
                else:
                    wait_slab(pe, c, None, 4)

                def rows(s, c=c, half=half):
                    s += half * PIECE
                    return a_hi[:, c % 2, s:s + 512], a_lo[:, c % 2, s:s + 512]

                def oT(r, t, j=j):
                    return xT(2 * j + r, t)

                start, _ = project_rows(pe, q0 + j, None, 1, rows, j == 0, j == KVH - 1, oT)
                if j == 2:
                    start.then_inc(a_used, 1)

        ffn = dict(sync=ffn_sync, scalar=ffn_act, vector=ffn_dve, tensor=ffn_pe)
        ssd = dict(sync=ssd_sync, scalar=ssd_act, vector=ssd_dve, tensor=ssd_pe)
        attn = dict(sync=attn_sync, scalar=attn_act, vector=attn_dve, tensor=attn_pe)
        kinds = dict(ffn=ffn, ssd=ssd, attn=attn)

        @block.sync
        def _(sp):
            for t in range(NT):
                sp.dma_start(x[:, t, :], x_dram[0, t * P:(t + 1) * P, :]).then_inc(x_in[t], 16)
            load_slab(sp, 0, None)
            for p, kind in enumerate(PHASES):
                kinds[kind]["sync"](sp, p)
            for t in range(NT):
                sp.wait_ge(x_made, 2 * last + t + 1)
                sp.dma_start(out_dram[0, t * P:(t + 1) * P, :], x[:, t, :]).then_inc(stored, 16)
            sp.wait_ge(stored, 16 * NT)

        @block.gpsimd
        def _(pool):
            own = Own(pool, pool_own)

            def load_norm(p):
                pool.dma_start(norm_w[:, p % 2, :], norm_dram[p:p + 1, :].broadcast_to([P, D])
                               ).then_inc(norm_in[p % 2], 16)

            pool.dma_start(consts[:, :, :], consts_dram).then_inc(small_in, 16)
            load_norm(0)
            for dst, src in ((convp, convp_dram), (ynw, ynw_dram),
                             (heads_in, heads_dram.unsqueeze(0).broadcast_to([P, 5, 32]))):
                pool.dma_start(dst, src).then_inc(small_in, 16)
            load_norm(1)
            own.done(pool.memset(minus_half, -0.5))
            own.wait()
            for p, kind in enumerate(PHASES):
                if kind == "attn":
                    attn_load(pool, p)
                norm_pool(pool, own, p)
                if p + 2 < len(PHASES):
                    pool.wait_ge(xn_made, 2 * p + 2)
                    load_norm(p + 2)
                if kind == "ssd":
                    ssd_pool(pool, own, p)
                elif kind == "attn":
                    attn_pool(pool, own, p)

        @block.scalar
        def _(act):
            for t in range(2):
                split_slab_hi(act, 0, None, t)
            for p, kind in enumerate(PHASES):
                kinds[kind]["scalar"](act, p)

        @block.vector
        def _(dve):
            own = Own(dve, dve_own)
            for t in range(2):
                split_slab_lo(dve, 0, None, t)
            for p, kind in enumerate(PHASES):
                kinds[kind]["vector"](dve, own, p)

        @block.tensor
        def _(pe):
            pe.wait_ge(small_in, SMALL_IN)
            for p, kind in enumerate(PHASES):
                kinds[kind]["tensor"](pe, p)


SMALL_IN = 16 * 4


def lay_out(inputs):
    w_gate, w_up, w_down = (np.asarray(inputs[n]) for n in ("ffn_w_gate", "ffn_w_up", "ffn_w_down"))
    w_in, w_out = np.asarray(inputs["ssd_w_in"])[0], np.asarray(inputs["ssd_w_out"])[0]
    w_qkv, w_o = np.asarray(inputs["attn_w_qkv"])[0], np.asarray(inputs["attn_w_out"])[0]

    def columns(w, *spans):
        w = w.reshape(KD, P, -1)
        return np.concatenate([w[:, :, a:b] for a, b in spans], axis=2).transpose(1, 0, 2)

    def down_rows(w, r):
        return w[r:r + 2 * P].reshape(2, P, D).transpose(1, 0, 2)

    def slabs(m):
        return list(m.reshape(P, 2, PIECE).transpose(1, 0, 2))

    a, b = [], []
    n_ffn = 0
    for kind in PHASES:
        if kind == "ffn":
            layer, which = divmod(n_ffn, 2)
            g, u, dn = w_gate[layer, which], w_up[layer, which], w_down[layer, which]
            for n in range(NBLK):
                s = (n * FB, (n + 1) * FB)
                a += slabs(np.concatenate([columns(g, s), columns(u, s)], axis=2))
                b.append(down_rows(dn, n * FB).reshape(P, PIECE))
            n_ffn += 1
        elif kind == "ssd":
            x0, b0, c0 = INNER, 2 * INNER, 2 * INNER + GROUPS * STATE
            dt0 = c0 + GROUPS * STATE
            for n in range(GROUPS):
                a += slabs(columns(w_in, (x0 + n * GC, x0 + (n + 1) * GC),
                                   (b0 + n * STATE, b0 + (n + 1) * STATE),
                                   (c0 + n * STATE, c0 + (n + 1) * STATE)))
            dtw = columns(w_in, (dt0, dt0 + 2 * HEADS)).reshape(P, -1)
            b.append(np.pad(dtw, ((0, 0), (0, PIECE - dtw.shape[1]))))
            z = [columns(w_in, (n * GC, (n + 1) * GC)).reshape(P, PIECE) for n in range(GROUPS)]
            o = [down_rows(w_out, n * GC).reshape(P, PIECE) for n in range(GROUPS)]
            b += z[0:2]
            for n in range(2, GROUPS):
                b += [z[n], o[n - 2]]
            b += o[GROUPS - 2:]
        else:
            for s in (QKV - 512, QKV), (0, 512), (512, 1024):
                a += slabs(columns(w_qkv, s))
            for n in range(KVH):
                a.append(down_rows(w_o, n * 2 * P).reshape(P, PIECE))
    r = np.arange(P)
    consts = np.stack([r[:, None] == r, r[:, None] <= r, r[:, None] >= r,
                       r[:, None] < r, r[:, None] > r], axis=1).astype(np.float32)
    cw = np.asarray(inputs["ssd_conv_w"])[0]
    cb = np.asarray(inputs["ssd_conv_b"])
    params = np.concatenate([cw, cb], axis=0)
    px, pb, pc = params[:, :INNER], params[:, INNER:INNER + 1024], params[:, INNER + 1024:]
    tiles = np.stack([pb.reshape(6, GROUPS, P), pc.reshape(6, GROUPS, P),
                      px.reshape(6, GROUPS, 2, P)[:, :, 0], px.reshape(6, GROUPS, 2, P)[:, :, 1]], axis=2)
    half = AD // 2
    inv_freq = np.float32(10000.0) ** (-np.arange(half, dtype=np.float32) / np.float32(half))
    angle = np.arange(TOK, dtype=np.float32)[:, None] * inv_freq[None, :].astype(np.float32)
    cos, sin = np.cos(angle), np.sin(angle)
    rope = np.stack([np.concatenate([cos, cos], axis=1), np.concatenate([-sin, sin], axis=1)], axis=1)
    rope = rope.reshape(NT, P, 2, AD).transpose(1, 0, 2, 3).astype(np.float32)
    tok = np.arange(TOK)
    mask = np.where(np.abs(tok[:, None] - tok[None, :]) <= WINDOW, 0.0, -3e38).astype(np.float32)
    qn, kn = np.asarray(inputs["attn_q_norm"])[0], np.asarray(inputs["attn_k_norm"])[0]
    return {
        "mask": np.ascontiguousarray(mask.reshape(NT, P, TOK).transpose(1, 0, 2)),
        "rope": np.ascontiguousarray(rope),
        "attn": np.concatenate([qn, qn[half:], qn[:half], kn, kn[half:], kn[:half],
                                np.asarray(inputs["attn_sink"])[0]]),
        "a": np.stack(a), "b": np.stack(b), "x": np.asarray(inputs["x"]),
        "norm": np.asarray(inputs["norm_w"]).reshape(-1, D),
        "convp": np.ascontiguousarray(tiles.transpose(3, 1, 2, 0)),
        "ynw": np.ascontiguousarray(np.asarray(inputs["ssd_norm_w"])[0].reshape(GROUPS, 2, P).transpose(2, 0, 1)),
        "heads": np.concatenate([np.asarray(inputs["ssd_dt_bias"])[0], np.asarray(inputs["ssd_a_log"])[0],
                                 np.asarray(inputs["ssd_d"])], axis=0),
        "consts": consts,
    }


def kernel(**inputs):
    import concourse.bacc as bacc
    from concourse.bass_utils import run_bass_kernel_spmd

    nc = bacc.Bacc("TRN2", target_bir_lowering=False, num_devices=1)
    arrays, drams = {}, {}
    for name, a in lay_out(inputs).items():
        arrays[f"in_{name}"] = a
        drams[name] = nc.dram_tensor(f"in_{name}", a.shape, mybir.dt.from_np(a.dtype),
                                     kind="ExternalInput").ap()
    rows = nc.dram_tensor("cum_rows", (HEADS, 2 * TOK), F32, kind="Internal").ap()
    out = nc.dram_tensor("out_0", (1, TOK, D), F32, kind="ExternalOutput").ap()
    build_program(nc, drams["a"], drams["b"], drams["x"], drams["norm"], drams["convp"],
                  drams["ynw"], drams["heads"], drams["consts"], rows,
                  drams["mask"], drams["rope"], drams["attn"], out)
    return run_bass_kernel_spmd(nc, [arrays], core_ids=[0]).results[0]["out_0"]
```

```python
from contextlib import ExitStack

import numpy as np
import concourse.bass as bass
from concourse import mybir

F32 = mybir.dt.float32
F32R = mybir.dt.float32r
ALU = mybir.AluOpType
ACT = mybir.ActivationFunctionType
AX_X = mybir.AxisListType.X

P = 128
TOK = 256
NT = TOK // P
D = 1024
KD = D // P
EPS = 1e-6

D_FF = 2816
FB = 256
NBLK = D_FF // FB

INNER = 2048
HEADS = 32
HD = 64
GROUPS = 8
STATE = 128
TAPS = 5
GH = HEADS // GROUPS
GC = GH * HD
NQ = 10

AH = 16
KVH = 4
AD = 64
WINDOW = 128
QKV = (AH + 2 * KVH) * AD

SLAB = KD * 512
PIECE = 2048

WORK = 9300

PHASES = ("ffn", "ssd", "ffn", "ffn", "attn", "ffn")
SLABS_OF = {"ffn": NBLK, "ssd": GROUPS, "attn": 5}
PIECES_OF = {"ffn": NBLK, "ssd": 2 * GROUPS, "attn": 0}
ROWS_OF = {"ffn": NBLK + 1, "ssd": GROUPS, "attn": KVH}


def before(of, p):
    return sum(of[k] for k in PHASES[:p])


def at(c, i, m):
    return c if i is None else i * m + c


def wait(eng, sem, value):
    if isinstance(value, int) and value <= 0:
        return
    eng.wait_ge(sem, value)


class Own:

    def __init__(self, eng, sem):
        self.eng, self.sem, self.n, self.turn = eng, sem, 0, None

    def count(self, n=0):
        return self.n + n if self.turn is None else self.turn + (self.n + n)

    def done(self, ins):
        ins.then_inc(self.sem, 1)
        self.n += 1

    def wait(self):
        self.eng.wait_ge(self.sem, self.count())

    def enter(self, i, per):
        self.turn, self.start, self.per = i * per, self.n, per

    def leave(self, turns):
        assert self.n - self.start == self.per, (self.n, self.start, self.per)
        self.turn, self.n = None, self.start + turns * self.per


def build_program(nc, a_dram, b_dram, x_dram, norm_dram, convp_dram, chan_dram, heads_dram, dtw_dram,
                  ident_dram, consts_dram, rows_dram, mask_dram, rope_dram, attn_dram, out_dram):
    last = len(PHASES) - 1

    with ExitStack() as ctx:
        def sb(name, shape, dt=F32):
            return ctx.enter_context(nc.sbuf_tensor(name, shape, dt))

        def sem(name):
            return ctx.enter_context(nc.semaphore(name))

        x = sb("x", [P, NT, D])
        xn = sb("xn", [P, NT, D])
        xT_hi = sb("xT_hi", [P, KD, TOK], F32R)
        xT_lo = sb("xT_lo", [P, KD, TOK], F32R)
        norm_w = sb("norm_w", [P, 2, D])
        raw_a = sb("raw_a", [P, 2, 2, PIECE])
        raw_b = sb("raw_b", [P, PIECE])
        a_hi = sb("a_hi", [P, 2, SLAB], F32R)
        a_lo = sb("a_lo", [P, 2, SLAB], F32R)
        b_hi = sb("b_hi", [P, PIECE], F32R)
        b_lo = sb("b_lo", [P, PIECE], F32R)
        hT_hi = sb("hT_hi", [P, 2, TOK], F32R)
        hT_lo = sb("hT_lo", [P, 2, TOK], F32R)
        ident = sb("ident", [P, P])[:, :]
        consts = sb("consts", [P, 4, P])
        small = sb("small", [P, 16])
        with nc.sbuf_tensor("b2_hi", [P, PIECE], F32R) as b2_hi, \
                nc.sbuf_tensor("b2_lo", [P, PIECE], F32R) as b2_lo:
            pass
        work = sb("work", [P, WORK])

        class Carve:
            def __init__(self):
                self.at = 0

            def __call__(self, *shape):
                n = int(np.prod(shape))
                v = work[:, self.at:self.at + n]
                self.at += n
                assert self.at <= WORK, self.at
                if len(shape) == 1:
                    return v
                names = "abcd"[:len(shape)]
                return v.rearrange(f"p ({' '.join(names)}) -> p {' '.join(names)}",
                                   **dict(zip(names, shape)))

        carve = Carve()
        carve(2, PIECE)
        b_slots = [(raw_b[:, :], b_hi[:, :], b_lo[:, :]), (carve(PIECE), b2_hi[:, :], b2_lo[:, :])]
        silu_g = carve(NT, FB)
        h = carve(NT, FB)
        FFN_WORK = carve.at

        upto, downto, above, below = (consts[:, i, :] for i in range(4))
        mean_sq, rms, minus_half = small[:, 0:2], small[:, 2:4], small[:, 4:5]
        mean_eps = small[:, 5:7]
        y_ss, y_mean, y_rms = small[:, 8:10], small[:, 10:12], small[:, 12:14]

        banks = [ctx.enter_context(nc.psum_tensor(f"bank{i}", [P, 512], F32)) for i in range(8)]
        acc = banks[0:4]

        ident_in = sem("ident_in")
        small_in = sem("small_in")
        x_in = [sem("x_in0"), sem("x_in1")]
        first_norm_in = sem("first_norm_in")
        norm_in = [sem("norm_in0"), sem("norm_in1")]
        a_in = [[sem(f"a_in{s}{h}") for h in range(2)] for s in range(2)]
        b_in = [sem("b_in0"), sem("b_in1")]
        a_hi_made = sem("a_hi_made")
        a_lo_made = sem("a_lo_made")
        a_used = sem("a_used")
        b_hi_made = sem("b_hi_made")
        b_lo_made = sem("b_lo_made")
        b_used = sem("b_used")
        squares = sem("squares")
        rms_made = sem("rms_made")
        xn_made = sem("xn_made")
        xT_put = sem("xT_put")
        xT_hi_made = sem("xT_hi_made")
        xT_lo_made = sem("xT_lo_made")
        gu_put = sem("gu_put")
        silu_made = sem("silu_made")
        h_made = sem("h_made")
        hT_put = sem("hT_put")
        hT_hi_made = sem("hT_hi_made")
        hT_lo_made = sem("hT_lo_made")
        acc_put = sem("acc_put")
        x_made = sem("x_made")
        stored = sem("stored")
        dve_own = sem("dve_own")
        pool_own = sem("pool_own")
        dt_hi_made = sem("dt_hi_made")
        dt_lo_made = sem("dt_lo_made")
        dt_put = sem("dt_put")
        absdt_made = sem("absdt_made")
        exp_dt_made = sem("exp_dt_made")
        da_made = sem("da_made")
        cums_put = sem("cums_put")
        rows_made = sem("rows_made")
        rows_out = sem("rows_out")
        rows_in = sem("rows_in")
        z_put = sem("z_put")
        zs_made = sem("zs_made")
        proj_put = sem("proj_put")
        conv_made = sem("conv_made")
        act_made = sem("act_made")
        cb_put = sem("cb_put")
        cb_made = sem("cb_made")
        xtok_put = sem("xtok_put")
        xtok_made = sem("xtok_made")
        scal_made = sem("scal_made")
        args_made = sem("args_made")
        exps_made = sem("exps_made")
        weights_made = sem("weights_made")
        m_made = sem("m_made")
        y_put = sem("y_put")
        gated = sem("gated")
        y_squares = sem("y_squares")
        squares_added = sem("squares_added")
        y_sum_put = sem("y_sum_put")
        y_sum = sem("y_sum")
        y_rms_made = sem("y_rms_made")
        attn_in = sem("attn_in")
        tables_made = sem("tables_made")
        qkv_put = sem("qkv_put")
        qkv_made = sem("qkv_made")
        sq_made = sem("sq_made")
        ss_made = sem("ss_made")
        head_rms_made = sem("head_rms_made")
        swap_made = sem("swap_made")
        rot_made = sem("rot_made")
        k_made = sem("k_made")
        turn_put = sem("turn_put")
        turn_made = sem("turn_made")
        s_put = sem("s_put")
        shift_made = sem("shift_made")
        probs_made = sem("probs_made")
        probsT_put = sem("probsT_put")
        probsT_hi = sem("probsT_hi")
        probsT_lo = sem("probsT_lo")
        o_put = sem("o_put")
        o_made = sem("o_made")

        block = ctx.enter_context(nc.Block())

        def blocks(eng, body, peel, end, own=None, per=0, first=0):
            for c in range(first, peel):
                body(c, None)
            turns = (end - peel) // 2
            assert peel + 2 * turns == end
            with eng.Fori(0, turns) as i:
                if own:
                    own.enter(i, per)
                for u in range(2):
                    body(peel + u, i)
            if own:
                own.leave(turns)

        def load_slab(sp, c, i, parts=range(2)):
            for h in parts:
                wait(sp, a_lo_made, at(2 * c - 3 + h, i, 4))
                src = a_dram[2 * c + h] if i is None else \
                    a_dram[bass.ds(i * 4 + (2 * c + h), 1)].rearrange("a p n -> p (a n)")
                sp.dma_start(raw_a[:, c % 2, h, :], src).then_inc(a_in[c % 2][h], 16)

        def load_b(sp, c, i, m, slot=0, split=None):
            wait(sp, b_lo_made, at(c if split is None else split, i, m))
            src = b_dram[c] if i is None else \
                b_dram[bass.ds(i * m + c, 1)].rearrange("a p n -> p (a n)")
            sp.dma_start(b_slots[slot][0], src).then_inc(b_in[slot], 16)

        def split_slab_hi(act, c, i, h):
            act.wait_ge(a_in[c % 2][h], at(16 * (c // 2 + 1), i, 16))
            if h == 0:
                wait(act, a_used, at(c - 1, i, 2))
            act.activation(a_hi[:, c % 2, h * PIECE:(h + 1) * PIECE], raw_a[:, c % 2, h, :],
                           ACT.Copy).then_inc(a_hi_made, 1)

        def split_slab_lo(dve, c, i, h):
            dve.wait_ge(a_hi_made, at(2 * c + h + 1, i, 4))
            dve.tensor_tensor(a_lo[:, c % 2, h * PIECE:(h + 1) * PIECE], raw_a[:, c % 2, h, :],
                              a_hi[:, c % 2, h * PIECE:(h + 1) * PIECE].bitcast(F32),
                              ALU.subtract).then_inc(a_lo_made, 1)

        def split_b_hi(act, c, i, m, loads, ml, slot=0, used=None):
            act.wait_ge(b_in[slot], at(16 * loads, i, 16 * ml))
            wait(act, b_used, at(c if used is None else used, i, m))
            act.activation(b_slots[slot][1], b_slots[slot][0], ACT.Copy).then_inc(b_hi_made, 1)

        def split_b_lo(dve, c, i, m, slot=0):
            dve.wait_ge(b_hi_made, at(c + 1, i, m))
            raw, hi, lo = b_slots[slot]
            dve.tensor_tensor(lo, raw, hi.bitcast(F32), ALU.subtract).then_inc(b_lo_made, 1)

        def three_passes(pe, out, still, moving, first, final):
            mms = (pe.matmul(out, lhsT=still[0], rhs=moving[0], start=first, stop=False),
                   pe.matmul(out, lhsT=still[1], rhs=moving[0], start=False, stop=False),
                   pe.matmul(out, lhsT=still[0], rhs=moving[1], start=False, stop=final))
            return mms[0], mms[2]

        def xT(k, t):
            return xT_hi[:, k, t * P:(t + 1) * P], xT_lo[:, k, t * P:(t + 1) * P]

        def slab(c, k, lo=0, n=512):
            s = k * 512 + lo
            return a_hi[:, c % 2, s:s + n], a_lo[:, c % 2, s:s + n]

        def wait_slab(pe, c, i, k):
            if k % 4 == 0:
                pe.wait_ge(a_lo_made, at(2 * c + k // 4 + 1, i, 4))

        def hT(j, t):
            return hT_hi[:, j, t * P:(t + 1) * P], hT_lo[:, j, t * P:(t + 1) * P]

        def project_rows(pe, q, i, m, rows, first, final, turned=hT, tiles=range(NT)):
            pe.wait_ge(hT_lo_made, at(q + 1, i, m))
            start = None
            for t in tiles:
                for j in range(2):
                    w = turned(j, t)
                    for half in range(2):
                        s = j * D + half * 512
                        a, b = three_passes(pe, acc[2 * t + half][:, :], w, rows(s),
                                            first and j == 0, final and j == 1)
                        start = start or a
                if final:
                    b.then_inc(acc_put, 1)
            return start, b

        def b_rows(slot):
            _, hi, lo = b_slots[slot]
            return lambda s: (hi[:, s:s + 512], lo[:, s:s + 512])

        def late_rms(p):
            return PHASES[p] == "ffn"

        def halves(p, t, half):
            return 4 * p + 2 * t + half + 1

        def norm_bank(t, half):
            return banks[((4, 7), (5, 6))[t][half]]

        def square_act(act, p, t):
            if p == 0:
                act.wait_ge(x_in[t], 16)
            else:
                act.wait_ge(x_made, 2 * (p - 1) + t + 1)
            if late_rms(p):
                act.wait_ge(xT_put, halves(p, t, 1))
            act.activation(xn[:, t, :], x[:, t, :], ACT.Square,
                           accum_out=mean_sq[:, t:t + 1]).then_inc(squares, 1)

        def norm_act_early(act, p, t):
            if not late_rms(p):
                square_act(act, p, t)

        def norm_act(act, p, t):
            for half in range(2):
                act.wait_ge(xT_put, halves(p, t, half))
                act.activation(xT_hi[:, 4 * half:4 * half + 4, t * P:(t + 1) * P],
                               norm_bank(t, half)[:, :].rearrange("p (k n) -> p k n", k=4),
                               ACT.Copy).then_inc(xT_hi_made, 1)
            if late_rms(p):
                square_act(act, p, t)

        def norm_pool(pool, own, p):
            for t in range(NT):
                pool.wait_ge(squares, 2 * p + t + 1)
                own.done(pool.tensor_scalar(mean_eps[:, t:t + 1], mean_sq[:, t:t + 1], 1.0 / D, EPS,
                                            ALU.mult, ALU.add))
                own.wait()
                pool.tensor_tensor(rms[:, t:t + 1], mean_eps[:, t:t + 1], minus_half,
                                   ALU.pow).then_inc(rms_made, 1)

        def norm_dve(dve, p, t):
            if p == 0:
                dve.wait_ge(x_in[t], 16)
            else:
                dve.wait_ge(x_made, 2 * (p - 1) + t + 1)
            if t == 0 and p == 0:
                dve.wait_ge(first_norm_in, 16)
            elif t == 0:
                dve.wait_ge(norm_in[p % 2], 16 * ((p + 1) // 2))
            if not late_rms(p):
                dve.wait_ge(rms_made, 2 * p + t + 1)
            for half in range(2):
                s = slice(half * 512, (half + 1) * 512)
                if late_rms(p):
                    ins = dve.tensor_tensor(xn[:, t, s], x[:, t, s], norm_w[:, p % 2, s], ALU.mult)
                else:
                    ins = dve.scalar_tensor_tensor(xn[:, t, s], x[:, t, s], rms[:, t:t + 1],
                                                   norm_w[:, p % 2, s], ALU.mult, ALU.mult)
                ins.then_inc(xn_made, 1)

        def norm_lo_dve(dve, p, t):
            n = slice(t * P, (t + 1) * P)
            for half in range(2):
                k = slice(4 * half, 4 * half + 4)
                dve.wait_ge(xT_hi_made, halves(p, t, half))
                dve.tensor_tensor(xT_lo[:, k, n],
                                  norm_bank(t, half)[:, :].rearrange("p (k n) -> p k n", k=4),
                                  xT_hi[:, k, n].bitcast(F32), ALU.subtract).then_inc(xT_lo_made, 1)

        def norm_pe(pe, p, t):
            for half in range(2):
                pe.wait_ge(xn_made, halves(p, t, half))
                for k in range(4):
                    mm = pe.transpose(norm_bank(t, half)[:, k * P:(k + 1) * P],
                                      xn[:, t, (4 * half + k) * P:(4 * half + k + 1) * P], ident)
                mm.then_inc(xT_put, 1)

        def first_product(mm, p):
            if p > 0:
                mm.then_inc(b_used if PIECES_OF[PHASES[p - 1]] else a_used, 1)

        def residual_dve(dve, p, t, scale):
            dve.wait_ge(acc_put, 2 * p + t + 1)
            for half in range(2):
                s = slice(half * 512, (half + 1) * 512)
                ins = dve.scalar_tensor_tensor(x[:, t, s], acc[2 * t + half][:, :], scale,
                                               x[:, t, s], ALU.mult, ALU.add)
            ins.then_inc(x_made, 1)

        def end_dve(dve, p, scale):
            residual_dve(dve, p, 0, scale(0))
            if p < last:
                norm_dve(dve, p + 1, 0)
            residual_dve(dve, p, 1, scale(1))
            if p < last:
                norm_lo_dve(dve, p + 1, 0)

        def rows_hi(act, q, i, m, bank, tiles=range(NT)):
            act.wait_ge(hT_put, at(q + 1, i, m))
            n = slice(tiles[0] * P, (tiles[-1] + 1) * P)
            act.activation(hT_hi[:, :, n], bank[:, :].rearrange("p (j n) -> p j n", j=2)[:, :, n],
                           ACT.Copy).then_inc(hT_hi_made, 1)

        def rows_lo(dve, q, i, m, bank, tiles=range(NT)):
            dve.wait_ge(hT_hi_made, at(q + 1, i, m))
            n = slice(tiles[0] * P, (tiles[-1] + 1) * P)
            dve.tensor_tensor(hT_lo[:, :, n], bank[:, :].rearrange("p (j n) -> p j n", j=2)[:, :, n],
                              hT_hi[:, :, n].bitcast(F32), ALU.subtract).then_inc(hT_lo_made, 1)

        gate_up, turned = banks[4:6], banks[6]

        def turns_before(p):
            return sum(ROWS_OF[k] for k in PHASES[:p] if k != "ssd")

        def bases(p):
            return (before(SLABS_OF, p), before(PIECES_OF, p), before(ROWS_OF, p),
                    NBLK * sum(k == "ffn" for k in PHASES[:p]))

        def slot_loads(p, c):
            ffn_before = sum(k == "ffn" for k in PHASES[:p])
            if c % 2:
                return ffn_before * (NBLK // 2) + c // 2 + 1
            return before(PIECES_OF, p) - ffn_before * (NBLK // 2) + c // 2 + 1

        def ffn_sync(sp, p):
            a0, b0, _, _ = bases(p)

            def load_rows(c, i):
                if c == 1 and p > 0:
                    sp.wait_ge(x_made, 2 * p)
                load_b(sp, b0 + c, i, 2, slot=c % 2, split=b0 + max(c - 1, 0))

            def body(c, i):
                load_slab(sp, a0 + c + 1, i)
                load_rows(c, i)

            blocks(sp, body, 2, NBLK - 1)
            if p < last:
                load_slab(sp, a0 + NBLK, None)
            load_rows(NBLK - 1, None)

        def ffn_act(act, p):
            a0, b0, q0, f0 = bases(p)

            def silu(c, i, t):
                if c == 0:
                    act.wait_ge(rms_made, 2 * p + t + 1)
                act.wait_ge(gu_put, at(2 * (f0 + c) + t + 1, i, 4))
                wait(act, h_made, at(2 * (f0 + c) + t - 1, i, 4))
                act.activation(silu_g[:, t, :], gate_up[t][:, 0:FB], ACT.Silu,
                               scale=rms[:, t:t + 1]).then_inc(silu_made, 1)

            def split_rows(c, i):
                split_b_hi(act, b0 + c, i, 2, loads=slot_loads(p, c), ml=1, slot=c % 2,
                           used=b0 + max(c - 1, 0))

            def block_act(c, i):
                for t in range(NT):
                    split_slab_hi(act, a0 + c + 1, i, t)
                    silu(c, i, t)
                rows_hi(act, turns_before(p) + c, i, 2, turned)
                split_rows(c, i)

            norm_act_early(act, p, 1)
            norm_act(act, p, 1)
            blocks(act, block_act, 2, NBLK - 1)
            c = NBLK - 1
            if p < last:
                split_slab_hi(act, a0 + NBLK, None, 0)
            silu(c, None, 0)
            split_rows(c, None)
            rows_hi(act, turns_before(p) + c, None, 2, turned, tiles=(0,))
            if p < last:
                split_slab_hi(act, a0 + NBLK, None, 1)
            silu(c, None, 1)
            if p < last:
                norm_act_early(act, p + 1, 0)
            rows_hi(act, turns_before(p) + c + 1, None, 2, turned, tiles=(1,))
            if p < last:
                norm_act(act, p + 1, 0)

        def ffn_dve(dve, own, p):
            a0, b0, q0, f0 = bases(p)

            def times_up(c, i, t):
                dve.wait_ge(silu_made, at(2 * (f0 + c) + t + 1, i, 4))
                wait(dve, hT_put, at(turns_before(p) + c, i, 2))
                dve.scalar_tensor_tensor(h[:, t, :], gate_up[t][:, FB:2 * FB], rms[:, t:t + 1],
                                         silu_g[:, t, :], ALU.mult, ALU.mult).then_inc(h_made, 1)

            def block_dve(c, i):
                for t in range(NT):
                    split_slab_lo(dve, a0 + c + 1, i, t)
                    times_up(c, i, t)
                rows_lo(dve, q0 + c, i, 2, turned)
                split_b_lo(dve, b0 + c, i, 2, slot=c % 2)

            norm_dve(dve, p, 1)
            norm_lo_dve(dve, p, 1)
            blocks(dve, block_dve, 2, NBLK - 1)
            c = NBLK - 1
            if p < last:
                split_slab_lo(dve, a0 + NBLK, None, 0)
            times_up(c, None, 0)
            split_b_lo(dve, b0 + c, None, 2, slot=0)
            rows_lo(dve, q0 + c, None, 2, turned, tiles=(0,))
            if p < last:
                split_slab_lo(dve, a0 + NBLK, None, 1)
            times_up(c, None, 1)
            residual_dve(dve, p, 0, 0.5)
            if p < last:
                norm_dve(dve, p + 1, 0)
            rows_lo(dve, q0 + c + 1, None, 2, turned, tiles=(1,))
            if p < last:
                norm_lo_dve(dve, p + 1, 0)
            residual_dve(dve, p, 1, 0.5)

        def ffn_pe(pe, p):
            a0, b0, q0, f0 = bases(p)

            def gate_and_up(c, i, t):
                for k in range(KD):
                    if t == 0:
                        wait_slab(pe, a0 + c, i, k)
                    if c == 0 and k % 4 == 0:
                        pe.wait_ge(xT_lo_made, halves(p, t, k // 4))
                    a, mm = three_passes(pe, gate_up[t][:, :], xT(k, t), slab(a0 + c, k),
                                         k == 0, k == KD - 1)
                    if k == 0:
                        first = a
                    if c == t == 0 and k == 3:
                        norm_pe(pe, p, 1)
                mm.then_inc(gu_put, 1)
                return first

            def down(c, i, final=False, tiles=range(NT)):
                pe.wait_ge(b_lo_made, at(b0 + c + 1, i, 2))
                q = q0 + c + (tiles == (1,) and c == NBLK - 1)
                return project_rows(pe, q, i, 2, b_rows(c % 2), c == 0, final, tiles=tiles)

            def turn(c, i, t):
                pe.wait_ge(h_made, at(2 * (f0 + c) + t + 1, i, 4))
                for j in range(2):
                    mm = pe.transpose(turned[:, j * TOK + t * P:j * TOK + (t + 1) * P],
                                      h[:, t, j * P:(j + 1) * P], ident)
                    if c == t == j == 0:
                        mm.then_inc(a_used, 1)
                return mm

            def block_pe(c, i):
                first = gate_and_up(c, i, 0)
                if c == 0:
                    first_product(first, p)
                gate_and_up(c, i, 1)
                if c > 0:
                    start, end = down(c - 1, i)
                    start.then_inc(a_used, 1)
                    end.then_inc(b_used, 1)
                turn(c, i, 0)
                turn(c, i, 1).then_inc(hT_put, 1)

            blocks(pe, block_pe, 2, NBLK - 1)
            c = NBLK - 1
            gate_and_up(c, None, 0)
            down(c - 1, None, tiles=(0,))
            turn(c, None, 0).then_inc(hT_put, 1)
            gate_and_up(c, None, 1)
            start, _ = down(c, None, final=True, tiles=(0,))
            start.then_inc(a_used, 1)
            _, end = down(c - 1, None, tiles=(1,))
            end.then_inc(b_used, 1)
            turn(c, None, 1).then_inc(hT_put, 1)
            if p < last:
                norm_pe(pe, p + 1, 0)
            down(c, None, final=True, tiles=(1,))

        proj_bc, proj_x, z_bank, y_bank = banks[4:8]
        carve = Carve()
        chan = carve(4, TOK)
        zs = carve(2, TOK)
        x_tok = carve(NT * GC)
        decay = carve(GH, 4, P)
        dt_masked = carve(GH, 2, P)
        dt_behind = carve(GH, 2, P)
        y = carve(2, TOK)
        y_sq = carve(2, TOK)
        y_sq_sum = carve(2, TOK)
        table = carve(GROUPS, NQ, GH)
        scal = carve(NQ, GH)
        convp = carve(GROUPS, 4, TAPS + 1)
        chan_par = carve(2, GROUPS, 2)
        heads_in = carve(4, HEADS)
        dt_w = carve(KD * 2 * HEADS)
        assert carve.at - (192 + 32 + 128 + 512) >= FFN_WORK
        ynw, d_skip = chan_par[:, 0], chan_par[:, 1]
        dt_hi, dt_lo = (v[:, :, :].rearrange("p a b -> p (a b)") for v in (hT_hi, hT_lo))
        dtv = decay.rearrange("p a b c -> p (a b c)")
        rows = xn[:, :, :].rearrange("p t d -> p (t d)").rearrange("p (h d n) -> p h d n", h=GH, d=2)
        rows_flat = xn[:, :, :].rearrange("p t d -> p (t d)")
        v_dt, max_dt, e_dt, s_dt, s2_dt, poly_dt, dt, da = (dtv[:, n * P:(n + 1) * P] for n in range(8))
        dt_bias, a_log = (heads_in[:, n:n + 2, :].rearrange("p a h -> p (a h)") for n in (0, 2))
        exp_a = dtv[:, 8 * P:8 * P + 2 * HEADS]
        rows_sb = dt_behind.rearrange("p a b c -> p (a b c)")[0:HEADS, 0:2 * TOK]
        dt_bank, cum_bank, row_bank = acc[0], acc[1], acc[2]
        NF, SD, REM, DTF, DTB = 0, 2, 4, 6, 8
        diagonal, across = slice(0, 4, 3), slice(1, 3)

        def z_piece(c):
            return max(2 * c - 1, 0)

        def rows_piece(c):
            return min(2 * c + 2, 2 * GROUPS - 1)

        def of_group(v, c, i):
            if i is None:
                return v[:, c]
            one = v[:, bass.ds(i * 2 + c, 1)]
            names = "bcd"[:len(v.shape) - 2]
            return one.rearrange(f"p a {' '.join(names)} -> p (a {names[0]}) {' '.join(names[1:])}")

        def ssd_sync(sp, p):
            a0, b0, _, _ = bases(p)

            def load_cums(c, i):
                wait(sp, exps_made, at(GH * c, i, 2 * GH))
                src = rows_dram[c * GH:(c + 1) * GH, :] if i is None else \
                    rows_dram[bass.ds(i * (2 * GH) + c * GH, GH), :]
                sp.dma_start(rows_flat, src.rearrange("h n -> (h n)").unsqueeze(0)
                             .broadcast_to([P, GH * 2 * TOK])).then_inc(rows_in, 16)

            def load_z(c, i):
                load_b(sp, b0 + z_piece(c), i, 4)

            def body(c, i):
                load_slab(sp, a0 + c + 1, i)
                if c < 2:
                    load_z(c, i)
                if c == 0:
                    sp.wait_ge(rows_made, 1)
                    sp.dma_start(rows_dram[:, :], rows_sb).then_inc(rows_out, 16)
                    sp.wait_ge(rows_out, 16)
                    sp.wait_ge(xT_put, halves(p, 1, 1))
                load_cums(c, i)
                if c >= 2:
                    load_z(c, i)
                if c >= 1:
                    load_b(sp, b0 + 2 * c, i, 4)

            blocks(sp, body, 2, GROUPS)
            load_b(sp, b0 + rows_piece(GROUPS - 1), None, 4)

        def ssd_pool(pool, own, p):
            def by_head(first, step=1):
                two = scal[:, first:first + step + 1:step, :]
                return two.rearrange("p n h -> p h n").unsqueeze(3).broadcast_to([P, GH, 2, P])

            def masked(v):
                return v.unsqueeze(1).unsqueeze(1).broadcast_to([P, GH, 2, P])

            def add_squares(c, i):
                pool.wait_ge(y_squares, at(c + 1, i, 2))
                pool.tensor_tensor(y_sq_sum, y_sq_sum, y_sq, ALU.add).then_inc(squares_added, 1)

            def body(c, i):
                pool.wait_ge(scal_made, at(c + 1, i, 2))
                if c == 0:
                    pool.wait_ge(rows_out, 16)
                own.done(pool.tensor_tensor(dt_masked, masked(upto), by_head(DTF), ALU.mult))
                own.done(pool.tensor_tensor(dt_behind, masked(downto), by_head(DTB), ALU.mult))
                own.wait()
                own.done(pool.tensor_tensor(dt_masked, dt_masked, dt_behind, ALU.add))
                own.wait()
                for j in range(GH):
                    pool.wait_ge(exps_made, at(GH * c + j + 1, i, 2 * GH))
                    pool.tensor_tensor(decay[:, j, diagonal, :], decay[:, j, diagonal, :],
                                       dt_masked[:, j, :, :], ALU.mult)
                    pool.tensor_tensor(decay[:, j, across, :], decay[:, j, across, :],
                                       scal[:, DTF:DTB + 2:3, j:j + 1].broadcast_to([P, 2, P]),
                                       ALU.mult).then_inc(weights_made, 1)
                if c >= 1:
                    add_squares(c - 1, i)

            own.done(pool.memset(y_sq_sum, 0.0))
            own.wait()
            blocks(pool, body, 2, GROUPS, own, 2 * 3)
            add_squares(GROUPS - 1, None)
            pool.wait_ge(y_sum, 1)
            for t in range(NT):
                ins = pool.tensor_tensor(y_rms[:, t:t + 1], y_mean[:, t:t + 1], minus_half, ALU.pow)
            ins.then_inc(y_rms_made, 1)

        def ssd_act(act, p):
            a0, b0, q0, _ = bases(p)
            loads = b0 - (NBLK // 2) * sum(k == "ffn" for k in PHASES[:p])

            def split_hi(piece, i):
                split_b_hi(act, b0 + piece, i, 4, loads=loads + piece + 1, ml=4)

            def y_out(c, i):
                act.wait_ge(gated, at(c + 1, i, 2))
                for j in range(2):
                    ins = act.activation(hT_hi[:, j, :], y[:, j, :], ACT.Copy,
                                         scale=of_group(ynw, c, i)[:, j:j + 1])
                ins.then_inc(hT_hi_made, 1)
                wait(act, squares_added, at(c, i, 2))
                act.activation(y_sq, y, ACT.Square).then_inc(y_squares, 1)

            def exps(c, i):
                for j in range(GH):
                    act.wait_ge(args_made, at(GH * c + j + 1, i, 2 * GH))
                    for n in range(2):
                        act.activation(decay[:, j, 3 * n, :], decay[:, j, 3 * n, :], ACT.Exp,
                                       bias=scal[:, NF + n, j:j + 1])
                    act.activation(decay[:, j, 1, :], rows[:, j, 0, P:2 * P], ACT.Exp,
                                   bias=scal[:, REM, j:j + 1])
                    act.activation(decay[:, j, 2, :], rows[:, j, 1, 0:P], ACT.Exp,
                                   bias=scal[:, REM + 1, j:j + 1]).then_inc(exps_made, 1)

            def finish_x(c, i):
                act.wait_ge(z_put, at(c + 1, i, 2))
                wait(act, gated, at(c, i, 2))
                act.activation(zs, z_bank[:, :].rearrange("p (a n) -> p a n", a=2), ACT.Silu
                               ).then_inc(zs_made, 1)
                act.wait_ge(conv_made, at(2 * c + 2, i, 4))
                act.activation(chan[:, 2:4, :], chan[:, 2:4, :], ACT.Silu).then_inc(act_made, 1)
                act.wait_ge(xtok_put, at(c + 1, i, 2))
                wait(act, y_put, at(c, i, 2))
                act.activation(x_tok, proj_x[:, :], ACT.Copy).then_inc(xtok_made, 1)

            def finish_bc(c, i):
                act.wait_ge(conv_made, at(2 * c + 1, i, 4))
                act.activation(chan[:, 0:2, :], chan[:, 0:2, :], ACT.Silu).then_inc(act_made, 1)

            def body(c, i):
                for t in range(2):
                    split_slab_hi(act, a0 + c + 1, i, t)
                finish_x(c - 1, i)
                split_hi(z_piece(c), i)
                exps(c, i)
                y_out(c - 1, i)
                split_hi(2 * c, i)
                finish_bc(c, i)

            act.wait_ge(small_in, SMALL_IN)
            act.wait_ge(acc_put, 2 * p)
            act.activation(dt_hi, dt_w, ACT.Copy).then_inc(dt_hi_made, 1)
            norm_act_early(act, p, 1)
            norm_act(act, p, 1)
            split_hi(0, None)
            act.wait_ge(absdt_made, 1)
            act.activation(exp_a, a_log, ACT.Exp)
            act.activation(e_dt, v_dt, ACT.Exp, scale=-1.0).then_inc(exp_dt_made, 1)
            for t in range(2):
                split_slab_hi(act, a0 + 1, None, t)
            act.wait_ge(cums_put, 1)
            act.activation(rows_sb, row_bank[0:HEADS, :], ACT.Copy).then_inc(rows_made, 1)
            finish_bc(0, None)
            exps(0, None)
            blocks(act, body, 2, GROUPS, first=1)
            finish_x(GROUPS - 1, None)
            split_hi(rows_piece(GROUPS - 1), None)
            y_out(GROUPS - 1, None)
            norm_act_early(act, p + 1, 0)
            norm_act(act, p + 1, 0)

        def ssd_dve(dve, own, p):
            a0, b0, q0, _ = bases(p)

            def discretise():
                dve.wait_ge(dt_put, 1)
                for t in range(NT):
                    s = slice(t * 2 * HEADS, (t + 1) * 2 * HEADS)
                    own.done(dve.tensor_tensor(v_dt[:, s], dt_bank[:, s], dt_bias, ALU.add))
                own.wait()
                own.done(dve.tensor_scalar(max_dt, v_dt, 0.0, None, ALU.max))
                own.wait()
                dve.scalar_tensor_tensor(v_dt, v_dt, -1.0, v_dt, ALU.mult, ALU.max).then_inc(absdt_made, 1)
                dve.wait_ge(exp_dt_made, 1)
                own.done(dve.tensor_scalar(s2_dt, e_dt, 2.0, None, ALU.add))
                own.wait()
                own.done(dve.reciprocal(poly_dt, s2_dt))
                own.wait()
                own.done(dve.tensor_tensor(s_dt, e_dt, poly_dt, ALU.mult))
                own.wait()
                own.done(dve.tensor_tensor(s2_dt, s_dt, s_dt, ALU.mult))
                own.wait()
                own.done(dve.tensor_scalar(poly_dt, s2_dt, 1.0 / 15, None, ALU.mult))
                for n in range(6, 0, -1):
                    own.wait()
                    own.done(dve.scalar_tensor_tensor(poly_dt, poly_dt, 1.0 / (2 * n + 1), s2_dt,
                                                      ALU.add, ALU.mult))
                own.wait()
                own.done(dve.scalar_tensor_tensor(poly_dt, poly_dt, 1.0, s_dt, ALU.add, ALU.mult))
                own.wait()
                own.done(dve.scalar_tensor_tensor(dt, poly_dt, 2.0, max_dt, ALU.mult, ALU.add))
                own.wait()
                for t in range(NT):
                    s = slice(t * 2 * HEADS, (t + 1) * 2 * HEADS)
                    ins = dve.scalar_tensor_tensor(da[:, s], dt[:, s], -1.0, exp_a, ALU.mult, ALU.mult)
                ins.then_inc(da_made, 1)

            def fill_table():
                def col(n):
                    return table[:, :, n, :]

                def heads(v):
                    return v.rearrange("p (g h) -> p g h", g=GROUPS)

                def cum(n):
                    return heads(cum_bank[:, n * HEADS:(n + 1) * HEADS])

                for n in range(2):
                    for d in range(2):
                        s = (2 * n + d) * HEADS
                        own.done(dve.tensor_copy(col(DTF + 2 * d + n), heads(dt[:, s:s + HEADS])))
                dve.wait_ge(cums_put, 1)
                for n in range(2):
                    own.done(dve.tensor_scalar(col(NF + n), cum(n), -1.0, None, ALU.mult))
                    own.done(dve.tensor_copy(col(REM + n), cum(4 + n)))
                own.wait()
                for n in range(2):
                    own.done(dve.scalar_tensor_tensor(col(SD + n), col(NF + n), -1.0, cum(2 + n),
                                                      ALU.mult, ALU.subtract))
                own.wait()

            def take_scalars(c, i):
                wait(dve, weights_made, at(GH * c, i, 2 * GH))
                src = table[:, c] if i is None else \
                    table[:, bass.ds(i * 2 + c, 1), :, :].rearrange("p a q h -> p (a q) h")
                dve.tensor_copy(scal, src).then_inc(scal_made, 1)

            def decay_args(c, i):
                dve.wait_ge(scal_made, at(c + 1, i, 2))
                dve.wait_ge(rows_in, at(16 * (c + 1), i, 32))
                wait(dve, y_put, at(c, i, 2))
                for j in range(GH):
                    for n in range(2):
                        s = slice(n * P, (n + 1) * P)
                        ins = dve.scalar_tensor_tensor(decay[:, j, 3 * n, :], rows[:, j, 1, s],
                                                       scal[:, SD + n, j:j + 1], rows[:, j, 0, s],
                                                       ALU.add, ALU.min)
                    ins.then_inc(args_made, 1)

            def weigh(c, i):
                dve.wait_ge(weights_made, at(GH * (c + 1), i, 2 * GH))
                dve.wait_ge(cb_put, at(c + 1, i, 2))
                w = decay.rearrange("p h a n -> p h (a n)")
                dve.tensor_tensor(w, w, proj_bc[:, :].unsqueeze(1).broadcast_to([P, GH, 2 * TOK]),
                                  ALU.mult).then_inc(m_made, 1)

            def convolve(c, i, o):
                bank = proj_x if o else proj_bc
                dve.wait_ge(proj_put, at(2 * c + o // 2 + 1, i, 4))
                par = of_group(convp, c, i).rearrange("p o n -> p (o n)")
                mid = TAPS // 2
                for n in [mid] + [n for n in range(TAPS) if n != mid]:
                    off = n - mid
                    to = slice(max(0, -off), TOK - max(0, off))
                    frm = slice(max(0, off), TOK - max(0, -off))
                    for r in range(2):
                        u = bank[:, r * TOK:(r + 1) * TOK]
                        out = chan[:, o + r, :]
                        at0 = (o + r) * (TAPS + 1)
                        tap = par[:, at0 + n:at0 + n + 1]
                        if n == mid:
                            ins = dve.tensor_scalar(out, u, tap, par[:, at0 + TAPS:at0 + TAPS + 1],
                                                    ALU.mult, ALU.add)
                        else:
                            dve.wait_ge(own.sem, own.count(-1))
                            ins = dve.scalar_tensor_tensor(out[:, to], u[:, frm], tap, out[:, to],
                                                           ALU.mult, ALU.add)
                        if n == TAPS - 1 and r == 1:
                            ins.then_inc(conv_made, 1)
                        else:
                            own.done(ins)

            def gate(c, i):
                dve.wait_ge(y_put, at(c + 1, i, 2))
                dve.wait_ge(zs_made, at(c + 1, i, 2))
                wait(dve, y_squares, at(c, i, 2))
                for j in range(2):
                    own.done(dve.scalar_tensor_tensor(y[:, j, :], chan[:, 2 + j, :],
                                                      of_group(d_skip, c, i)[:, j:j + 1],
                                                      y_bank[:, j * TOK:(j + 1) * TOK],
                                                      ALU.mult, ALU.add))
                own.wait()
                dve.tensor_tensor(y, y, zs, ALU.mult).then_inc(gated, 1)

            def y_lo(c, i):
                dve.wait_ge(hT_hi_made, at(q0 + c + 1, i, 2))
                for j in range(2):
                    ins = dve.scalar_tensor_tensor(hT_lo[:, j, :], y[:, j, :],
                                                   of_group(ynw, c, i)[:, j:j + 1],
                                                   hT_hi[:, j, :].bitcast(F32), ALU.mult, ALU.subtract)
                ins.then_inc(hT_lo_made, 1)

            def body(c, i):
                take_scalars(c, i)
                for t in range(2):
                    split_slab_lo(dve, a0 + c + 1, i, t)
                split_b_lo(dve, b0 + z_piece(c), i, 4)
                decay_args(c, i)
                gate(c - 1, i)
                convolve(c, i, 0)
                y_lo(c - 1, i)
                split_b_lo(dve, b0 + 2 * c, i, 4)
                weigh(c, i)
                convolve(c, i, 2)

            norm_dve(dve, p, 1)
            dve.wait_ge(dt_hi_made, 1)
            dve.tensor_tensor(dt_lo, dt_w, dt_hi.bitcast(F32), ALU.subtract).then_inc(dt_lo_made, 1)
            norm_lo_dve(dve, p, 1)
            split_b_lo(dve, b0, None, 4)
            discretise()
            for t in range(2):
                split_slab_lo(dve, a0 + 1, None, t)
            fill_table()
            convolve(0, None, 0)
            take_scalars(0, None)
            decay_args(0, None)
            convolve(0, None, 2)
            weigh(0, None)
            blocks(dve, body, 2, GROUPS, own, 2 * (2 * 9 + 2), first=1)
            split_b_lo(dve, b0 + rows_piece(GROUPS - 1), None, 4)
            gate(GROUPS - 1, None)
            y_lo(GROUPS - 1, None)
            dve.wait_ge(y_sum_put, 1)
            dve.tensor_scalar(y_mean, z_bank[:, 0:NT], 1.0 / INNER, EPS, ALU.mult, ALU.add
                              ).then_inc(y_sum, 1)
            dve.wait_ge(y_rms_made, 1)
            end_dve(dve, p, lambda t: y_rms[:, t:t + 1])

        def ssd_pe(pe, p):
            a0, b0, q0, _ = bases(p)

            def z_proj(c, i):
                pe.wait_ge(b_lo_made, at(b0 + z_piece(c) + 1, i, 4))
                wait(pe, zs_made, at(c, i, 2))
                for m in range(2):
                    for k in range(KD):
                        s = slice(k * GC + m * P, k * GC + (m + 1) * P)
                        _, mm = three_passes(pe, z_bank[:, m * TOK:(m + 1) * TOK],
                                             (b_hi[:, s], b_lo[:, s]), (xT_hi[:, k, :], xT_lo[:, k, :]),
                                             k == 0, k == KD - 1)
                mm.then_inc(z_put, 1)

            def chan_proj(c, i, o, n=slice(0, TOK)):
                bank = (proj_bc, proj_bc, proj_x, proj_x)[o]
                s = ((o + 2) % 4) * P
                start = None
                for k in range(KD):
                    if o == 0:
                        wait_slab(pe, a0 + c, i, k)
                    a, mm = three_passes(pe, bank[:, (o % 2) * TOK + n.start:(o % 2) * TOK + n.stop],
                                         slab(a0 + c, k, s, P), (xT_hi[:, k, n], xT_lo[:, k, n]),
                                         k == 0, k == KD - 1)
                    start = start or a
                return start, mm

            def out_rows(c, i, piece, m, final=False):
                pe.wait_ge(b_lo_made, at(b0 + piece + 1, i, m))
                return project_rows(pe, q0 + c, i, 2, b_rows(0), c == 0, final)

            def y_heads(c, i):
                pe.wait_ge(m_made, at(c + 1, i, 2))
                pe.wait_ge(xtok_made, at(c + 1, i, 2))
                wait(pe, gated, at(c, i, 2))
                for j in range(GH):
                    out = y_bank[(j % 2) * HD:(j % 2 + 1) * HD, (j // 2) * TOK:(j // 2 + 1) * TOK]
                    for s in range(NT):
                        mm = pe.matmul(out, lhsT=x_tok[:, s * GC + j * HD:s * GC + (j + 1) * HD],
                                       rhs=decay[:, j, 2 * s:2 * s + 2, :].rearrange("p a n -> p (a n)"),
                                       start=s == 0, stop=s == NT - 1)
                mm.then_inc(y_put, 1)

            def c_dot_b(c, i):
                pe.wait_ge(act_made, at(2 * c + 1, i, 4))
                start = None
                for s in range(NT):
                    mm = pe.matmul(proj_bc[:, s * TOK:(s + 1) * TOK], lhsT=chan[:, 0, s * P:(s + 1) * P],
                                   rhs=chan[:, 1, :], start=True, stop=True)
                    start = start or mm
                mm.then_inc(cb_put, 1)
                return start

            def x_turn(c, i):
                pe.wait_ge(act_made, at(2 * c + 2, i, 4))
                for t in range(NT):
                    for j in range(2):
                        mm = pe.transpose(proj_x[:, t * GC + j * P:t * GC + (j + 1) * P],
                                          chan[:, 2 + j, t * P:(t + 1) * P], ident)
                mm.then_inc(xtok_put, 1)

            def project_x(c, i):
                wait(pe, xtok_made, at(c, i, 2))
                chan_proj(c, i, 2)[0].then_inc(b_used, 1)
                if c > 0:
                    c_dot_b(c, i)
                chan_proj(c, i, 3)[1].then_inc(proj_put, 1)

            def body(c, i):
                pe.wait_ge(m_made, at(c, i, 2))
                chan_proj(c, i, 0)
                y_heads(c - 1, i)
                chan_proj(c, i, 1)[1].then_inc(proj_put, 1)
                z_proj(c, i)
                project_x(c, i)
                start, end = out_rows(c - 1, i, 2 * c, 4)
                start.then_inc(a_used, 1)
                end.then_inc(b_used, 1)
                x_turn(c, i)

            def dt_proj(t):
                pe.wait_ge(dt_lo_made, 1)
                pe.wait_ge(xT_lo_made, halves(p, t, 1))
                for k in range(KD):
                    s = slice(k * 2 * HEADS, (k + 1) * 2 * HEADS)
                    _, mm = three_passes(pe, dt_bank[:, t * 2 * HEADS:(t + 1) * 2 * HEADS], xT(k, t),
                                         (dt_hi[:, s], dt_lo[:, s]), k == 0, k == KD - 1)
                if t == NT - 1:
                    mm.then_inc(dt_put, 1)

            def cumulate():
                pe.wait_ge(da_made, 1)
                fwd = [da[:, n * 2 * HEADS:n * 2 * HEADS + HEADS] for n in range(2)]
                bwd = [da[:, n * 2 * HEADS + HEADS:(n + 1) * 2 * HEADS] for n in range(2)]
                for n, (tri, v) in enumerate([(upto, fwd[0]), (upto, fwd[1]), (downto, bwd[0]),
                                              (downto, bwd[1]), (below, fwd[0]), (above, bwd[1])]):
                    pe.matmul(cum_bank[:, n * HEADS:(n + 1) * HEADS], lhsT=tri, rhs=v,
                              start=True, stop=True)
                for n, (tri, v) in enumerate([(upto, fwd[0]), (upto, fwd[1]),
                                              (downto, bwd[0]), (downto, bwd[1])]):
                    mm = pe.matmul(row_bank[0:HEADS, n * P:(n + 1) * P], lhsT=v, rhs=tri,
                                   start=True, stop=True)
                mm.then_inc(cums_put, 1)

            for half in range(2):
                pe.wait_ge(xT_lo_made, halves(p, 0, half))
            first_product(chan_proj(0, None, 0, slice(0, P))[0], p)
            chan_proj(0, None, 1, slice(0, P))
            dt_proj(0)
            norm_pe(pe, p, 1)
            dt_proj(1)
            chan_proj(0, None, 0, slice(P, TOK))
            chan_proj(0, None, 1, slice(P, TOK))[1].then_inc(proj_put, 1)
            z_proj(0, None)
            project_x(0, None)
            cumulate()
            c_dot_b(0, None).then_inc(a_used, 1)
            x_turn(0, None)
            blocks(pe, body, 2, GROUPS, first=1)
            y_heads(GROUPS - 1, None)
            pe.wait_ge(squares_added, GROUPS)
            pe.wait_ge(zs_made, GROUPS)
            for t in range(NT):
                for j in range(2):
                    mm = pe.matmul(z_bank[:, t:t + 1], lhsT=y_sq_sum[:, j, t * P:(t + 1) * P],
                                   rhs=upto[:, P - 1:P], start=j == 0, stop=j == 1)
            mm.then_inc(y_sum_put, 1)
            out_rows(GROUPS - 1, None, rows_piece(GROUPS - 1), 4, final=True)
            norm_pe(pe, p + 1, 0)

        STEPS = AH // 2
        carve = Carve()
        q_in = carve(2, NT, 512)
        qT = q_in.rearrange("p a b c -> p a (b c)").rearrange("p a (s n) -> p (a s) n", s=4)
        kv = carve(NT, 512)
        k_twice = carve(NT, KVH, 2, AD)
        prT = k_twice.rearrange("p a b c d -> p (a b c d)").rearrange("p (c s n) -> p c s n", c=4, s=2)
        kT = carve(KVH, TOK)
        k_rot = kT.rearrange("p a b -> p (a b)")[:, 0:NT * 256].rearrange("p (t n) -> p t n", t=NT)
        probs = carve(2, 4, TOK)
        scratch = probs.rearrange("p a b c -> p (a b c)")
        squared = scratch[:, 0:NT * 512].rearrange("p (t n) -> p t n", t=NT)
        swapped = scratch[:, NT * 512:2 * NT * 512].rearrange("p (t n) -> p t n", t=NT)
        q_rot = xn[:, :, :].rearrange("p t d -> p (t d)").rearrange("p (a t n) -> p a t n", a=2, t=NT)
        o = xn
        mask = carve(NT, TOK)
        rope = carve(NT, 2, AD)
        norm_rows = carve(4 * AD + AH)
        rope_w = carve(2, NT, 2, AD)
        head_ss = carve(NT, AH + KVH)
        head_mean = carve(NT, AH + KVH)
        head_rms = carve(NT, AH + KVH)
        half_down = carve(NT, AH)
        minus_sink = carve(AH, NT)
        stats = carve(2, 8, 4)
        PARTS = [(AH, KVH, kv, 0), (0, 8, q_in[:, 0, :, :], 1), (8, 8, q_in[:, 1, :, :], 2)]

        def attn_sync(sp, p):
            a0 = bases(p)[0]
            for c in range(1, 5 + (p < last)):
                load_slab(sp, a0 + c, None)

        def heads64(v, n):
            return v.rearrange("p (h d) -> p h d", h=n)

        def attn_load(pool, p):
            pool.wait_ge(xn_made, 4 * p)
            pool.dma_start(mask, mask_dram).then_inc(attn_in, 16)
            pool.dma_start(rope, rope_dram).then_inc(attn_in, 16)
            pool.dma_start(norm_rows, attn_dram.unsqueeze(0).broadcast_to([P, 4 * AD + AH])
                           ).then_inc(attn_in, 16)

        def attn_pool(pool, own, p):
            pool.wait_ge(attn_in, 48)
            for n in range(2):
                for r in range(2):
                    w = norm_rows[:, (2 * n + r) * AD:(2 * n + r + 1) * AD]
                    own.done(pool.tensor_tensor(rope_w[:, n, :, r, :], rope[:, :, r, :],
                                                w.unsqueeze(1).broadcast_to([P, NT, AD]), ALU.mult))
            own.done(pool.memset(half_down, -0.5))
            own.done(pool.tensor_scalar(minus_sink,
                                        norm_rows[:, 4 * AD:].unsqueeze(2).broadcast_to([P, AH, NT]),
                                        -1.0, None, ALU.mult))
            own.wait()
            pool.memset(stats[:, 0, 7, 0:1], 0.0).then_inc(tables_made, 1)
            for h0, nh, src, u in PARTS:
                n = 1 if u == 0 else 0
                for t in range(NT):
                    pool.wait_ge(qkv_made, 2 * u + t + 1)
                    wait(pool, rot_made, 2 * (u - 1) + t + 1)
                    v = heads64(src[:, t, 0:nh * AD], nh)
                    to = heads64(swapped[:, t, 0:nh * AD], nh)
                    half = AD // 2
                    sin = rope_w[:, n, t, 1, :].unsqueeze(1).broadcast_to([P, nh, AD])
                    pool.tensor_tensor(to[:, :, 0:half], v[:, :, half:], sin[:, :, 0:half], ALU.mult)
                    pool.tensor_tensor(to[:, :, half:], v[:, :, 0:half], sin[:, :, half:],
                                       ALU.mult).then_inc(swap_made, 1)
                pool.wait_ge(ss_made, 2 * u + 2)
                s = slice(h0, h0 + nh)
                scale = (1.0 / AD, EPS) if u == 0 else (1.0, AD * EPS)
                own.done(pool.tensor_scalar(head_mean[:, :, s], head_ss[:, :, s], *scale,
                                            ALU.mult, ALU.add))
                own.wait()
                pool.tensor_tensor(head_rms[:, :, s], head_mean[:, :, s], half_down[:, :, 0:nh],
                                   ALU.pow).then_inc(head_rms_made, 1)

        def proj_bank(u, t):
            return banks[2 * u + t]

        def turn_bank(u, s):
            return banks[(6, 0, 2)[u] + s]

        def attn_act(act, p):
            a0, _, q0, _ = bases(p)
            norm_act_early(act, p, 1)
            norm_act(act, p, 1)
            for c in (1,):
                for t in range(2):
                    split_slab_hi(act, a0 + c, None, t)

            def take_in(u):
                h0, nh, dst, _ = PARTS[u]
                for t in range(NT):
                    act.wait_ge(qkv_put, 2 * u + t + 1)
                    act.activation(dst[:, t, :], proj_bank(u, t)[:, :], ACT.Copy).then_inc(qkv_made, 1)
                    wait(act, ss_made, 2 * (u - 1) + t + 1)
                    act.activation(squared[:, t, 0:nh * AD], proj_bank(u, t)[:, 0:nh * AD],
                                   ACT.Square).then_inc(sq_made, 1)

            def turned_in(u, dst):
                act.wait_ge(turn_put, u + 1)
                for s in range(2):
                    ins = act.activation(dst[:, 2 * s:2 * s + 2, :],
                                         turn_bank(u, s)[:, :].rearrange("p (a n) -> p a n", a=2), ACT.Copy)
                ins.then_inc(turn_made, 1)

            def exps(n):
                act.wait_ge(shift_made, n + 1)
                st = stats[:, n % 2]
                for c in range(4):
                    act.activation(probs[:, n % 2, c, :], probs[:, n % 2, c, :], ACT.Exp,
                                   bias=st[:, NEG, c:c + 1], accum_out=st[:, DEN, c:c + 1])
                act.activation(st[:, SINK, :], st[:, SINK_ARG, :], ACT.Exp).then_inc(probs_made, 1)

            take_in(0)
            for t in range(2):
                split_slab_hi(act, a0 + 2, None, t)
            take_in(1)
            turned_in(0, kT)
            for t in range(2):
                split_slab_hi(act, a0 + 3, None, t)
            take_in(2)
            turned_in(1, qT[:, 0:4, :])
            turned_in(2, qT[:, 4:8, :])
            exps(0)
            for n in range(STEPS):
                if n + 1 < STEPS:
                    exps(n + 1)
                if n == 0:
                    for t in range(2):
                        split_slab_hi(act, a0 + 4, None, t)
                act.wait_ge(probsT_put, n + 1)
                act.activation(prT[:, 0:2, :, :], banks[2][:, :].rearrange("p (c s n) -> p c s n", c=2, s=2),
                               ACT.Copy).then_inc(probsT_hi, 1)
                if n % 2 == 0 and n >= 2:
                    rows_in_hi(act, turns_before(p), n // 2 - 1)
            rows_in_hi(act, turns_before(p), KVH - 1)
            if p < last:
                for t in range(2):
                    split_slab_hi(act, a0 + 5, None, t)
                norm_act_early(act, p + 1, 0)
                norm_act(act, p + 1, 0)

        def rows_in_hi(act, turns, j):
            act.wait_ge(hT_put, turns + j + 1)
            act.activation(xT_hi[:, 2 * j:2 * j + 2, :], banks[1][:, :].rearrange("p (a n) -> p a n", a=2),
                           ACT.Copy).then_inc(hT_hi_made, 1)

        MAX, NEG, DEN, SINK_ARG, SINK, SUM, INV = range(7)

        def attn_dve(dve, own, p):
            a0, _, q0, _ = bases(p)

            def take_squares(u):
                h0, nh, _, _ = PARTS[u]
                for t in range(NT):
                    dve.wait_ge(sq_made, 2 * u + t + 1)
                    dve.tensor_reduce(head_ss[:, t, h0:h0 + nh], heads64(squared[:, t, 0:nh * AD], nh),
                                      AX_X, ALU.add).then_inc(ss_made, 1)

            def rotate(u):
                h0, nh, src, _ = PARTS[u]
                n = 1 if u == 0 else 0
                for t in range(NT):
                    to = k_rot[:, t, :] if u == 0 else q_rot[:, u - 1, t, :]
                    dve.wait_ge(qkv_made, 2 * u + t + 1)
                    own.done(dve.tensor_tensor(heads64(to, nh), heads64(src[:, t, 0:nh * AD], nh),
                                               rope_w[:, n, t, 0, :].unsqueeze(1).broadcast_to([P, nh, AD]),
                                               ALU.mult))
                    own.wait()
                    dve.wait_ge(swap_made, 2 * u + t + 1)
                    dve.tensor_tensor(to, to, swapped[:, t, 0:nh * AD], ALU.add).then_inc(rot_made, 1)

            def softmax_args(n):
                st = stats[:, n % 2]
                dve.wait_ge(s_put, n + 1)
                wait(dve, probsT_put, n - 1)
                for c in range(4):
                    e, t = divmod(c, 2)
                    h = 2 * n + e
                    ins = dve.scalar_tensor_tensor(probs[:, n % 2, c, :],
                                                   banks[4 + 2 * (n % 2) + e][:, t * TOK:(t + 1) * TOK],
                                                   head_rms[:, t, h:h + 1], mask[:, t, :],
                                                   ALU.mult, ALU.add)
                own.done(ins)
                own.wait()
                own.done(dve.tensor_reduce(st[:, MAX, :], probs[:, n % 2, :, :], AX_X, ALU.max))
                own.wait()
                sink = minus_sink[:, 2 * n:2 * n + 2, :].rearrange("p a b -> p (a b)")
                own.done(dve.scalar_tensor_tensor(st[:, NEG, :], st[:, MAX, :], -1.0, sink,
                                                  ALU.mult, ALU.min))
                own.wait()
                dve.tensor_tensor(st[:, SINK_ARG, :], st[:, NEG, :], sink, ALU.subtract
                                  ).then_inc(shift_made, 1)

            def rows_in_lo(j):
                dve.wait_ge(hT_hi_made, q0 + j + 1)
                dve.tensor_tensor(xT_lo[:, 2 * j:2 * j + 2, :],
                                  banks[1][:, :].rearrange("p (a n) -> p a n", a=2),
                                  xT_hi[:, 2 * j:2 * j + 2, :].bitcast(F32), ALU.subtract
                                  ).then_inc(hT_lo_made, 1)

            norm_dve(dve, p, 1)
            norm_lo_dve(dve, p, 1)
            for t in range(2):
                split_slab_lo(dve, a0 + 1, None, t)
            dve.wait_ge(tables_made, 1)
            take_squares(0)
            rotate(0)
            dve.wait_ge(head_rms_made, 1)
            dve.wait_ge(rot_made, 2)
            for t in range(NT):
                for r in range(2):
                    ins = dve.tensor_tensor(k_twice[:, t, :, r, :], heads64(k_rot[:, t, :], KVH),
                                            head_rms[:, t, AH:].unsqueeze(2).broadcast_to([P, KVH, AD]),
                                            ALU.mult)
            ins.then_inc(k_made, 1)
            for t in range(2):
                split_slab_lo(dve, a0 + 2, None, t)
            take_squares(1)
            rotate(1)
            for t in range(2):
                split_slab_lo(dve, a0 + 3, None, t)
            take_squares(2)
            rotate(2)
            dve.wait_ge(head_rms_made, 3)
            softmax_args(0)
            for n in range(STEPS):
                if n + 1 < STEPS:
                    softmax_args(n + 1)
                if n == 0:
                    for t in range(2):
                        split_slab_lo(dve, a0 + 4, None, t)
                st = stats[:, n % 2]
                dve.wait_ge(probsT_put, n + 1)
                dve.tensor_copy(prT[:, 2:4, :, :], banks[3][:, :].rearrange("p (c s n) -> p c s n", c=2, s=2)
                                ).then_inc(probsT_lo, 1)
                own.done(dve.tensor_tensor(st[:, SUM, :], st[:, DEN, :], st[:, SINK, :], ALU.add))
                own.wait()
                own.done(dve.reciprocal(st[:, INV, :], st[:, SUM, :]))
                own.wait()
                if n % 2 == 0 and n >= 2:
                    rows_in_lo(n // 2 - 1)
                dve.wait_ge(o_put, n + 1)
                dve.tensor_tensor(o[:, :, 2 * n * AD:(2 * n + 2) * AD].rearrange("p t (e d) -> p e t d", e=2),
                                  banks[n % 2][:, 0:4 * AD].rearrange("p (e t d) -> p e t d", e=2, t=2),
                                  st[:, INV, :].rearrange("p (e t) -> p e t", e=2).unsqueeze(3)
                                  .broadcast_to([P, 2, NT, AD]), ALU.mult).then_inc(o_made, 1)
            rows_in_lo(KVH - 1)
            if p < last:
                for t in range(2):
                    split_slab_lo(dve, a0 + 5, None, t)
            end_dve(dve, p, lambda t: 1.0)

        def attn_pe(pe, p):
            a0, _, q0, _ = bases(p)

            def project(u):
                for t in range(NT):
                    for k in range(KD):
                        if u == 0 and k % 4 == 0:
                            pe.wait_ge(xT_lo_made, halves(p, t, k // 4))
                        if t == 0:
                            wait_slab(pe, a0 + u, None, k)
                        first, mm = three_passes(pe, proj_bank(u, t)[:, :], xT(k, t), slab(a0 + u, k),
                                                 k == 0, k == KD - 1)
                        if u > 0 and t == k == 0:
                            first.then_inc(a_used, 1)
                        elif t == k == 0:
                            first_product(first, p)
                        if u == t == 0 and k == 3:
                            norm_pe(pe, p, 1)
                    mm.then_inc(qkv_put, 1)

            def turn(u):
                if u == 0:
                    pe.wait_ge(k_made, 1)
                else:
                    pe.wait_ge(rot_made, 2 * u + 2)
                    pe.wait_ge(sq_made, 2 * u)
                for s in range(4):
                    for t in range(NT):
                        src = k_twice[:, t, s, :, :].rearrange("p a b -> p (a b)") if u == 0 else \
                            q_rot[:, u - 1, t, s * P:(s + 1) * P]
                        mm = pe.transpose(turn_bank(u, s // 2)[:, (s % 2) * TOK + t * P:(s % 2) * TOK + (t + 1) * P],
                                          src, ident)
                        if u == 1 and s == t == 0:
                            mm.then_inc(a_used, 1)
                mm.then_inc(turn_put, 1)

            def scores(n):
                if n < 2:
                    pe.wait_ge(turn_made, 3)
                    pe.wait_ge(sq_made, 6)
                else:
                    pe.wait_ge(shift_made, n - 1)
                for e in range(2):
                    for t in range(NT):
                        mm = pe.matmul(banks[4 + 2 * (n % 2) + e][:, t * TOK:(t + 1) * TOK],
                                       lhsT=qT[e * AD:(e + 1) * AD, n, t * P:(t + 1) * P],
                                       rhs=kT[e * AD:(e + 1) * AD, n // 2, :], start=True, stop=True)
                mm.then_inc(s_put, 1)

            def turn_probs(n):
                pe.wait_ge(probs_made, n + 1)
                wait(pe, probsT_hi, n)
                wait(pe, probsT_lo, n)
                for c in range(4):
                    for s in range(NT):
                        mm = pe.transpose(banks[2 + c // 2][:, ((c % 2) * 2 + s) * P:((c % 2) * 2 + s + 1) * P],
                                          probs[:, n % 2, c, s * P:(s + 1) * P], ident)
                mm.then_inc(probsT_put, 1)

            def values(n):
                pe.wait_ge(probsT_hi, n + 1)
                pe.wait_ge(probsT_lo, n + 1)
                wait(pe, o_made, n - 1)
                if n % 2 and n > 2:
                    pe.wait_ge(hT_lo_made, q0 + n // 2)
                for c in range(4):
                    for s in range(NT):
                        mm = pe.matmul(banks[n % 2][:, c * AD:(c + 1) * AD], lhsT=prT[:, c, s, :],
                                       rhs=kv[:, s, 256 + (n // 2) * AD:256 + (n // 2 + 1) * AD],
                                       start=s == 0, stop=s == NT - 1)
                mm.then_inc(o_put, 1)

            def turn_out(j):
                pe.wait_ge(o_made, 2 * j + 2)
                for t in range(NT):
                    for r in range(2):
                        mm = pe.transpose(banks[1][:, r * TOK + t * P:r * TOK + (t + 1) * P],
                                          o[:, t, (2 * j + r) * P:(2 * j + r + 1) * P], ident)
                mm.then_inc(hT_put, 1)

            project(0)
            project(1)
            turn(0)
            project(2)
            turn(1)
            turn(2)
            scores(0)
            scores(1)
            for n in range(STEPS):
                turn_probs(n)
                if n + 2 < STEPS:
                    scores(n + 2)
                if n % 2 == 0 and n >= 2:
                    turn_out(n // 2 - 1)
                values(n)
            turn_out(KVH - 1)
            pe.wait_ge(hT_lo_made, q0 + KVH)
            for j, tiles in ((0, (0, 1)), (1, (0, 1)), (2, (0,)), (3, (0,)), (2, (1,)), (3, (1,))):
                c, half = a0 + 3 + j // 2, j % 2
                wait_slab(pe, c, None, 4 * half)

                def rows(s, c=c, half=half):
                    s += half * PIECE
                    return a_hi[:, c % 2, s:s + 512], a_lo[:, c % 2, s:s + 512]

                def oT(r, t, j=j):
                    return xT(2 * j + r, t)

                start, _ = project_rows(pe, q0 + j, None, 1, rows, j == 0, j == KVH - 1, oT, tiles)
                if j == 2 and tiles == (0,):
                    start.then_inc(a_used, 1)
            norm_pe(pe, p + 1, 0)

        ffn = dict(sync=ffn_sync, scalar=ffn_act, vector=ffn_dve, tensor=ffn_pe)
        ssd = dict(sync=ssd_sync, scalar=ssd_act, vector=ssd_dve, tensor=ssd_pe)
        attn = dict(sync=attn_sync, scalar=attn_act, vector=attn_dve, tensor=attn_pe)
        kinds = dict(ffn=ffn, ssd=ssd, attn=attn)

        @block.sync
        def _(sp):
            sp.dma_start(ident, ident_dram).then_inc(ident_in, 16)
            sp.dma_start(x[:, 0, :], x_dram[0, 0:P, :]).then_inc(x_in[0], 16)
            load_slab(sp, 0, None, (0,))
            sp.dma_start(x[:, 1, :], x_dram[0, P:2 * P, :]).then_inc(x_in[1], 16)
            load_slab(sp, 0, None, (1,))
            for p, kind in enumerate(PHASES):
                kinds[kind]["sync"](sp, p)
            for t in range(NT):
                sp.wait_ge(x_made, 2 * last + t + 1)
                sp.dma_start(out_dram[0, t * P:(t + 1) * P, :], x[:, t, :]).then_inc(stored, 16)
            sp.wait_ge(stored, 16 * NT)

        @block.gpsimd
        def _(pool):
            own = Own(pool, pool_own)

            def load_norm(p):
                pool.dma_start(norm_w[:, p % 2, :], norm_dram[p:p + 1, :].broadcast_to([P, D])
                               ).then_inc(norm_in[p % 2], 16)

            own.done(pool.memset(minus_half, -0.5))
            own.wait()
            pool.wait_ge(xn_made, 1)
            for dst, src in ((consts[:, :, :], consts_dram), (convp, convp_dram),
                             (chan_par, chan_dram), (dt_w, dtw_dram),
                             (heads_in, heads_dram.unsqueeze(0).broadcast_to([P, 4, HEADS]))):
                pool.dma_start(dst, src).then_inc(small_in, 16)
            load_norm(1)
            for p, kind in enumerate(PHASES):
                if kind == "attn":
                    attn_load(pool, p)
                norm_pool(pool, own, p)
                if p + 2 < len(PHASES):
                    pool.wait_ge(xn_made, 4 * p + 4)
                    load_norm(p + 2)
                if kind == "ssd":
                    ssd_pool(pool, own, p)
                elif kind == "attn":
                    attn_pool(pool, own, p)

        @block.scalar
        def _(act):
            act.dma_start(norm_w[:, 0, :], norm_dram[0:1, :].broadcast_to([P, D])).then_inc(first_norm_in, 16)
            norm_act(act, 0, 0)
            for t in range(2):
                split_slab_hi(act, 0, None, t)
            for p, kind in enumerate(PHASES):
                kinds[kind]["scalar"](act, p)

        @block.vector
        def _(dve):
            own = Own(dve, dve_own)
            norm_dve(dve, 0, 0)
            norm_lo_dve(dve, 0, 0)
            for t in range(2):
                split_slab_lo(dve, 0, None, t)
            for p, kind in enumerate(PHASES):
                kinds[kind]["vector"](dve, own, p)

        @block.tensor
        def _(pe):
            pe.wait_ge(ident_in, 16)
            norm_pe(pe, 0, 0)
            for p, kind in enumerate(PHASES):
                kinds[kind]["tensor"](pe, p)


SMALL_IN = 16 * 5


def lay_out(inputs):
    w_gate, w_up, w_down = (np.asarray(inputs[n]) for n in ("ffn_w_gate", "ffn_w_up", "ffn_w_down"))
    w_in, w_out = np.asarray(inputs["ssd_w_in"])[0], np.asarray(inputs["ssd_w_out"])[0]
    w_qkv, w_o = np.asarray(inputs["attn_w_qkv"])[0], np.asarray(inputs["attn_w_out"])[0]

    def columns(w, *spans):
        w = w.reshape(KD, P, -1)
        return np.concatenate([w[:, :, a:b] for a, b in spans], axis=2).transpose(1, 0, 2)

    def down_rows(w, r):
        return w[r:r + 2 * P].reshape(2, P, D).transpose(1, 0, 2)

    def slabs(m):
        return list(m.reshape(P, 2, PIECE).transpose(1, 0, 2))

    a, b = [], []
    n_ffn = 0
    for kind in PHASES:
        if kind == "ffn":
            layer, which = divmod(n_ffn, 2)
            g, u, dn = w_gate[layer, which], w_up[layer, which], w_down[layer, which]
            for n in range(NBLK):
                s = (n * FB, (n + 1) * FB)
                a += slabs(np.concatenate([columns(g, s), columns(u, s)], axis=2))
                b.append(down_rows(dn, n * FB).reshape(P, PIECE))
            n_ffn += 1
        elif kind == "ssd":
            x0, b0, c0 = INNER, 2 * INNER, 2 * INNER + GROUPS * STATE
            dt0 = c0 + GROUPS * STATE
            for n in range(GROUPS):
                a += slabs(columns(w_in, (x0 + n * GC, x0 + (n + 1) * GC),
                                   (b0 + n * STATE, b0 + (n + 1) * STATE),
                                   (c0 + n * STATE, c0 + (n + 1) * STATE)))
            dtw = columns(w_in, (dt0, dt0 + 2 * HEADS)).reshape(P, -1)
            z = [columns(w_in, (n * GC, (n + 1) * GC)).reshape(P, PIECE) for n in range(GROUPS)]
            o = [down_rows(w_out, n * GC).reshape(P, PIECE) for n in range(GROUPS)]
            b.append(z[0])
            for n in range(1, GROUPS):
                b += [z[n], o[n - 1]]
            b.append(o[GROUPS - 1])
        else:
            for s in (QKV - 512, QKV), (0, 512), (512, 1024):
                a += slabs(columns(w_qkv, s))
            for n in range(KVH):
                a.append(down_rows(w_o, n * 2 * P).reshape(P, PIECE))
    r = np.arange(P)
    ident = np.eye(P, dtype=np.float32)
    consts = np.stack([r[:, None] <= r, r[:, None] >= r,
                       r[:, None] < r, r[:, None] > r], axis=1).astype(np.float32)
    cw = np.asarray(inputs["ssd_conv_w"])[0]
    cb = np.asarray(inputs["ssd_conv_b"])
    params = np.concatenate([cw, cb], axis=0)
    px, pb, pc = params[:, :INNER], params[:, INNER:INNER + 1024], params[:, INNER + 1024:]
    tiles = np.stack([pb.reshape(6, GROUPS, P), pc.reshape(6, GROUPS, P),
                      px.reshape(6, GROUPS, 2, P)[:, :, 0], px.reshape(6, GROUPS, 2, P)[:, :, 1]], axis=2)
    half = AD // 2
    inv_freq = np.float32(10000.0) ** (-np.arange(half, dtype=np.float32) / np.float32(half))
    angle = np.arange(TOK, dtype=np.float32)[:, None] * inv_freq[None, :].astype(np.float32)
    cos, sin = np.cos(angle), np.sin(angle)
    rope = np.stack([np.concatenate([cos, cos], axis=1), np.concatenate([-sin, sin], axis=1)], axis=1)
    rope = rope.reshape(NT, P, 2, AD).transpose(1, 0, 2, 3).astype(np.float32)
    tok = np.arange(TOK)
    mask = np.where(np.abs(tok[:, None] - tok[None, :]) <= WINDOW, 0.0, -3e38).astype(np.float32)
    qn, kn = np.asarray(inputs["attn_q_norm"])[0], np.asarray(inputs["attn_k_norm"])[0]
    return {
        "mask": np.ascontiguousarray(mask.reshape(NT, P, TOK).transpose(1, 0, 2)),
        "rope": np.ascontiguousarray(rope),
        "attn": np.concatenate([qn, qn[half:], qn[:half], kn, kn[half:], kn[:half],
                                np.asarray(inputs["attn_sink"])[0]]),
        "a": np.stack(a), "b": np.stack(b), "x": np.asarray(inputs["x"]),
        "norm": np.asarray(inputs["norm_w"]).reshape(-1, D),
        "convp": np.ascontiguousarray(tiles.transpose(3, 1, 2, 0)),
        "chan": np.ascontiguousarray(np.stack(
            [np.asarray(inputs["ssd_norm_w"])[0], np.repeat(np.asarray(inputs["ssd_d"])[0], HD)]
        ).reshape(2, GROUPS, 2, P).transpose(3, 0, 1, 2)),
        "heads": np.concatenate([np.asarray(inputs["ssd_dt_bias"])[0],
                                 np.asarray(inputs["ssd_a_log"])[0]], axis=0),
        "dtw": np.ascontiguousarray(dtw),
        "consts": consts,
        "ident": ident,
    }


def kernel(**inputs):
    import concourse.bacc as bacc
    from concourse.bass_utils import run_bass_kernel_spmd

    nc = bacc.Bacc("TRN2", target_bir_lowering=False, num_devices=1)
    arrays, drams = {}, {}
    for name, a in lay_out(inputs).items():
        arrays[f"in_{name}"] = a
        drams[name] = nc.dram_tensor(f"in_{name}", a.shape, mybir.dt.from_np(a.dtype),
                                     kind="ExternalInput").ap()
    rows = nc.dram_tensor("cum_rows", (HEADS, 2 * TOK), F32, kind="Internal").ap()
    out = nc.dram_tensor("out_0", (1, TOK, D), F32, kind="ExternalOutput").ap()
    build_program(nc, drams["a"], drams["b"], drams["x"], drams["norm"], drams["convp"],
                  drams["chan"], drams["heads"], drams["dtw"], drams["ident"], drams["consts"], rows,
                  drams["mask"], drams["rope"], drams["attn"], out)
    return run_bass_kernel_spmd(nc, [arrays], core_ids=[0]).results[0]["out_0"]
```

```python
from contextlib import ExitStack

import numpy as np
import concourse.bass as bass
from concourse import mybir

F32 = mybir.dt.float32
F32R = mybir.dt.float32r
ALU = mybir.AluOpType
ACT = mybir.ActivationFunctionType
AX_X = mybir.AxisListType.X

P = 128
TOK = 256
NT = TOK // P
D = 1024
KD = D // P
EPS = 1e-6

D_FF = 2816
FB = 256
NBLK = D_FF // FB

INNER = 2048
HEADS = 32
HD = 64
GROUPS = 8
STATE = 128
TAPS = 5
GH = HEADS // GROUPS
GC = GH * HD
NQ = 10

AH = 16
KVH = 4
AD = 64
WINDOW = 128
QKV = (AH + 2 * KVH) * AD

SLAB = KD * 512
PIECE = 2048

WORK = 9300

PHASES = ("ffn", "ssd", "ffn", "ffn", "attn", "ffn")
SLABS_OF = {"ffn": NBLK, "ssd": GROUPS, "attn": 5}
PIECES_OF = {"ffn": NBLK, "ssd": 2 * GROUPS, "attn": 0}
ROWS_OF = {"ffn": NBLK + 1, "ssd": GROUPS, "attn": AH // 2}


def before(of, p):
    return sum(of[k] for k in PHASES[:p])


def at(c, i, m):
    return c if i is None else i * m + c


def wait(eng, sem, value):
    if isinstance(value, int) and value <= 0:
        return
    eng.wait_ge(sem, value)


class Own:

    def __init__(self, eng, sem):
        self.eng, self.sem, self.n, self.turn = eng, sem, 0, None

    def count(self, n=0):
        return self.n + n if self.turn is None else self.turn + (self.n + n)

    def done(self, ins):
        ins.then_inc(self.sem, 1)
        self.n += 1

    def wait(self):
        self.eng.wait_ge(self.sem, self.count())

    def enter(self, i, per):
        self.turn, self.start, self.per = i * per, self.n, per

    def leave(self, turns):
        assert self.n - self.start == self.per, (self.n, self.start, self.per)
        self.turn, self.n = None, self.start + turns * self.per


def build_program(nc, a_dram, b_dram, x_dram, norm_dram, convp_dram, chan_dram, heads_dram, dtw_dram,
                  ident_dram, consts_dram, rows_dram, mask_dram, rope_dram, attn_dram, out_dram):
    last = len(PHASES) - 1

    with ExitStack() as ctx:
        def sb(name, shape, dt=F32):
            return ctx.enter_context(nc.sbuf_tensor(name, shape, dt))

        def sem(name):
            return ctx.enter_context(nc.semaphore(name))

        x = sb("x", [P, NT, D])
        xn = sb("xn", [P, NT, D])
        xT_hi = sb("xT_hi", [P, KD, TOK], F32R)
        xT_lo = sb("xT_lo", [P, KD, TOK], F32R)
        norm_w = sb("norm_w", [P, 2, D])
        raw_a = sb("raw_a", [P, 2, 2, PIECE])
        raw_b = sb("raw_b", [P, PIECE])
        a_hi = sb("a_hi", [P, 2, SLAB], F32R)
        a_lo = sb("a_lo", [P, 2, SLAB], F32R)
        b_hi = sb("b_hi", [P, PIECE], F32R)
        b_lo = sb("b_lo", [P, PIECE], F32R)
        hT_hi = sb("hT_hi", [P, 2, TOK], F32R)
        dt_hi = sb("dt_hi", [P, KD * 2 * HEADS], F32R)[:, :]
        dt_lo = sb("dt_lo", [P, KD * 2 * HEADS], F32R)[:, :]
        hT_lo = sb("hT_lo", [P, 2, TOK], F32R)
        ident = sb("ident", [P, P])[:, :]
        consts = sb("consts", [P, 4, P])
        small = sb("small", [P, 16])
        with nc.sbuf_tensor("b2_hi", [P, PIECE], F32R) as b2_hi, \
                nc.sbuf_tensor("b2_lo", [P, PIECE], F32R) as b2_lo:
            pass
        work = sb("work", [P, WORK])

        class Carve:
            def __init__(self):
                self.at = 0

            def __call__(self, *shape):
                n = int(np.prod(shape))
                v = work[:, self.at:self.at + n]
                self.at += n
                assert self.at <= WORK, self.at
                if len(shape) == 1:
                    return v
                names = "abcd"[:len(shape)]
                return v.rearrange(f"p ({' '.join(names)}) -> p {' '.join(names)}",
                                   **dict(zip(names, shape)))

        carve = Carve()
        carve(2, PIECE)
        b_slots = [(raw_b[:, :], b_hi[:, :], b_lo[:, :]), (carve(PIECE), b2_hi[:, :], b2_lo[:, :])]
        silu_g = carve(NT, FB)
        h = carve(NT, FB)
        FFN_WORK = carve.at

        upto, downto, above, below = (consts[:, i, :] for i in range(4))
        mean_sq, rms, minus_half = small[:, 0:2], small[:, 2:4], small[:, 4:5]
        mean_eps = small[:, 5:7]
        y_ss, y_mean, y_rms = small[:, 8:10], small[:, 10:12], small[:, 12:14]

        banks = [ctx.enter_context(nc.psum_tensor(f"bank{i}", [P, 512], F32)) for i in range(8)]
        acc = banks[0:4]

        ident_in = sem("ident_in")
        small_in = sem("small_in")
        x_in = [sem("x_in0"), sem("x_in1")]
        first_norm_in = sem("first_norm_in")
        norm_in = [sem("norm_in0"), sem("norm_in1")]
        a_in = [[sem(f"a_in{s}{h}") for h in range(2)] for s in range(2)]
        b_in = [sem("b_in0"), sem("b_in1")]
        a_hi_made = sem("a_hi_made")
        a_lo_made = sem("a_lo_made")
        a_used = sem("a_used")
        b_hi_made = sem("b_hi_made")
        b_lo_made = sem("b_lo_made")
        b_used = sem("b_used")
        first_hi_made = sem("first_hi_made")
        first_lo_made = sem("first_lo_made")
        squares = sem("squares")
        rms_made = sem("rms_made")
        xn_made = sem("xn_made")
        xT_put = sem("xT_put")
        xT_hi_made = sem("xT_hi_made")
        xT_lo_made = sem("xT_lo_made")
        gu_put = sem("gu_put")
        silu_made = sem("silu_made")
        h_made = sem("h_made")
        hT_put = sem("hT_put")
        hT_hi_made = sem("hT_hi_made")
        hT_lo_made = sem("hT_lo_made")
        acc_put = sem("acc_put")
        x_made = sem("x_made")
        stored = sem("stored")
        dve_own = sem("dve_own")
        pool_own = sem("pool_own")
        dt_hi_made = sem("dt_hi_made")
        dt_lo_made = sem("dt_lo_made")
        dt_put = sem("dt_put")
        absdt_made = sem("absdt_made")
        exp_dt_made = sem("exp_dt_made")
        da_made = sem("da_made")
        cums_put = sem("cums_put")
        rows_made = sem("rows_made")
        rows_out = sem("rows_out")
        rows_in = sem("rows_in")
        z_put = sem("z_put")
        zs_made = sem("zs_made")
        proj_put = sem("proj_put")
        conv_made = sem("conv_made")
        act_made = sem("act_made")
        cb_put = sem("cb_put")
        xtok_put = sem("xtok_put")
        xtok_made = sem("xtok_made")
        table_made = sem("table_made")
        args_made = sem("args_made")
        exps_made = sem("exps_made")
        weights_made = sem("weights_made")
        m_made = sem("m_made")
        y_put = sem("y_put")
        gated = sem("gated")
        y_squares = sem("y_squares")
        squares_added = sem("squares_added")
        y_sum_put = sem("y_sum_put")
        y_sum = sem("y_sum")
        y_rms_made = sem("y_rms_made")
        attn_in = sem("attn_in")
        tables_made = sem("tables_made")
        qkv_put = sem("qkv_put")
        qkv_made = sem("qkv_made")
        sq_made = sem("sq_made")
        ss_made = sem("ss_made")
        head_rms_made = sem("head_rms_made")
        swap_made = sem("swap_made")
        rot_made = sem("rot_made")
        k_made = sem("k_made")
        turn_put = sem("turn_put")
        turn_made = sem("turn_made")
        s_put = sem("s_put")
        shift_made = sem("shift_made")
        probs_made = sem("probs_made")
        probsT_put = sem("probsT_put")
        probsT_hi = sem("probsT_hi")
        probsT_lo = sem("probsT_lo")
        o_put = sem("o_put")
        probs_normed = sem("probs_normed")

        block = ctx.enter_context(nc.Block())

        def blocks(eng, body, peel, end, own=None, per=0, first=0):
            for c in range(first, peel):
                body(c, None)
            turns = (end - peel) // 2
            assert peel + 2 * turns == end
            with eng.Fori(0, turns) as i:
                if own:
                    own.enter(i, per)
                for u in range(2):
                    body(peel + u, i)
            if own:
                own.leave(turns)

        def load_slab(sp, c, i, parts=range(2)):
            for h in parts:
                wait(sp, a_lo_made, at(2 * c - 3 + h, i, 4))
                src = a_dram[2 * c + h] if i is None else \
                    a_dram[bass.ds(i * 4 + (2 * c + h), 1)].rearrange("a p n -> p (a n)")
                sp.dma_start(raw_a[:, c % 2, h, :], src).then_inc(a_in[c % 2][h], 16)

        def load_b(sp, c, i, m, slot=0, split=None):
            wait(sp, b_lo_made, at(c if split is None else split, i, m))
            src = b_dram[c] if i is None else \
                b_dram[bass.ds(i * m + c, 1)].rearrange("a p n -> p (a n)")
            sp.dma_start(b_slots[slot][0], src).then_inc(b_in[slot], 16)

        def split_slab_hi(act, c, i, h):
            act.wait_ge(a_in[c % 2][h], at(16 * (c // 2 + 1), i, 16))
            if h == 0:
                wait(act, a_used, at(c - 1, i, 2))
            act.activation(a_hi[:, c % 2, h * PIECE:(h + 1) * PIECE], raw_a[:, c % 2, h, :],
                           ACT.Copy).then_inc(a_hi_made, 1)

        def split_slab_lo(dve, c, i, h):
            dve.wait_ge(a_hi_made, at(2 * c + h + 1, i, 4))
            dve.tensor_tensor(a_lo[:, c % 2, h * PIECE:(h + 1) * PIECE], raw_a[:, c % 2, h, :],
                              a_hi[:, c % 2, h * PIECE:(h + 1) * PIECE].bitcast(F32),
                              ALU.subtract).then_inc(a_lo_made, 1)

        def split_b_hi(act, c, i, m, loads, ml, slot=0, used=None):
            act.wait_ge(b_in[slot], at(16 * loads, i, 16 * ml))
            wait(act, b_used, at(c if used is None else used, i, m))
            act.activation(b_slots[slot][1], b_slots[slot][0], ACT.Copy).then_inc(b_hi_made, 1)

        def split_b_lo(dve, c, i, m, slot=0):
            dve.wait_ge(b_hi_made, at(c + 1, i, m))
            raw, hi, lo = b_slots[slot]
            dve.tensor_tensor(lo, raw, hi.bitcast(F32), ALU.subtract).then_inc(b_lo_made, 1)

        def three_passes(pe, out, still, moving, first, final):
            mms = (pe.matmul(out, lhsT=still[0], rhs=moving[0], start=first, stop=False),
                   pe.matmul(out, lhsT=still[1], rhs=moving[0], start=False, stop=False),
                   pe.matmul(out, lhsT=still[0], rhs=moving[1], start=False, stop=final))
            return mms[0], mms[2]

        def xT(k, t):
            return xT_hi[:, k, t * P:(t + 1) * P], xT_lo[:, k, t * P:(t + 1) * P]

        def slab(c, k, lo=0, n=512):
            s = k * 512 + lo
            return a_hi[:, c % 2, s:s + n], a_lo[:, c % 2, s:s + n]

        def wait_slab(pe, c, i, k):
            if k % 4 == 0:
                pe.wait_ge(a_lo_made, at(2 * c + k // 4 + 1, i, 4))

        def hT(j, t):
            return hT_hi[:, j, t * P:(t + 1) * P], hT_lo[:, j, t * P:(t + 1) * P]

        def project_rows(pe, q, i, m, rows, first, final, turned=hT, tiles=range(NT)):
            pe.wait_ge(hT_lo_made, at(q + 1, i, m))
            start = None
            for t in tiles:
                for j in range(2):
                    w = turned(j, t)
                    for half in range(2):
                        s = j * D + half * 512
                        a, b = three_passes(pe, acc[2 * t + half][:, :], w, rows(s),
                                            first and j == 0, final and j == 1)
                        start = start or a
                if final:
                    b.then_inc(acc_put, 1)
            return start, b

        def b_rows(slot):
            _, hi, lo = b_slots[slot]
            return lambda s: (hi[:, s:s + 512], lo[:, s:s + 512])

        def late_rms(p):
            return PHASES[p] in ("ffn", "attn")

        def halves(p, t, half):
            return 4 * p + 2 * t + half + 1

        def norm_bank(t, half):
            return banks[((4, 7), (5, 6))[t][half]]

        def square_act(act, p, t):
            if p == 0:
                act.wait_ge(x_in[t], 16)
            else:
                act.wait_ge(x_made, 2 * (p - 1) + t + 1)
            if late_rms(p):
                act.wait_ge(xT_put, halves(p, t, 1))
            act.activation(xn[:, t, :], x[:, t, :], ACT.Square,
                           accum_out=mean_sq[:, t:t + 1]).then_inc(squares, 1)

        def norm_act_early(act, p, t):
            if not late_rms(p):
                square_act(act, p, t)

        def norm_act(act, p, t, square=True):
            for half in range(2):
                act.wait_ge(xT_put, halves(p, t, half))
                act.activation(xT_hi[:, 4 * half:4 * half + 4, t * P:(t + 1) * P],
                               norm_bank(t, half)[:, :].rearrange("p (k n) -> p k n", k=4),
                               ACT.Copy).then_inc(xT_hi_made, 1)
            if late_rms(p) and square:
                square_act(act, p, t)

        def norm_pool(pool, own, p):
            for t in range(NT):
                pool.wait_ge(squares, 2 * p + t + 1)
                own.done(pool.tensor_scalar(mean_eps[:, t:t + 1], mean_sq[:, t:t + 1], 1.0 / D, EPS,
                                            ALU.mult, ALU.add))
                own.wait()
                pool.tensor_tensor(rms[:, t:t + 1], mean_eps[:, t:t + 1], minus_half,
                                   ALU.pow).then_inc(rms_made, 1)

        def norm_dve(dve, p, t):
            if p == 0:
                dve.wait_ge(x_in[t], 16)
            else:
                dve.wait_ge(x_made, 2 * (p - 1) + t + 1)
            if t == 0 and p == 0:
                dve.wait_ge(first_norm_in, 16)
            elif t == 0:
                dve.wait_ge(norm_in[p % 2], 16 * ((p + 1) // 2))
            if not late_rms(p):
                dve.wait_ge(rms_made, 2 * p + t + 1)
            for half in range(2):
                s = slice(half * 512, (half + 1) * 512)
                if late_rms(p):
                    ins = dve.tensor_tensor(xn[:, t, s], x[:, t, s], norm_w[:, p % 2, s], ALU.mult)
                else:
                    ins = dve.scalar_tensor_tensor(xn[:, t, s], x[:, t, s], rms[:, t:t + 1],
                                                   norm_w[:, p % 2, s], ALU.mult, ALU.mult)
                ins.then_inc(xn_made, 1)

        def norm_lo_dve(dve, p, t):
            n = slice(t * P, (t + 1) * P)
            for half in range(2):
                k = slice(4 * half, 4 * half + 4)
                dve.wait_ge(xT_hi_made, halves(p, t, half))
                dve.tensor_tensor(xT_lo[:, k, n],
                                  norm_bank(t, half)[:, :].rearrange("p (k n) -> p k n", k=4),
                                  xT_hi[:, k, n].bitcast(F32), ALU.subtract).then_inc(xT_lo_made, 1)

        def norm_pe(pe, p, t):
            for half in range(2):
                pe.wait_ge(xn_made, halves(p, t, half))
                for k in range(4):
                    mm = pe.transpose(norm_bank(t, half)[:, k * P:(k + 1) * P],
                                      xn[:, t, (4 * half + k) * P:(4 * half + k + 1) * P], ident)
                mm.then_inc(xT_put, 1)

        def first_product(mm, p):
            if p > 0:
                mm.then_inc(b_used if PIECES_OF[PHASES[p - 1]] else a_used, 1)

        def residual_dve(dve, p, t, scale):
            dve.wait_ge(acc_put, 2 * p + t + 1)
            for half in range(2):
                s = slice(half * 512, (half + 1) * 512)
                ins = dve.scalar_tensor_tensor(x[:, t, s], acc[2 * t + half][:, :], scale,
                                               x[:, t, s], ALU.mult, ALU.add)
            ins.then_inc(x_made, 1)

        def end_dve(dve, p, scale):
            residual_dve(dve, p, 0, scale(0))
            if p < last:
                norm_dve(dve, p + 1, 0)
            if p < last:
                norm_lo_dve(dve, p + 1, 0)
            residual_dve(dve, p, 1, scale(1))

        def rows_hi(act, q, i, m, bank, tiles=range(NT)):
            act.wait_ge(hT_put, at(q + 1, i, m))
            n = slice(tiles[0] * P, (tiles[-1] + 1) * P)
            act.activation(hT_hi[:, :, n], bank[:, :].rearrange("p (j n) -> p j n", j=2)[:, :, n],
                           ACT.Copy).then_inc(hT_hi_made, 1)

        def rows_lo(dve, q, i, m, bank, tiles=range(NT)):
            dve.wait_ge(hT_hi_made, at(q + 1, i, m))
            n = slice(tiles[0] * P, (tiles[-1] + 1) * P)
            dve.tensor_tensor(hT_lo[:, :, n], bank[:, :].rearrange("p (j n) -> p j n", j=2)[:, :, n],
                              hT_hi[:, :, n].bitcast(F32), ALU.subtract).then_inc(hT_lo_made, 1)

        gate_up, turned = banks[4:6], banks[6]

        def turns_before(p):
            return sum(ROWS_OF[k] for k in PHASES[:p] if k == "ffn")

        def bases(p):
            return (before(SLABS_OF, p), before(PIECES_OF, p), before(ROWS_OF, p),
                    NBLK * sum(k == "ffn" for k in PHASES[:p]))

        def slot_loads(p, c):
            ffn_before = sum(k == "ffn" for k in PHASES[:p])
            if c % 2:
                return ffn_before * (NBLK // 2) + c // 2 + 1
            return before(PIECES_OF, p) - ffn_before * (NBLK // 2) + c // 2 + 1

        def ffn_sync(sp, p):
            a0, b0, _, _ = bases(p)

            def load_rows(c, i):
                if c == 1 and p > 0:
                    sp.wait_ge(x_made, 2 * p)
                load_b(sp, b0 + c, i, 2, slot=c % 2, split=b0 + max(c - 1, 0))

            def body(c, i):
                load_slab(sp, a0 + c + 1, i)
                load_rows(c, i)

            blocks(sp, body, 2, NBLK - 1)
            if p < last:
                load_slab(sp, a0 + NBLK, None)
            load_rows(NBLK - 1, None)

        def ffn_act(act, p):
            a0, b0, q0, f0 = bases(p)

            def silu(c, i, t):
                if c == 0:
                    act.wait_ge(rms_made, 2 * p + t + 1)
                act.wait_ge(gu_put, at(2 * (f0 + c) + t + 1, i, 4))
                wait(act, h_made, at(2 * (f0 + c) + t - 1, i, 4))
                act.activation(silu_g[:, t, :], gate_up[t][:, 0:FB], ACT.Silu,
                               scale=rms[:, t:t + 1]).then_inc(silu_made, 1)

            def split_rows(c, i):
                split_b_hi(act, b0 + c, i, 2, loads=slot_loads(p, c), ml=1, slot=c % 2,
                           used=b0 + max(c - 1, 0))

            def block_act(c, i):
                for t in range(NT):
                    split_slab_hi(act, a0 + c + 1, i, t)
                    silu(c, i, t)
                rows_hi(act, turns_before(p) + c, i, 2, turned)
                split_rows(c, i)

            norm_act_early(act, p, 1)
            norm_act(act, p, 1)
            blocks(act, block_act, 2, NBLK - 1)
            c = NBLK - 1
            if p < last and PHASES[p + 1] == "ssd":
                act.wait_ge(small_in, SMALL_IN)
                act.activation(dt_hi, dt_w, ACT.Copy).then_inc(dt_hi_made, 1)
            if p < last:
                split_slab_hi(act, a0 + NBLK, None, 0)
            silu(c, None, 0)
            split_rows(c, None)
            rows_hi(act, turns_before(p) + c, None, 2, turned, tiles=(0,))
            if p < last:
                split_slab_hi(act, a0 + NBLK, None, 1)
            silu(c, None, 1)
            if p < last:
                norm_act_early(act, p + 1, 0)
            rows_hi(act, turns_before(p) + c + 1, None, 2, turned, tiles=(1,))
            if p < last:
                norm_act(act, p + 1, 0)

        def ffn_dve(dve, own, p):
            a0, b0, q0, f0 = bases(p)

            def times_up(c, i, t):
                dve.wait_ge(silu_made, at(2 * (f0 + c) + t + 1, i, 4))
                wait(dve, hT_put, at(turns_before(p) + c, i, 2))
                dve.scalar_tensor_tensor(h[:, t, :], gate_up[t][:, FB:2 * FB], rms[:, t:t + 1],
                                         silu_g[:, t, :], ALU.mult, ALU.mult).then_inc(h_made, 1)

            def block_dve(c, i):
                for t in range(NT):
                    split_slab_lo(dve, a0 + c + 1, i, t)
                    times_up(c, i, t)
                rows_lo(dve, q0 + c, i, 2, turned)
                split_b_lo(dve, b0 + c, i, 2, slot=c % 2)

            norm_dve(dve, p, 1)
            norm_lo_dve(dve, p, 1)
            blocks(dve, block_dve, 2, NBLK - 1)
            c = NBLK - 1
            if p < last and PHASES[p + 1] == "ssd":
                dve.wait_ge(dt_hi_made, 1)
                dve.tensor_tensor(dt_lo, dt_w, dt_hi.bitcast(F32), ALU.subtract).then_inc(dt_lo_made, 1)
            if p < last:
                split_slab_lo(dve, a0 + NBLK, None, 0)
            times_up(c, None, 0)
            split_b_lo(dve, b0 + c, None, 2, slot=0)
            rows_lo(dve, q0 + c, None, 2, turned, tiles=(0,))
            if p < last:
                split_slab_lo(dve, a0 + NBLK, None, 1)
            times_up(c, None, 1)
            residual_dve(dve, p, 0, 0.5)
            if p < last:
                norm_dve(dve, p + 1, 0)
            rows_lo(dve, q0 + c + 1, None, 2, turned, tiles=(1,))
            if p < last:
                norm_lo_dve(dve, p + 1, 0)
            residual_dve(dve, p, 1, 0.5)

        def ffn_pe(pe, p):
            a0, b0, q0, f0 = bases(p)

            def gate_and_up(c, i, t):
                for k in range(KD):
                    if t == 0 and a0 + c == 0:
                        if k % 4 == 3:
                            pe.wait_ge(a_lo_made, k // 4 + 1)
                        else:
                            pe.wait_ge(first_lo_made, 3 * (k // 4) + k % 4 + 1)
                    elif t == 0:
                        wait_slab(pe, a0 + c, i, k)
                    if c == 0 and k % 4 == 0:
                        pe.wait_ge(xT_lo_made, halves(p, t, k // 4))
                    a, mm = three_passes(pe, gate_up[t][:, :], xT(k, t), slab(a0 + c, k),
                                         k == 0, k == KD - 1)
                    if k == 0:
                        first = a
                    if c == t == 0 and k == (3 if p else KD - 1):
                        norm_pe(pe, p, 1)
                mm.then_inc(gu_put, 1)
                return first

            def down(c, i, final=False, tiles=range(NT)):
                pe.wait_ge(b_lo_made, at(b0 + c + 1, i, 2))
                q = q0 + c + (tiles == (1,) and c == NBLK - 1)
                return project_rows(pe, q, i, 2, b_rows(c % 2), c == 0, final, tiles=tiles)

            def turn(c, i, t):
                pe.wait_ge(h_made, at(2 * (f0 + c) + t + 1, i, 4))
                for j in range(2):
                    mm = pe.transpose(turned[:, j * TOK + t * P:j * TOK + (t + 1) * P],
                                      h[:, t, j * P:(j + 1) * P], ident)
                return mm

            def block_pe(c, i):
                if c == 0:
                    first_product(gate_and_up(c, i, 0), p)
                    gate_and_up(c, i, 1)
                    return
                if c == 1:
                    pe.wait_ge(h_made, 2 * f0 + 1)
                    gate_and_up(c, i, 0).then_inc(a_used, 1)
                    turn(0, i, 0)
                    turn(0, i, 1).then_inc(hT_put, 1)
                else:
                    gate_and_up(c, i, 0)
                gate_and_up(c, i, 1)
                start, end = down(c - 1, i)
                start.then_inc(a_used, 1)
                end.then_inc(b_used, 1)
                turn(c, i, 0)
                turn(c, i, 1).then_inc(hT_put, 1)

            blocks(pe, block_pe, 2, NBLK - 1)
            c = NBLK - 1
            gate_and_up(c, None, 0)
            down(c - 1, None, tiles=(0,))
            turn(c, None, 0).then_inc(hT_put, 1)
            gate_and_up(c, None, 1)
            start, _ = down(c, None, final=True, tiles=(0,))
            start.then_inc(a_used, 1)
            _, end = down(c - 1, None, tiles=(1,))
            end.then_inc(b_used, 1)
            turn(c, None, 1).then_inc(hT_put, 1)
            if p < last:
                norm_pe(pe, p + 1, 0)
            down(c, None, final=True, tiles=(1,))

        proj_bc, proj_x, z_bank, y_bank = banks[4:8]
        carve = Carve()
        chan = carve(4, TOK)
        zs = carve(2, TOK)
        x_tok = carve(NT * GC)
        decay = carve(GH, 4, P)
        dt_masked = carve(GH, 2, P)
        dt_behind = carve(GH, 2, P)
        y = carve(2, TOK)
        y_sq = carve(2, TOK)
        y_sq_sum = carve(2, TOK)
        table = carve(GROUPS, NQ, GH)
        assert carve.at >= FFN_WORK
        convp = carve(GROUPS, 4, TAPS + 1)
        chan_par = carve(2, GROUPS, 2)
        heads_in = carve(4, HEADS)
        dt_w = carve(KD * 2 * HEADS)
        ynw, d_skip = chan_par[:, 0], chan_par[:, 1]
        dtv = decay.rearrange("p a b c -> p (a b c)")
        rows = xn[:, :, :].rearrange("p t d -> p (t d)").rearrange("p (h d n) -> p h d n", h=GH, d=2)
        rows_flat = xn[:, :, :].rearrange("p t d -> p (t d)")
        v_dt, max_dt, e_dt, s_dt, s2_dt, poly_dt, dt, da = (dtv[:, n * P:(n + 1) * P] for n in range(8))
        dt_bias, a_log = (heads_in[:, n:n + 2, :].rearrange("p a h -> p (a h)") for n in (0, 2))
        exp_a = dtv[:, 8 * P:8 * P + 2 * HEADS]
        rows_sb = dt_behind.rearrange("p a b c -> p (a b c)")[0:HEADS, 0:2 * TOK]
        dt_bank, cum_bank, row_bank = acc[0], acc[1], acc[2]
        NF, SD, REM, DTF, DTB = 0, 2, 4, 6, 8
        diagonal, across = slice(0, 4, 3), slice(1, 3)

        def cb_bank(c):
            return acc[3] if c == 0 else proj_bc

        def z_piece(c):
            return max(2 * c - 1, 0)

        def rows_piece(c):
            return min(2 * c + 2, 2 * GROUPS - 1)

        def of_group(v, c, i):
            if i is None:
                return v[:, c]
            one = v[:, bass.ds(i * 2 + c, 1)]
            names = "bcd"[:len(v.shape) - 2]
            return one.rearrange(f"p a {' '.join(names)} -> p (a {names[0]}) {' '.join(names[1:])}")

        def scalars(c, i):
            return table[:, c] if i is None else \
                table[:, bass.ds(i * 2 + c, 1), :, :].rearrange("p a q h -> p (a q) h")

        def ssd_sync(sp, p):
            a0, b0, _, _ = bases(p)

            def load_cums(c, i):
                wait(sp, exps_made, at(GH * c, i, 2 * GH))
                src = rows_dram[c * GH:(c + 1) * GH, :] if i is None else \
                    rows_dram[bass.ds(i * (2 * GH) + c * GH, GH), :]
                sp.dma_start(rows_flat, src.rearrange("h n -> (h n)").unsqueeze(0)
                             .broadcast_to([P, GH * 2 * TOK])).then_inc(rows_in, 16)

            def load_z(c, i):
                load_b(sp, b0 + z_piece(c), i, 4)

            def body(c, i):
                if c >= 2:
                    load_slab(sp, a0 + c + 1, i)
                    load_z(c, i)
                if c == 1:
                    load_b(sp, b0 + 2 * c, i, 4)
                load_cums(c, i)
                if c > 1:
                    load_b(sp, b0 + 2 * c, i, 4)

            for c in range(2):
                load_slab(sp, a0 + c + 1, None)
                load_z(c, None)
            sp.wait_ge(rows_made, 1)
            sp.dma_start(rows_dram[:, :], rows_sb).then_inc(rows_out, 16)
            sp.wait_ge(rows_out, 16)
            sp.wait_ge(xT_put, halves(p, 1, 1))
            load_cums(0, None)
            blocks(sp, body, 2, GROUPS, first=1)
            load_b(sp, b0 + rows_piece(GROUPS - 1), None, 4)

        POOL_SPLITS = ((1, 0), (1, 1), (2, 1))

        def ssd_pool(pool, own, p):
            a0, b0, _, _ = bases(p)

            def by_head(c, i, first):
                two = scalars(c, i)[:, first:first + 2, :]
                return two.rearrange("p n h -> p h n").unsqueeze(3).broadcast_to([P, GH, 2, P])

            def masked(v):
                return v.unsqueeze(1).unsqueeze(1).broadcast_to([P, GH, 2, P])

            def mask_dt(c, i):
                wait(pool, weights_made, at(GH * c, i, 2 * GH))
                own.done(pool.tensor_tensor(dt_masked, masked(upto), by_head(c, i, DTF), ALU.mult))
                own.done(pool.tensor_tensor(dt_behind, masked(downto), by_head(c, i, DTB), ALU.mult))
                own.wait()
                own.done(pool.tensor_tensor(dt_masked, dt_masked, dt_behind, ALU.add))
                own.wait()

            def weights(c, i):
                for j in range(GH):
                    pool.wait_ge(exps_made, at(GH * c + j + 1, i, 2 * GH))
                    pool.tensor_tensor(decay[:, j, diagonal, :], decay[:, j, diagonal, :],
                                       dt_masked[:, j, :, :], ALU.mult)
                    pool.tensor_tensor(decay[:, j, across, :], decay[:, j, across, :],
                                       scalars(c, i)[:, DTF:DTB + 2:3, j:j + 1].broadcast_to([P, 2, P]),
                                       ALU.mult).then_inc(weights_made, 1)

            def add_squares(c, i):
                pool.wait_ge(y_squares, at(c + 1, i, 2))
                pool.tensor_tensor(y_sq_sum, y_sq_sum, y_sq, ALU.add).then_inc(squares_added, 1)

            def split_slab(c, h):
                pool.wait_ge(a_lo_made, 2 * c + h)
                split_slab_lo(pool, c, None, h)

            def body(c, i):
                mask_dt(c, i)
                if c > 1:
                    split_b_lo(pool, b0 + z_piece(c), i, 4)
                weights(c, i)
                add_squares(c - 1, i)

            own.done(pool.memset(y_sq_sum, 0.0))
            own.wait()
            pool.wait_ge(b_lo_made, b0)
            split_b_lo(pool, b0, None, 4)
            for c, h in POOL_SPLITS[:2]:
                split_slab(a0 + c, h)
            pool.wait_ge(table_made, 1)
            pool.wait_ge(rows_out, 16)
            mask_dt(0, None)
            weights(0, None)
            for c, h in POOL_SPLITS[2:]:
                split_slab(a0 + c, h)
            blocks(pool, body, 2, GROUPS, own, 2 * 3, first=1)
            add_squares(GROUPS - 1, None)
            pool.wait_ge(y_sum, 1)
            for t in range(NT):
                ins = pool.tensor_tensor(y_rms[:, t:t + 1], y_mean[:, t:t + 1], minus_half, ALU.pow)
            ins.then_inc(y_rms_made, 1)

        def ssd_act(act, p):
            a0, b0, q0, _ = bases(p)
            loads = b0 - (NBLK // 2) * sum(k == "ffn" for k in PHASES[:p])

            def split_hi(piece, i):
                split_b_hi(act, b0 + piece, i, 4, loads=loads + piece + 1, ml=4)

            def y_out(c, i):
                act.wait_ge(gated, at(c + 1, i, 2))
                for j in range(2):
                    ins = act.activation(hT_hi[:, j, :], y[:, j, :], ACT.Copy,
                                         scale=of_group(ynw, c, i)[:, j:j + 1])
                ins.then_inc(hT_hi_made, 1)

            def square_y(c, i):
                wait(act, squares_added, at(c, i, 2))
                act.activation(y_sq, y, ACT.Square).then_inc(y_squares, 1)

            def exps(c, i, heads=range(GH)):
                q = scalars(c, i)
                for j in heads:
                    act.wait_ge(args_made, at(GH * c + j + 1, i, 2 * GH))
                    for n in range(2):
                        act.activation(decay[:, j, 3 * n, :], decay[:, j, 3 * n, :], ACT.Exp,
                                       bias=q[:, NF + n, j:j + 1])
                    act.activation(decay[:, j, 1, :], rows[:, j, 0, P:2 * P], ACT.Exp,
                                   bias=q[:, REM, j:j + 1])
                    act.activation(decay[:, j, 2, :], rows[:, j, 1, 0:P], ACT.Exp,
                                   bias=q[:, REM + 1, j:j + 1]).then_inc(exps_made, 1)

            def silu_x(c, i):
                act.wait_ge(z_put, at(c + 1, i, 2))
                wait(act, gated, at(c, i, 2))
                act.activation(zs, z_bank[:, :].rearrange("p (a n) -> p a n", a=2), ACT.Silu
                               ).then_inc(zs_made, 1)
                act.wait_ge(conv_made, at(2 * c + 2, i, 4))
                act.activation(chan[:, 2:4, :], chan[:, 2:4, :], ACT.Silu).then_inc(act_made, 1)

            def take_x(c, i):
                act.wait_ge(xtok_put, at(c + 1, i, 2))
                wait(act, y_put, at(c, i, 2))
                act.activation(x_tok, proj_x[:, :], ACT.Copy).then_inc(xtok_made, 1)

            def silu_bc(c, i):
                act.wait_ge(conv_made, at(2 * c + 1, i, 4))
                act.activation(chan[:, 0:2, :], chan[:, 0:2, :], ACT.Silu).then_inc(act_made, 1)

            def body(c, i):
                for t in range(2):
                    split_slab_hi(act, a0 + c + 1, i, t)
                silu_x(c - 1, i)
                split_hi(z_piece(c), i)
                if c == 1:
                    exps(0, None)
                take_x(c - 1, i)
                if c == 1:
                    split_hi(2 * c, i)
                exps(c, i, range(2))
                y_out(c - 1, i)
                if c > 1:
                    split_hi(2 * c, i)
                exps(c, i, range(2, GH))
                silu_bc(c, i)
                square_y(c - 1, i)

            norm_act_early(act, p, 1)
            norm_act(act, p, 1)
            split_hi(0, None)
            split_slab_hi(act, a0 + 1, None, 0)
            act.wait_ge(absdt_made, 1)
            act.activation(exp_a, a_log, ACT.Exp)
            act.activation(e_dt, v_dt, ACT.Exp, scale=-1.0).then_inc(exp_dt_made, 1)
            split_slab_hi(act, a0 + 1, None, 1)
            act.wait_ge(cums_put, 1)
            act.activation(rows_sb, row_bank[0:HEADS, :], ACT.Copy).then_inc(rows_made, 1)
            silu_bc(0, None)
            blocks(act, body, 2, GROUPS, first=1)
            silu_x(GROUPS - 1, None)
            take_x(GROUPS - 1, None)
            split_hi(rows_piece(GROUPS - 1), None)
            y_out(GROUPS - 1, None)
            square_y(GROUPS - 1, None)
            norm_act_early(act, p + 1, 0)
            norm_act(act, p + 1, 0)

        def ssd_dve(dve, own, p):
            a0, b0, q0, _ = bases(p)

            def discretise():
                dve.wait_ge(dt_put, 1)
                for t in range(NT):
                    s = slice(t * 2 * HEADS, (t + 1) * 2 * HEADS)
                    own.done(dve.tensor_tensor(v_dt[:, s], dt_bank[:, s], dt_bias, ALU.add))
                own.wait()
                own.done(dve.tensor_scalar(max_dt, v_dt, 0.0, None, ALU.max))
                own.wait()
                dve.scalar_tensor_tensor(v_dt, v_dt, -1.0, v_dt, ALU.mult, ALU.max).then_inc(absdt_made, 1)
                dve.wait_ge(exp_dt_made, 1)
                own.done(dve.tensor_scalar(s2_dt, e_dt, 2.0, None, ALU.add))
                own.wait()
                own.done(dve.reciprocal(poly_dt, s2_dt))
                own.wait()
                own.done(dve.tensor_tensor(s_dt, e_dt, poly_dt, ALU.mult))
                own.wait()
                own.done(dve.tensor_tensor(s2_dt, s_dt, s_dt, ALU.mult))
                own.wait()
                own.done(dve.tensor_scalar(poly_dt, s2_dt, 1.0 / 15, None, ALU.mult))
                for n in range(6, 0, -1):
                    own.wait()
                    own.done(dve.scalar_tensor_tensor(poly_dt, poly_dt, 1.0 / (2 * n + 1), s2_dt,
                                                      ALU.add, ALU.mult))
                own.wait()
                own.done(dve.scalar_tensor_tensor(poly_dt, poly_dt, 1.0, s_dt, ALU.add, ALU.mult))
                own.wait()
                own.done(dve.scalar_tensor_tensor(dt, poly_dt, 2.0, max_dt, ALU.mult, ALU.add))
                own.wait()
                for t in range(NT):
                    s = slice(t * 2 * HEADS, (t + 1) * 2 * HEADS)
                    ins = dve.scalar_tensor_tensor(da[:, s], dt[:, s], -1.0, exp_a, ALU.mult, ALU.mult)
                ins.then_inc(da_made, 1)

            def fill_table():
                def col(n):
                    return table[:, :, n, :]

                def heads(v):
                    return v.rearrange("p (g h) -> p g h", g=GROUPS)

                def cum(n):
                    return heads(cum_bank[:, n * HEADS:(n + 1) * HEADS])

                for n in range(2):
                    for d in range(2):
                        s = (2 * n + d) * HEADS
                        own.done(dve.tensor_copy(col(DTF + 2 * d + n), heads(dt[:, s:s + HEADS])))
                dve.wait_ge(cums_put, 1)
                for n in range(2):
                    own.done(dve.tensor_scalar(col(NF + n), cum(n), -1.0, None, ALU.mult))
                    own.done(dve.tensor_copy(col(REM + n), cum(4 + n)))
                own.wait()
                for n in range(2):
                    ins = dve.scalar_tensor_tensor(col(SD + n), col(NF + n), -1.0, cum(2 + n),
                                                   ALU.mult, ALU.subtract)
                ins.then_inc(table_made, 1)

            def decay_args(c, i):
                if c == 0:
                    dve.wait_ge(table_made, 1)
                q = scalars(c, i)
                dve.wait_ge(rows_in, at(16 * (c + 1), i, 32))
                wait(dve, y_put, at(c, i, 2))
                for j in range(GH):
                    for n in range(2):
                        s = slice(n * P, (n + 1) * P)
                        ins = dve.scalar_tensor_tensor(decay[:, j, 3 * n, :], rows[:, j, 1, s],
                                                       q[:, SD + n, j:j + 1], rows[:, j, 0, s],
                                                       ALU.add, ALU.min)
                    ins.then_inc(args_made, 1)

            def weigh(c, i):
                dve.wait_ge(weights_made, at(GH * (c + 1), i, 2 * GH))
                dve.wait_ge(cb_put, at(c + 1, i, 2))
                w = decay.rearrange("p h a n -> p h (a n)")
                dve.tensor_tensor(w, w, cb_bank(c)[:, :].unsqueeze(1).broadcast_to([P, GH, 2 * TOK]),
                                  ALU.mult).then_inc(m_made, 1)

            def convolve(c, i, o):
                bank = proj_x if o else proj_bc
                dve.wait_ge(proj_put, at(2 * c + o // 2 + 1, i, 4))
                par = of_group(convp, c, i).rearrange("p o n -> p (o n)")
                mid = TAPS // 2
                for n in [mid] + [n for n in range(TAPS) if n != mid]:
                    off = n - mid
                    to = slice(max(0, -off), TOK - max(0, off))
                    frm = slice(max(0, off), TOK - max(0, -off))
                    for r in range(2):
                        u = bank[:, r * TOK:(r + 1) * TOK]
                        out = chan[:, o + r, :]
                        at0 = (o + r) * (TAPS + 1)
                        tap = par[:, at0 + n:at0 + n + 1]
                        if n == mid:
                            ins = dve.tensor_scalar(out, u, tap, par[:, at0 + TAPS:at0 + TAPS + 1],
                                                    ALU.mult, ALU.add)
                        else:
                            dve.wait_ge(own.sem, own.count(-1))
                            ins = dve.scalar_tensor_tensor(out[:, to], u[:, frm], tap, out[:, to],
                                                           ALU.mult, ALU.add)
                        if n == TAPS - 1 and r == 1:
                            ins.then_inc(conv_made, 1)
                        else:
                            own.done(ins)

            def gate(c, i):
                dve.wait_ge(y_put, at(c + 1, i, 2))
                dve.wait_ge(zs_made, at(c + 1, i, 2))
                wait(dve, y_squares, at(c, i, 2))
                for j in range(2):
                    own.done(dve.scalar_tensor_tensor(y[:, j, :], chan[:, 2 + j, :],
                                                      of_group(d_skip, c, i)[:, j:j + 1],
                                                      y_bank[:, j * TOK:(j + 1) * TOK],
                                                      ALU.mult, ALU.add))
                own.wait()
                dve.tensor_tensor(y, y, zs, ALU.mult).then_inc(gated, 1)

            def y_lo(c, i):
                dve.wait_ge(hT_hi_made, at(q0 + c + 1, i, 2))
                for j in range(2):
                    ins = dve.scalar_tensor_tensor(hT_lo[:, j, :], y[:, j, :],
                                                   of_group(ynw, c, i)[:, j:j + 1],
                                                   hT_hi[:, j, :].bitcast(F32), ALU.mult, ALU.subtract)
                ins.then_inc(hT_lo_made, 1)

            def body(c, i):
                if c == 1:
                    split_b_lo(dve, b0 + z_piece(c), i, 4)
                for t in range(2):
                    if (c + 1, t) not in POOL_SPLITS:
                        dve.wait_ge(a_lo_made, at(2 * (a0 + c + 1) + t, i, 4))
                        split_slab_lo(dve, a0 + c + 1, i, t)
                if c == 1:
                    convolve(c, i, 0)
                    weigh(0, None)
                    split_b_lo(dve, b0 + 2 * c, i, 4)
                decay_args(c, i)
                gate(c - 1, i)
                if c > 1:
                    convolve(c, i, 0)
                y_lo(c - 1, i)
                if c > 1:
                    split_b_lo(dve, b0 + 2 * c, i, 4)
                convolve(c, i, 2)
                weigh(c, i)

            norm_dve(dve, p, 1)
            norm_lo_dve(dve, p, 1)
            discretise()
            convolve(0, None, 0)
            fill_table()
            convolve(0, None, 2)
            decay_args(0, None)
            blocks(dve, body, 2, GROUPS, own, 2 * (2 * 9 + 2), first=1)
            gate(GROUPS - 1, None)
            split_b_lo(dve, b0 + rows_piece(GROUPS - 1), None, 4)
            y_lo(GROUPS - 1, None)
            dve.wait_ge(y_sum_put, 1)
            dve.tensor_scalar(y_mean, z_bank[:, 0:NT], 1.0 / INNER, EPS, ALU.mult, ALU.add
                              ).then_inc(y_sum, 1)
            dve.wait_ge(y_rms_made, 1)
            end_dve(dve, p, lambda t: y_rms[:, t:t + 1])

        def ssd_pe(pe, p):
            a0, b0, q0, _ = bases(p)

            def z_proj(c, i, started=None):
                pe.wait_ge(b_lo_made, at(b0 + z_piece(c) + 1, i, 4))
                wait(pe, zs_made, at(c, i, 2))
                for m in range(2):
                    for k in range(KD):
                        s = slice(k * GC + m * P, k * GC + (m + 1) * P)
                        first, mm = three_passes(pe, z_bank[:, m * TOK:(m + 1) * TOK],
                                                 (b_hi[:, s], b_lo[:, s]),
                                                 (xT_hi[:, k, :], xT_lo[:, k, :]), k == 0, k == KD - 1)
                        if m == k == 0 and started:
                            first.then_inc(started, 1)
                mm.then_inc(z_put, 1)

            def chan_proj(c, i, o, started=None):
                bank = (proj_bc, proj_bc, proj_x, proj_x)[o]
                s = ((o + 2) % 4) * P
                for k in range(KD):
                    if o == 0:
                        wait_slab(pe, a0 + c, i, k)
                    first, mm = three_passes(pe, bank[:, (o % 2) * TOK:(o % 2 + 1) * TOK],
                                             slab(a0 + c, k, s, P), (xT_hi[:, k, :], xT_lo[:, k, :]),
                                             k == 0, k == KD - 1)
                    if k == 0 and started:
                        first.then_inc(started, 1)
                return mm

            def out_rows(c, i, piece, m, final=False, tiles=range(NT)):
                pe.wait_ge(b_lo_made, at(b0 + piece + 1, i, m))
                return project_rows(pe, q0 + c, i, 2, b_rows(0), c == 0, final, tiles=tiles)

            def y_heads(c, i):
                pe.wait_ge(m_made, at(c + 1, i, 2))
                pe.wait_ge(xtok_made, at(c + 1, i, 2))
                wait(pe, gated, at(c, i, 2))
                for j in range(GH):
                    out = y_bank[(j % 2) * HD:(j % 2 + 1) * HD, (j // 2) * TOK:(j // 2 + 1) * TOK]
                    for s in range(NT):
                        mm = pe.matmul(out, lhsT=x_tok[:, s * GC + j * HD:s * GC + (j + 1) * HD],
                                       rhs=decay[:, j, 2 * s:2 * s + 2, :].rearrange("p a n -> p (a n)"),
                                       start=s == 0, stop=s == NT - 1)
                mm.then_inc(y_put, 1)

            def c_dot_b(c, i, started=None):
                pe.wait_ge(act_made, at(2 * c + 1, i, 4))
                for s in range(NT):
                    mm = pe.matmul(cb_bank(c)[:, s * TOK:(s + 1) * TOK],
                                   lhsT=chan[:, 0, s * P:(s + 1) * P], rhs=chan[:, 1, :],
                                   start=True, stop=True)
                    if s == 0 and started:
                        mm.then_inc(started, 1)
                mm.then_inc(cb_put, 1)

            def x_turn(c, i):
                pe.wait_ge(act_made, at(2 * c + 2, i, 4))
                for t in range(NT):
                    for j in range(2):
                        mm = pe.transpose(proj_x[:, t * GC + j * P:t * GC + (j + 1) * P],
                                          chan[:, 2 + j, t * P:(t + 1) * P], ident)
                mm.then_inc(xtok_put, 1)

            def body(c, i):
                if c > 1:
                    pe.wait_ge(m_made, at(c, i, 2))
                chan_proj(c, i, 0)
                x_turn(c - 1, i)
                chan_proj(c, i, 1).then_inc(proj_put, 1)
                if c > 1:
                    y_heads(c - 1, i)
                z_proj(c, i)
                wait(pe, xtok_made, at(c, i, 2))
                chan_proj(c, i, 2, started=b_used)
                if c == 1:
                    y_heads(c - 1, i)
                chan_proj(c, i, 3).then_inc(proj_put, 1)
                start, _ = out_rows(c - 1, i, 2 * c, 4, tiles=(0,))
                start.then_inc(a_used, 1)
                c_dot_b(c, i)
                _, end = out_rows(c - 1, i, 2 * c, 4, tiles=(1,))
                end.then_inc(b_used, 1)

            def dt_proj(t):
                pe.wait_ge(dt_lo_made, 1)
                pe.wait_ge(xT_lo_made, halves(p, t, 1))
                for k in range(KD):
                    s = slice(k * 2 * HEADS, (k + 1) * 2 * HEADS)
                    first, mm = three_passes(pe, dt_bank[:, t * 2 * HEADS:(t + 1) * 2 * HEADS], xT(k, t),
                                         (dt_hi[:, s], dt_lo[:, s]), k == 0, k == KD - 1)
                    if t == k == 0:
                        first_product(first, p)
                if t == NT - 1:
                    mm.then_inc(dt_put, 1)

            def cumulate():
                pe.wait_ge(da_made, 1)
                fwd = [da[:, n * 2 * HEADS:n * 2 * HEADS + HEADS] for n in range(2)]
                bwd = [da[:, n * 2 * HEADS + HEADS:(n + 1) * 2 * HEADS] for n in range(2)]
                for n, (tri, v) in enumerate([(upto, fwd[0]), (upto, fwd[1]), (downto, bwd[0]),
                                              (downto, bwd[1]), (below, fwd[0]), (above, bwd[1])]):
                    pe.matmul(cum_bank[:, n * HEADS:(n + 1) * HEADS], lhsT=tri, rhs=v,
                              start=True, stop=True)
                for n, (tri, v) in enumerate([(upto, fwd[0]), (upto, fwd[1]),
                                              (downto, bwd[0]), (downto, bwd[1])]):
                    mm = pe.matmul(row_bank[0:HEADS, n * P:(n + 1) * P], lhsT=v, rhs=tri,
                                   start=True, stop=True)
                mm.then_inc(cums_put, 1)

            dt_proj(0)
            norm_pe(pe, p, 1)
            dt_proj(1)
            chan_proj(0, None, 0)
            chan_proj(0, None, 1).then_inc(proj_put, 1)
            chan_proj(0, None, 2)
            cumulate()
            chan_proj(0, None, 3).then_inc(proj_put, 1)
            z_proj(0, None, started=a_used)
            c_dot_b(0, None, started=b_used)
            blocks(pe, body, 2, GROUPS, first=1)
            x_turn(GROUPS - 1, None)
            y_heads(GROUPS - 1, None)
            out_rows(GROUPS - 1, None, rows_piece(GROUPS - 1), 4, final=True, tiles=(0,))
            pe.wait_ge(squares_added, GROUPS)
            pe.wait_ge(zs_made, GROUPS)
            for t in range(NT):
                for j in range(2):
                    mm = pe.matmul(z_bank[:, t:t + 1], lhsT=y_sq_sum[:, j, t * P:(t + 1) * P],
                                   rhs=upto[:, P - 1:P], start=j == 0, stop=j == 1)
            mm.then_inc(y_sum_put, 1)
            out_rows(GROUPS - 1, None, rows_piece(GROUPS - 1), 4, final=True, tiles=(1,))
            norm_pe(pe, p + 1, 0)

        STEPS = AH // 2
        carve = Carve()
        q_in = carve(2, NT, 512)
        qT = q_in.rearrange("p a b c -> p a (b c)").rearrange("p a (s n) -> p (a s) n", s=4)
        kv = carve(NT, 512)
        k_twice = carve(NT, KVH, 2, AD)
        kT = carve(KVH, TOK)
        k_rot = kT.rearrange("p a b -> p (a b)")[:, 0:NT * 256].rearrange("p (t n) -> p t n", t=NT)
        probs = carve(2, 4, TOK)
        scratch = probs.rearrange("p a b c -> p (a b c)")
        assert all(k != "attn" or p + 2 >= len(PHASES) for p, k in enumerate(PHASES))
        p_attn = PHASES.index("attn") if "attn" in PHASES else 0
        squared = [scratch[:, 0:NT * 512].rearrange("p (t n) -> p t n", t=NT)] * 2 + \
            [k_twice.rearrange("p t a b c -> p t (a b c)")]
        swapped = [scratch[:, NT * 512:2 * NT * 512].rearrange("p (t n) -> p t n", t=NT)] * 2 + \
            [norm_w[:, p_attn % 2, :].rearrange("p (t n) -> p t n", t=NT)]
        q_rot = xn[:, :, :].rearrange("p t d -> p (t d)").rearrange("p (a t n) -> p a t n", a=2, t=NT)
        prT = xn[:, :, :].rearrange("p t d -> p (t d)").rearrange("p (a e s n) -> p a e s n", a=2, e=2, s=2)
        assert carve.at >= FFN_WORK
        mask = carve(NT, TOK)
        rope = carve(NT, 2, AD)
        norm_rows = carve(4 * AD + AH)
        rope_w = carve(2, NT, 2, AD)
        head_ss = carve(NT, AH + KVH)
        head_mean = carve(NT, AH + KVH)
        head_rms = carve(NT, AH + KVH)
        half_down = carve(NT, AH)
        minus_sink = carve(AH, NT)
        stats = carve(2, 8, 4)
        minus_one = carve(4)
        MAX, NEG, DEN, SINK_ARG, SINK, SUM, INV = range(7)
        PARTS = [(AH, KVH, kv, 0), (0, 8, q_in[:, 0, :, :], 1), (8, 8, q_in[:, 1, :, :], 2)]

        def attn_sync(sp, p):
            a0 = bases(p)[0]
            for c in range(1, 5 + (p < last)):
                load_slab(sp, a0 + c, None)

        def heads64(v, n):
            return v.rearrange("p (h d) -> p h d", h=n)

        def attn_load(pool, p):
            pool.wait_ge(xn_made, 4 * p)
            pool.dma_start(mask, mask_dram).then_inc(attn_in, 16)
            pool.dma_start(rope, rope_dram).then_inc(attn_in, 16)
            pool.dma_start(norm_rows, attn_dram.unsqueeze(0).broadcast_to([P, 4 * AD + AH])
                           ).then_inc(attn_in, 16)

        def attn_pool(pool, own, p):
            pool.wait_ge(attn_in, 48)
            for n in range(2):
                for r in range(2):
                    w = norm_rows[:, (2 * n + r) * AD:(2 * n + r + 1) * AD]
                    own.done(pool.tensor_tensor(rope_w[:, n, :, r, :], rope[:, :, r, :],
                                                w.unsqueeze(1).broadcast_to([P, NT, AD]), ALU.mult))
            own.done(pool.memset(half_down, -0.5))
            own.done(pool.memset(minus_one, -1.0))
            pool.tensor_scalar(minus_sink, norm_rows[:, 4 * AD:].unsqueeze(2).broadcast_to([P, AH, NT]),
                               -1.0, None, ALU.mult).then_inc(tables_made, 1)
            own.wait()
            def swap(u, tiles=range(NT)):
                _, nh, src, _ = PARTS[u]
                n = 1 if u == 0 else 0
                for t in tiles:
                    pool.wait_ge(qkv_made, 2 * u + t + 1)
                    wait(pool, rot_made, 2 * (u - 1) + t + 1)
                    v = heads64(src[:, t, 0:nh * AD], nh)
                    to = heads64(swapped[u][:, t, 0:nh * AD], nh)
                    half = AD // 2
                    sin = rope_w[:, n, t, 1, :].unsqueeze(1).broadcast_to([P, nh, AD])
                    pool.tensor_tensor(to[:, :, 0:half], v[:, :, half:], sin[:, :, 0:half], ALU.mult)
                    pool.tensor_tensor(to[:, :, half:], v[:, :, 0:half], sin[:, :, half:],
                                       ALU.mult).then_inc(swap_made, 1)

            def one_over_rms(u):
                h0, nh, _, _ = PARTS[u]
                pool.wait_ge(ss_made, 2 * u + 2)
                s = slice(h0, h0 + nh)
                scale = (1.0 / AD, EPS) if u == 0 else (1.0, AD * EPS)
                own.done(pool.tensor_scalar(head_mean[:, :, s], head_ss[:, :, s], *scale,
                                            ALU.mult, ALU.add))
                own.wait()
                pool.tensor_tensor(head_rms[:, :, s], head_mean[:, :, s], half_down[:, :, 0:nh],
                                   ALU.pow).then_inc(head_rms_made, 1)

            for u in range(2):
                swap(u)
                one_over_rms(u)
            swap(2, (0,))
            for n in range(STEPS):
                st = stats[:, n % 2]
                pool.wait_ge(probs_made, n + 1)
                own.done(pool.tensor_tensor(st[:, SUM, :], st[:, DEN, :], st[:, SINK, :], ALU.add))
                own.wait()
                own.done(pool.tensor_tensor(st[:, INV, :], st[:, SUM, :], minus_one, ALU.pow))
                own.wait()
                for e in range(2):
                    c = slice(2 * e, 2 * e + 2)
                    pool.tensor_tensor(probs[:, n % 2, c, :], probs[:, n % 2, c, :],
                                       st[:, INV, c].unsqueeze(2).broadcast_to([P, 2, TOK]),
                                       ALU.mult).then_inc(probs_normed, 1)
                if n == 0:
                    swap(2, (1,))
                if n == 1:
                    one_over_rms(2)

        def proj_bank(u, t):
            return banks[min(2 * u, 2) + t]

        def turn_bank(u, s):
            return banks[(6, 0, 0)[u] + s]

        def attn_act(act, p):
            a0, _, q0, _ = bases(p)
            norm_act_early(act, p, 1)
            norm_act(act, p, 1)
            for c in (1,):
                for t in range(2):
                    split_slab_hi(act, a0 + c, None, t)

            def take_in(u, tiles=range(NT)):
                h0, nh, dst, _ = PARTS[u]
                for t in tiles:
                    if u == 0:
                        act.wait_ge(rms_made, 2 * p + t + 1)
                    act.wait_ge(qkv_put, 2 * u + t + 1)
                    act.activation(dst[:, t, :], proj_bank(u, t)[:, :], ACT.Copy,
                                   scale=rms[:, t:t + 1]).then_inc(qkv_made, 1)
                    wait(act, ss_made, 2 * (u - 1) + t + 1)
                    act.activation(squared[u][:, t, 0:nh * AD], proj_bank(u, t)[:, 0:nh * AD],
                                   ACT.Square, scale=rms[:, t:t + 1]).then_inc(sq_made, 1)

            def turned_in(u, dst):
                act.wait_ge(turn_put, u + 1)
                for s in range(2):
                    ins = act.activation(dst[:, 2 * s:2 * s + 2, :],
                                         turn_bank(u, s)[:, :].rearrange("p (a n) -> p a n", a=2), ACT.Copy)
                ins.then_inc(turn_made, 1)

            def exps(n):
                act.wait_ge(shift_made, n + 1)
                st = stats[:, n % 2]
                for c in range(4):
                    act.activation(probs[:, n % 2, c, :], probs[:, n % 2, c, :], ACT.Exp,
                                   bias=st[:, NEG, c:c + 1], accum_out=st[:, DEN, c:c + 1])
                act.activation(st[:, SINK, :], st[:, SINK_ARG, :], ACT.Exp).then_inc(probs_made, 1)

            take_in(0)
            for t in range(2):
                split_slab_hi(act, a0 + 2, None, t)
            take_in(1)
            turned_in(0, kT)
            for t in range(2):
                split_slab_hi(act, a0 + 3, None, t)
            take_in(2, (0,))
            turned_in(1, qT[:, 0:4, :])
            def outputs_hi(n):
                act.wait_ge(o_put, n + 1)
                act.activation(xT_hi[:, n, :], banks[n % 2][:, 0:TOK], ACT.Copy).then_inc(hT_hi_made, 1)

            exps(0)
            take_in(2, (1,))
            for n in range(STEPS):
                if n + 1 < STEPS:
                    exps(n + 1)
                act.wait_ge(probsT_put, n + 1)
                wait(act, o_put, n - 1)
                act.activation(prT[:, n % 2, 0, :, :], banks[2][:, :].rearrange("p (s n) -> p s n", s=2),
                               ACT.Copy).then_inc(probsT_hi, 1)
                if n == 0:
                    turned_in(2, qT[:, 4:8, :])
                if n > 1:
                    outputs_hi(n - 2)
            for n in range(STEPS - 2, STEPS):
                outputs_hi(n)
            for c in (4, 5)[:2 if p < last else 1]:
                for t in range(2):
                    split_slab_hi(act, a0 + c, None, t)
            norm_act_early(act, p + 1, 0)
            norm_act(act, p + 1, 0)

        def attn_dve(dve, own, p):
            a0, _, q0, _ = bases(p)

            def take_squares(u):
                h0, nh, _, _ = PARTS[u]
                for t in range(NT):
                    dve.wait_ge(sq_made, 2 * u + t + 1)
                    dve.tensor_reduce(head_ss[:, t, h0:h0 + nh], heads64(squared[u][:, t, 0:nh * AD], nh),
                                      AX_X, ALU.add).then_inc(ss_made, 1)

            def rotate(u):
                h0, nh, src, _ = PARTS[u]
                n = 1 if u == 0 else 0
                for t in range(NT):
                    to = k_rot[:, t, :] if u == 0 else q_rot[:, u - 1, t, :]
                    dve.wait_ge(qkv_made, 2 * u + t + 1)
                    own.done(dve.tensor_tensor(heads64(to, nh), heads64(src[:, t, 0:nh * AD], nh),
                                               rope_w[:, n, t, 0, :].unsqueeze(1).broadcast_to([P, nh, AD]),
                                               ALU.mult))
                    own.wait()
                    dve.wait_ge(swap_made, 2 * u + t + 1)
                    dve.tensor_tensor(to, to, swapped[u][:, t, 0:nh * AD], ALU.add).then_inc(rot_made, 1)

            def softmax_args(n):
                st = stats[:, n % 2]
                if n in (0, 4):
                    dve.wait_ge(head_rms_made, 2 + n // 4)
                dve.wait_ge(s_put, n + 1)
                wait(dve, probsT_put, n - 1)
                for c in range(4):
                    e, t = divmod(c, 2)
                    h = 2 * n + e
                    ins = dve.scalar_tensor_tensor(probs[:, n % 2, c, :],
                                                   banks[4 + 2 * (n % 2) + e][:, t * TOK:(t + 1) * TOK],
                                                   head_rms[:, t, h:h + 1], mask[:, t, :],
                                                   ALU.mult, ALU.add)
                own.done(ins)
                own.wait()
                own.done(dve.tensor_reduce(st[:, MAX, :], probs[:, n % 2, :, :], AX_X, ALU.max))
                own.wait()
                sink = minus_sink[:, 2 * n:2 * n + 2, :].rearrange("p a b -> p (a b)")
                own.done(dve.scalar_tensor_tensor(st[:, NEG, :], st[:, MAX, :], -1.0, sink,
                                                  ALU.mult, ALU.min))
                own.wait()
                dve.tensor_tensor(st[:, SINK_ARG, :], st[:, NEG, :], sink, ALU.subtract
                                  ).then_inc(shift_made, 1)

            norm_dve(dve, p, 1)
            norm_lo_dve(dve, p, 1)
            for t in range(2):
                split_slab_lo(dve, a0 + 1, None, t)
            dve.wait_ge(tables_made, 1)
            take_squares(0)
            rotate(0)
            dve.wait_ge(head_rms_made, 1)
            dve.wait_ge(rot_made, 2)
            for t in range(NT):
                for r in range(2):
                    ins = dve.tensor_tensor(k_twice[:, t, :, r, :], heads64(k_rot[:, t, :], KVH),
                                            head_rms[:, t, AH:].unsqueeze(2).broadcast_to([P, KVH, AD]),
                                            ALU.mult)
            ins.then_inc(k_made, 1)
            for t in range(2):
                split_slab_lo(dve, a0 + 2, None, t)
            take_squares(1)
            rotate(1)
            for t in range(2):
                split_slab_lo(dve, a0 + 3, None, t)
            def outputs_lo(n):
                dve.wait_ge(hT_hi_made, q0 + n + 1)
                dve.tensor_tensor(xT_lo[:, n, :], banks[n % 2][:, 0:TOK], xT_hi[:, n, :].bitcast(F32),
                                  ALU.subtract).then_inc(hT_lo_made, 1)

            softmax_args(0)
            for n in range(STEPS):
                if n + 1 < STEPS:
                    softmax_args(n + 1)
                if n == 0:
                    take_squares(2)
                    rotate(2)
                dve.wait_ge(probsT_put, n + 1)
                wait(dve, o_put, n - 1)
                dve.tensor_copy(prT[:, n % 2, 1, :, :], banks[3][:, :].rearrange("p (s n) -> p s n", s=2)
                                ).then_inc(probsT_lo, 1)
                if n > 1:
                    outputs_lo(n - 2)
            for n in range(STEPS - 2, STEPS):
                outputs_lo(n)
            for c in (4, 5)[:2 if p < last else 1]:
                for t in range(2):
                    split_slab_lo(dve, a0 + c, None, t)
            end_dve(dve, p, lambda t: 1.0)

        def attn_pe(pe, p):
            a0, _, q0, _ = bases(p)

            def project(u, tiles=range(NT)):
                if u == 2:
                    pe.wait_ge(sq_made, 4)
                for t in tiles:
                    for k in range(KD):
                        if u == 0 and k % 4 == 0:
                            pe.wait_ge(xT_lo_made, halves(p, t, k // 4))
                        if t == 0:
                            wait_slab(pe, a0 + u, None, k)
                        first, mm = three_passes(pe, proj_bank(u, t)[:, :], xT(k, t), slab(a0 + u, k),
                                                 k == 0, k == KD - 1)
                        if u > 0 and t == k == 0:
                            first.then_inc(a_used, 1)
                        elif t == k == 0:
                            first_product(first, p)
                        if u == t == 0 and k == 3:
                            norm_pe(pe, p, 1)
                    mm.then_inc(qkv_put, 1)

            def turn(u):
                if u == 0:
                    pe.wait_ge(k_made, 1)
                else:
                    pe.wait_ge(rot_made, 2 * u + 2)
                    pe.wait_ge(sq_made, 2)
                for s in range(4):
                    for t in range(NT):
                        src = k_twice[:, t, s, :, :].rearrange("p a b -> p (a b)") if u == 0 else \
                            q_rot[:, u - 1, t, s * P:(s + 1) * P]
                        mm = pe.transpose(turn_bank(u, s // 2)[:, (s % 2) * TOK + t * P:(s % 2) * TOK + (t + 1) * P],
                                          src, ident)
                        if u == 2 and s == t == 0:
                            mm.then_inc(a_used, 1)
                mm.then_inc(turn_put, 1)

            def scores(n):
                if n < 2:
                    pe.wait_ge(turn_made, 2)
                else:
                    pe.wait_ge(shift_made, n - 1)
                if n == 4:
                    pe.wait_ge(turn_made, 3)
                for e in range(2):
                    for t in range(NT):
                        mm = pe.matmul(banks[4 + 2 * (n % 2) + e][:, t * TOK:(t + 1) * TOK],
                                       lhsT=qT[e * AD:(e + 1) * AD, n, t * P:(t + 1) * P],
                                       rhs=kT[e * AD:(e + 1) * AD, n // 2, :], start=True, stop=True)
                mm.then_inc(s_put, 1)

            def turn_probs(n):
                wait(pe, probsT_hi, n)
                wait(pe, probsT_lo, n)
                if n == 0:
                    pe.wait_ge(sq_made, 6)
                for e in range(2):
                    pe.wait_ge(probs_normed, 2 * n + e + 1)
                    for s in range(NT):
                        for t in range(NT):
                            mm = pe.transpose(banks[2 + e][:, (2 * s + t) * P:(2 * s + t + 1) * P],
                                              probs[:, n % 2, 2 * e + t, s * P:(s + 1) * P], ident)
                mm.then_inc(probsT_put, 1)

            def values(n):
                pe.wait_ge(probsT_hi, n + 1)
                pe.wait_ge(probsT_lo, n + 1)
                wait(pe, hT_lo_made, q0 + n - 1 if n > 1 else 0)
                if n == 0:
                    pe.wait_ge(turn_made, 3)
                v = 256 + (n // 2) * AD
                for e in range(2):
                    for s in range(NT):
                        mm = pe.matmul(banks[n % 2][e * AD:(e + 1) * AD, 0:TOK], lhsT=kv[:, s, v:v + AD],
                                       rhs=prT[:, n % 2, e, s, :], start=s == 0, stop=s == NT - 1)
                mm.then_inc(o_put, 1)

            project(0)
            project(1)
            turn(0)
            project(2, (0,))
            turn(1)
            scores(0)
            scores(1)
            project(2, (1,))
            for n in range(STEPS):
                turn_probs(n)
                if n + 2 < STEPS:
                    scores(n + 2)
                if n == 0:
                    turn(2)
                if n > 0:
                    values(n - 1)
            values(STEPS - 1)
            pe.wait_ge(hT_lo_made, q0 + STEPS)
            for j, tiles in ((0, (0, 1)), (1, (0, 1)), (2, (0,)), (3, (0,)), (2, (1,)), (3, (1,))):
                c, half = a0 + 3 + j // 2, j % 2
                wait_slab(pe, c, None, 4 * half)

                def rows(s, c=c, half=half):
                    s += half * PIECE
                    return a_hi[:, c % 2, s:s + 512], a_lo[:, c % 2, s:s + 512]

                def oT(r, t, j=j):
                    return xT(2 * j + r, t)

                if j == KVH - 1 and tiles == (1,):
                    norm_pe(pe, p + 1, 0)
                start, _ = project_rows(pe, q0 + 2 * j + 1, None, 1, rows, j == 0, j == KVH - 1, oT, tiles)
                if j == 2 and tiles == (0,):
                    start.then_inc(a_used, 1)

        ffn = dict(sync=ffn_sync, scalar=ffn_act, vector=ffn_dve, tensor=ffn_pe)
        ssd = dict(sync=ssd_sync, scalar=ssd_act, vector=ssd_dve, tensor=ssd_pe)
        attn = dict(sync=attn_sync, scalar=attn_act, vector=attn_dve, tensor=attn_pe)
        kinds = dict(ffn=ffn, ssd=ssd, attn=attn)

        @block.sync
        def _(sp):
            sp.dma_start(ident, ident_dram).then_inc(ident_in, 16)
            sp.dma_start(x[:, 0, :], x_dram[0, 0:P, :]).then_inc(x_in[0], 16)
            load_slab(sp, 0, None, (0,))
            load_slab(sp, 0, None, (1,))
            sp.dma_start(x[:, 1, :], x_dram[0, P:2 * P, :]).then_inc(x_in[1], 16)
            for p, kind in enumerate(PHASES):
                kinds[kind]["sync"](sp, p)
            for t in range(NT):
                sp.wait_ge(x_made, 2 * last + t + 1)
                sp.dma_start(out_dram[0, t * P:(t + 1) * P, :], x[:, t, :]).then_inc(stored, 16)
            sp.wait_ge(stored, 16 * NT)

        @block.gpsimd
        def _(pool):
            own = Own(pool, pool_own)

            def load_norm(p):
                pool.dma_start(norm_w[:, p % 2, :], norm_dram[p:p + 1, :].broadcast_to([P, D])
                               ).then_inc(norm_in[p % 2], 16)

            own.done(pool.memset(minus_half, -0.5))
            own.wait()
            pool.wait_ge(xn_made, 1)
            for dst, src in ((consts[:, :, :], consts_dram), (convp, convp_dram),
                             (chan_par, chan_dram), (dt_w, dtw_dram),
                             (heads_in, heads_dram.unsqueeze(0).broadcast_to([P, 4, HEADS]))):
                pool.dma_start(dst, src).then_inc(small_in, 16)
            load_norm(1)
            for p, kind in enumerate(PHASES):
                if kind == "attn":
                    attn_load(pool, p)
                norm_pool(pool, own, p)
                if p + 2 < len(PHASES):
                    pool.wait_ge(xn_made, 4 * p + 4)
                    load_norm(p + 2)
                if kind == "ssd":
                    ssd_pool(pool, own, p)
                elif kind == "attn":
                    attn_pool(pool, own, p)

        @block.scalar
        def _(act):
            act.dma_start(norm_w[:, 0, :], norm_dram[0:1, :].broadcast_to([P, D])).then_inc(first_norm_in, 16)
            norm_act(act, 0, 0, square=False)
            for h in range(2):
                act.wait_ge(a_in[0][h], 16)
                for k in range(4):
                    s = slice(k * 512, (k + 1) * 512)
                    act.activation(a_hi[:, 0, h * PIECE + k * 512:h * PIECE + (k + 1) * 512],
                                   raw_a[:, 0, h, s], ACT.Copy
                                   ).then_inc(a_hi_made if k == 3 else first_hi_made, 1)
            square_act(act, 0, 0)
            for p, kind in enumerate(PHASES):
                kinds[kind]["scalar"](act, p)

        @block.vector
        def _(dve):
            own = Own(dve, dve_own)
            norm_dve(dve, 0, 0)
            norm_lo_dve(dve, 0, 0)
            for h in range(2):
                for k in range(4):
                    s = slice(k * 512, (k + 1) * 512)
                    to = slice(h * PIECE + k * 512, h * PIECE + (k + 1) * 512)
                    if k == 3:
                        dve.wait_ge(a_hi_made, h + 1)
                    else:
                        dve.wait_ge(first_hi_made, 3 * h + k + 1)
                    dve.tensor_tensor(a_lo[:, 0, to], raw_a[:, 0, h, s], a_hi[:, 0, to].bitcast(F32),
                                      ALU.subtract).then_inc(a_lo_made if k == 3 else first_lo_made, 1)
            for p, kind in enumerate(PHASES):
                kinds[kind]["vector"](dve, own, p)

        @block.tensor
        def _(pe):
            pe.wait_ge(ident_in, 16)
            norm_pe(pe, 0, 0)
            for p, kind in enumerate(PHASES):
                kinds[kind]["tensor"](pe, p)


SMALL_IN = 16 * 5


def lay_out(inputs):
    w_gate, w_up, w_down = (np.asarray(inputs[n]) for n in ("ffn_w_gate", "ffn_w_up", "ffn_w_down"))
    w_in, w_out = np.asarray(inputs["ssd_w_in"])[0], np.asarray(inputs["ssd_w_out"])[0]
    w_qkv, w_o = np.asarray(inputs["attn_w_qkv"])[0], np.asarray(inputs["attn_w_out"])[0]

    def columns(w, *spans):
        w = w.reshape(KD, P, -1)
        return np.concatenate([w[:, :, a:b] for a, b in spans], axis=2).transpose(1, 0, 2)

    def down_rows(w, r):
        return w[r:r + 2 * P].reshape(2, P, D).transpose(1, 0, 2)

    def slabs(m):
        return list(m.reshape(P, 2, PIECE).transpose(1, 0, 2))

    a, b = [], []
    n_ffn = 0
    for kind in PHASES:
        if kind == "ffn":
            layer, which = divmod(n_ffn, 2)
            g, u, dn = w_gate[layer, which], w_up[layer, which], w_down[layer, which]
            for n in range(NBLK):
                s = (n * FB, (n + 1) * FB)
                a += slabs(np.concatenate([columns(g, s), columns(u, s)], axis=2))
                b.append(down_rows(dn, n * FB).reshape(P, PIECE))
            n_ffn += 1
        elif kind == "ssd":
            x0, b0, c0 = INNER, 2 * INNER, 2 * INNER + GROUPS * STATE
            dt0 = c0 + GROUPS * STATE
            for n in range(GROUPS):
                a += slabs(columns(w_in, (x0 + n * GC, x0 + (n + 1) * GC),
                                   (b0 + n * STATE, b0 + (n + 1) * STATE),
                                   (c0 + n * STATE, c0 + (n + 1) * STATE)))
            dtw = columns(w_in, (dt0, dt0 + 2 * HEADS)).reshape(P, -1)
            z = [columns(w_in, (n * GC, (n + 1) * GC)).reshape(P, PIECE) for n in range(GROUPS)]
            o = [down_rows(w_out, n * GC).reshape(P, PIECE) for n in range(GROUPS)]
            b.append(z[0])
            for n in range(1, GROUPS):
                b += [z[n], o[n - 1]]
            b.append(o[GROUPS - 1])
        else:
            for s in (QKV - 512, QKV), (0, 512), (512, 1024):
                a += slabs(columns(w_qkv, s))
            for n in range(KVH):
                a.append(down_rows(w_o, n * 2 * P).reshape(P, PIECE))
    r = np.arange(P)
    ident = np.eye(P, dtype=np.float32)
    consts = np.stack([r[:, None] <= r, r[:, None] >= r,
                       r[:, None] < r, r[:, None] > r], axis=1).astype(np.float32)
    cw = np.asarray(inputs["ssd_conv_w"])[0]
    cb = np.asarray(inputs["ssd_conv_b"])
    params = np.concatenate([cw, cb], axis=0)
    px, pb, pc = params[:, :INNER], params[:, INNER:INNER + 1024], params[:, INNER + 1024:]
    tiles = np.stack([pb.reshape(6, GROUPS, P), pc.reshape(6, GROUPS, P),
                      px.reshape(6, GROUPS, 2, P)[:, :, 0], px.reshape(6, GROUPS, 2, P)[:, :, 1]], axis=2)
    half = AD // 2
    inv_freq = np.float32(10000.0) ** (-np.arange(half, dtype=np.float32) / np.float32(half))
    angle = np.arange(TOK, dtype=np.float32)[:, None] * inv_freq[None, :].astype(np.float32)
    cos, sin = np.cos(angle), np.sin(angle)
    rope = np.stack([np.concatenate([cos, cos], axis=1), np.concatenate([-sin, sin], axis=1)], axis=1)
    rope = rope.reshape(NT, P, 2, AD).transpose(1, 0, 2, 3).astype(np.float32)
    tok = np.arange(TOK)
    mask = np.where(np.abs(tok[:, None] - tok[None, :]) <= WINDOW, 0.0, -3e38).astype(np.float32)
    qn, kn = np.asarray(inputs["attn_q_norm"])[0], np.asarray(inputs["attn_k_norm"])[0]
    return {
        "mask": np.ascontiguousarray(mask.reshape(NT, P, TOK).transpose(1, 0, 2)),
        "rope": np.ascontiguousarray(rope),
        "attn": np.concatenate([qn, qn[half:], qn[:half], kn, kn[half:], kn[:half],
                                np.asarray(inputs["attn_sink"])[0]]),
        "a": np.stack(a), "b": np.stack(b), "x": np.asarray(inputs["x"]),
        "norm": np.asarray(inputs["norm_w"]).reshape(-1, D),
        "convp": np.ascontiguousarray(tiles.transpose(3, 1, 2, 0)),
        "chan": np.ascontiguousarray(np.stack(
            [np.asarray(inputs["ssd_norm_w"])[0], np.repeat(np.asarray(inputs["ssd_d"])[0], HD)]
        ).reshape(2, GROUPS, 2, P).transpose(3, 0, 1, 2)),
        "heads": np.concatenate([np.asarray(inputs["ssd_dt_bias"])[0],
                                 np.asarray(inputs["ssd_a_log"])[0]], axis=0),
        "dtw": np.ascontiguousarray(dtw),
        "consts": consts,
        "ident": ident,
    }


def kernel(**inputs):
    import concourse.bacc as bacc
    from concourse.bass_utils import run_bass_kernel_spmd

    nc = bacc.Bacc("TRN2", target_bir_lowering=False, num_devices=1)
    arrays, drams = {}, {}
    for name, a in lay_out(inputs).items():
        arrays[f"in_{name}"] = a
        drams[name] = nc.dram_tensor(f"in_{name}", a.shape, mybir.dt.from_np(a.dtype),
                                     kind="ExternalInput").ap()
    rows = nc.dram_tensor("cum_rows", (HEADS, 2 * TOK), F32, kind="Internal").ap()
    out = nc.dram_tensor("out_0", (1, TOK, D), F32, kind="ExternalOutput").ap()
    build_program(nc, drams["a"], drams["b"], drams["x"], drams["norm"], drams["convp"],
                  drams["chan"], drams["heads"], drams["dtw"], drams["ident"], drams["consts"], rows,
                  drams["mask"], drams["rope"], drams["attn"], out)
    return run_bass_kernel_spmd(nc, [arrays], core_ids=[0]).results[0]["out_0"]
```
